# Optimizing a Trainium2 kernel written in Bass

```python
import math
import jax, jax.numpy as jnp
from jax import lax
import numpy as np

D_MODEL = 1024
BATCH = 1
SEQ = 1024
DEPTH = 2

N_MIXERS = 2
N_ATTN_LAYERS = (DEPTH + 1) // 2
N_CONV_LAYERS = DEPTH // 2

N_HEADS = 16
QK_NOPE_DIM = 64
QK_ROPE_DIM = 32
V_HEAD_DIM = 64
Q_LORA_RANK = 384
KV_LORA_RANK = 256
ROPE_THETA = 10000.0
Q_BLOCK = 128

CONV_WIDTH = 31
CONV_PAD = CONV_WIDTH // 2

FF_MULT = 256
D_FF = ((8 * D_MODEL + 3 * FF_MULT - 1) // (3 * FF_MULT)) * FF_MULT

DEEPNORM_ALPHA = float((2 * DEPTH) ** 0.25)
DEEPNORM_BETA = float((8 * DEPTH) ** -0.25)

LN_EPS = 1e-5
RMS_EPS = 1e-6

kernel_name = "hybrid_mla_conformer_deepnorm_encoder"

def layer_norm(x, g, b):
    xf = x.astype(jnp.float32)
    mu = jnp.mean(xf, axis=-1, keepdims=True)
    var = jnp.mean(jnp.square(xf - mu), axis=-1, keepdims=True)
    y = (xf - mu) * lax.rsqrt(var + LN_EPS) * g.astype(jnp.float32) + b.astype(jnp.float32)
    return y.astype(x.dtype)

def rms_norm(x, g):
    xf = x.astype(jnp.float32)
    y = xf * lax.rsqrt(jnp.mean(jnp.square(xf), axis=-1, keepdims=True) + RMS_EPS)
    return (y * g.astype(jnp.float32)).astype(x.dtype)

def rope_tables(positions, dtype):
    inv_freq = ROPE_THETA ** (-jnp.arange(0, QK_ROPE_DIM, 2, dtype=jnp.float32) / QK_ROPE_DIM)
    ang = positions.astype(jnp.float32)[..., None] * inv_freq
    return jnp.cos(ang).astype(dtype), jnp.sin(ang).astype(dtype)

def apply_rope(t, cos, sin):
    h = QK_ROPE_DIM // 2
    t1, t2 = t[..., :h], t[..., h:]
    return jnp.concatenate([t1 * cos - t2 * sin, t2 * cos + t1 * sin], axis=-1)

def mla_mixer(x, cos, sin, w_dq, q_norm, w_uq, w_dkv, kv_norm, w_ukv, w_o):
    B, S, _ = x.shape
    H = N_HEADS
    cq = rms_norm(x @ w_dq, q_norm)
    q = (cq @ w_uq).reshape(B, S, H, QK_NOPE_DIM + QK_ROPE_DIM)
    q_nope = q[..., :QK_NOPE_DIM]
    q_rope = apply_rope(q[..., QK_NOPE_DIM:], cos[:, :, None, :], sin[:, :, None, :])
    ckv_full = x @ w_dkv
    ckv = rms_norm(ckv_full[..., :KV_LORA_RANK], kv_norm)
    k_rope = apply_rope(ckv_full[..., KV_LORA_RANK:], cos, sin)
    kv = (ckv @ w_ukv).reshape(B, S, H, QK_NOPE_DIM + V_HEAD_DIM)
    k_nope = kv[..., :QK_NOPE_DIM]
    v = kv[..., QK_NOPE_DIM:]
    scale = 1.0 / math.sqrt(QK_NOPE_DIM + QK_ROPE_DIM)

    nblk = S // Q_BLOCK
    qn_blocks = q_nope.reshape(B, nblk, Q_BLOCK, H, QK_NOPE_DIM).transpose(1, 0, 2, 3, 4)
    qr_blocks = q_rope.reshape(B, nblk, Q_BLOCK, H, QK_ROPE_DIM).transpose(1, 0, 2, 3, 4)

    def attend(blk):
        qn, qr = blk
        s = (jnp.einsum('bqhd,bkhd->bhqk', qn, k_nope).astype(jnp.float32)
             + jnp.einsum('bqhd,bkd->bhqk', qr, k_rope).astype(jnp.float32)) * scale
        p = jax.nn.softmax(s, axis=-1).astype(v.dtype)
        return jnp.einsum('bhqk,bkhd->bqhd', p, v)

    o = lax.map(attend, (qn_blocks, qr_blocks))
    o = o.transpose(1, 0, 2, 3, 4).reshape(B, S, H * V_HEAD_DIM)
    return o @ w_o

def conformer_conv_mixer(x, w_in, b_in, dw, dw_b, ln_g, ln_b, w_out, b_out):
    D = x.shape[-1]
    h = x @ w_in + b_in
    h = h[..., :D] * jax.nn.sigmoid(h[..., D:])
    h = lax.conv_general_dilated(
        h, dw[:, None, :].astype(h.dtype), window_strides=(1,),
        padding=[(CONV_PAD, CONV_PAD)],
        dimension_numbers=('NWC', 'WIO', 'NWC'),
        feature_group_count=D) + dw_b
    h = layer_norm(h, ln_g, ln_b)
    h = jax.nn.silu(h)
    return h @ w_out + b_out

def swiglu_ffn(x, w1, w3, w2):
    return (jax.nn.silu(x @ w1) * (x @ w3)) @ w2

def setup_inputs(seed: int = 0) -> dict:
    key = jax.random.key(seed)
    ks = jax.random.split(key, 24)
    f32 = jnp.float32
    D, H = D_MODEL, N_HEADS
    La, Lc = N_ATTN_LAYERS, N_CONV_LAYERS

    def w(k, shape, fan_in, mult=1.0):
        return jax.random.normal(k, shape, f32) * (fan_in ** -0.5) * mult

    x = jax.random.normal(ks[0], (BATCH, SEQ, D), f32)
    offsets = jax.random.randint(ks[1], (BATCH, 1), 0, 1024, dtype=jnp.int32)
    positions = (jnp.arange(SEQ, dtype=jnp.int32)[None, :] + offsets).astype(jnp.int32)

    ln_g = 1.0 + 0.02 * jax.random.normal(ks[2], (DEPTH, 2, D), f32)
    ln_b = 0.02 * jax.random.normal(ks[3], (DEPTH, 2, D), f32)

    mla_w_dq = w(ks[4], (La, D, Q_LORA_RANK), D)
    mla_q_norm = 1.0 + 0.02 * jax.random.normal(ks[5], (La, Q_LORA_RANK), f32)
    mla_w_uq = w(ks[6], (La, Q_LORA_RANK, H * (QK_NOPE_DIM + QK_ROPE_DIM)), Q_LORA_RANK)
    mla_w_dkv = w(ks[7], (La, D, KV_LORA_RANK + QK_ROPE_DIM), D)
    mla_kv_norm = 1.0 + 0.02 * jax.random.normal(ks[8], (La, KV_LORA_RANK), f32)
    mla_w_ukv = w(ks[9], (La, KV_LORA_RANK, H * (QK_NOPE_DIM + V_HEAD_DIM)), KV_LORA_RANK)
    mla_w_o = w(ks[10], (La, H * V_HEAD_DIM, D), H * V_HEAD_DIM, DEEPNORM_BETA)

    conv_w_in = w(ks[11], (Lc, D, 2 * D), D)
    conv_b_in = 0.02 * jax.random.normal(ks[12], (Lc, 2 * D), f32)
    conv_dw = w(ks[13], (Lc, CONV_WIDTH, D), CONV_WIDTH)
    conv_dw_b = 0.02 * jax.random.normal(ks[14], (Lc, D), f32)
    conv_ln_g = 1.0 + 0.02 * jax.random.normal(ks[15], (Lc, D), f32)
    conv_ln_b = 0.02 * jax.random.normal(ks[16], (Lc, D), f32)
    conv_w_out = w(ks[17], (Lc, D, D), D, DEEPNORM_BETA)
    conv_b_out = 0.02 * jax.random.normal(ks[18], (Lc, D), f32)

    ffn_w1 = w(ks[19], (DEPTH, D, D_FF), D)
    ffn_w3 = w(ks[20], (DEPTH, D, D_FF), D)
    ffn_w2 = w(ks[21], (DEPTH, D_FF, D), D_FF, DEEPNORM_BETA)

    return {
        "x": x, "positions": positions, "ln_g": ln_g, "ln_b": ln_b,
        "mla_w_dq": mla_w_dq, "mla_q_norm": mla_q_norm, "mla_w_uq": mla_w_uq,
        "mla_w_dkv": mla_w_dkv, "mla_kv_norm": mla_kv_norm, "mla_w_ukv": mla_w_ukv,
        "mla_w_o": mla_w_o,
        "conv_w_in": conv_w_in, "conv_b_in": conv_b_in, "conv_dw": conv_dw,
        "conv_dw_b": conv_dw_b, "conv_ln_g": conv_ln_g, "conv_ln_b": conv_ln_b,
        "conv_w_out": conv_w_out, "conv_b_out": conv_b_out,
        "ffn_w1": ffn_w1, "ffn_w3": ffn_w3, "ffn_w2": ffn_w2,
    }

def reference(x, positions, ln_g, ln_b,
              mla_w_dq, mla_q_norm, mla_w_uq, mla_w_dkv, mla_kv_norm, mla_w_ukv, mla_w_o,
              conv_w_in, conv_b_in, conv_dw, conv_dw_b, conv_ln_g, conv_ln_b,
              conv_w_out, conv_b_out,
              ffn_w1, ffn_w3, ffn_w2):
    cos, sin = rope_tables(positions, x.dtype)
    for i in range(DEPTH):
        j = i // N_MIXERS
        if i % N_MIXERS == 0:
            h = mla_mixer(x, cos, sin, mla_w_dq[j], mla_q_norm[j], mla_w_uq[j],
                          mla_w_dkv[j], mla_kv_norm[j], mla_w_ukv[j], mla_w_o[j])
        else:
            h = conformer_conv_mixer(x, conv_w_in[j], conv_b_in[j], conv_dw[j], conv_dw_b[j],
                                     conv_ln_g[j], conv_ln_b[j], conv_w_out[j], conv_b_out[j])
        x = layer_norm(DEEPNORM_ALPHA * x + h, ln_g[i, 0], ln_b[i, 0])
        f = swiglu_ffn(x, ffn_w1[i], ffn_w3[i], ffn_w2[i])
        x = layer_norm(DEEPNORM_ALPHA * x + f, ln_g[i, 1], ln_b[i, 1])
    return x


_drawn_inputs = setup_inputs


def setup_inputs(seed=0):
    import zlib

    import numpy as np

    out = dict(_drawn_inputs(seed))
    spreads = {}
    factors = {'mla_q_norm': 8.0,
     'mla_kv_norm': 8.0,
     'conv_b_in': 8.0,
     'conv_dw_b': 7.257,
     'conv_ln_g': 8.0,
     'conv_ln_b': 8.0,
     'conv_b_out': 4.107}
    for name, (base, spread) in spreads.items():
        noise = np.random.default_rng([zlib.crc32(name.encode()), seed]).standard_normal(out[name].shape)
        drawn = base * np.exp(spread * noise) if base else spread * noise
        out[name] = __import__('jax').numpy.asarray(drawn.astype(out[name].dtype))
    for name, factor in factors.items():
        out[name] = (out[name] * factor).astype(out[name].dtype)
    return out
```

```python
import math
from contextlib import ExitStack

import numpy as np
import concourse.bass as bass
from concourse import mybir

F32 = mybir.dt.float32
F32R = mybir.dt.float32r
I32 = mybir.dt.int32
ALU = mybir.AluOpType
ACT = mybir.ActivationFunctionType

P = 128
D = 1024
SEQ = 1024
NK = D // P
NT = SEQ // P
HALF = 512
HEADS, NOPE, ROPE, VDIM = 16, 64, 32, 64
QK = NOPE + ROPE
PAIRS = HEADS // 2
Q_RANK, KV_RANK = 384, 256
NQ, NKV = Q_RANK // P, KV_RANK // P
DOWN = Q_RANK + KV_RANK + ROPE
D_FF = 2816
NF = D_FF // P
TAPS = 31
PAD = TAPS // 2
ALPHA = float(4 ** 0.25)
LN_EPS, RMS_EPS = 1e-5, 1e-6
SCALE = 1.0 / math.sqrt(QK)
CHUNK = 2 * P
NQT = 2 * NT
CREDIT = 4
MAGIC = 1.5 * 2.0 ** 23


class Flow:

    def __init__(self, sem):
        self.sem = sem

    def ready(self, item):
        return item + (1 + CREDIT)

    def free(self, item, slots):
        return item + (1 - slots + CREDIT)


class Chain:

    def __init__(self, sem, eng):
        self.sem, self.eng, self.count = sem, eng, 0

    def link(self, ins):
        ins.then_inc(self.sem, 1)
        self.count += 1
        self.eng.wait_ge(self.sem, self.count)


def turn_pieces(turns, count):
    rest, out = 2 * math.pi * turns, []
    for _ in range(count):
        unit = 2.0 ** (math.floor(math.log2(rest)) - 11)
        out.append(math.floor(rest / unit) * unit)
        rest -= out[-1]
    return out


def pair_views(w, raw):
    src = raw[:].rearrange("p k (j d) -> p k j d", j=2)
    h = ROPE // 2

    def dst(a, d):
        return w[:, :, a:a + 2 * d].rearrange("p k (j d) -> p k j d", j=2)

    swapped = dst(P + 2 * ROPE, ROPE)
    return [(dst(0, NOPE), src[:, :, :, 0:NOPE]), (dst(P, ROPE), src[:, :, :, NOPE:QK]),
            (swapped[:, :, :, 0:h], src[:, :, :, NOPE + h:QK]), (swapped[:, :, :, h:ROPE], src[:, :, :, NOPE:NOPE + h])]


def kv_views(w, raw):
    src = raw[:].rearrange("p k (j d) -> p k j d", j=2)
    return [(w[:, :, a:a + P].rearrange("p k (j d) -> p k j d", j=2), src[:, :, :, b:b + NOPE])
            for a, b in ((0, 0), (P, NOPE))]


def trunk(nc, x, positions, ln_g, ln_b, w_dq, q_norm, w_uq, w_dkv, kv_norm, w_ukv, w_o, w_in, b_in,
          conv_dw, conv_dw_b, conv_ln_g, conv_ln_b, w_out, b_out, ffn_w1, ffn_w3, ffn_w2, rope_const, out):
    x_v = x[0].rearrange("(t p) d -> t p d", p=P)
    out_v = out[0].rearrange("(t p) d -> t p d", p=P)
    dq_v = w_dq[0].rearrange("(k p) n -> p k n", p=P)
    dkv_v = w_dkv[0].rearrange("(k p) n -> p k n", p=P)
    uq_v = w_uq[0].rearrange("(k p) n -> p k n", p=P)
    ukv_v = w_ukv[0].rearrange("(k p) n -> p k n", p=P)
    wo_v = w_o[0].rearrange("(k p) n -> k p n", p=P)
    wout_v = w_out[0].rearrange("(k p) n -> k p n", p=P)
    win_v = w_in[0].rearrange("(k p) (g n) -> p g k n", p=P, g=2)
    w1_v = [ffn_w1[l].rearrange("(k p) n -> p k n", p=P) for l in range(2)]
    w3_v = [ffn_w3[l].rearrange("(k p) n -> p k n", p=P) for l in range(2)]
    w2_v = [ffn_w2[l].rearrange("(f p) n -> p f n", p=P) for l in range(2)]

    ctx = ExitStack()
    with ctx:
        def sb(name, shape, dt=F32):
            return ctx.enter_context(nc.sbuf_tensor(name, shape, dt))

        gaps = [0]

        def region(start_kb, *specs):
            got = []
            with ExitStack() as r:
                if start_kb:
                    gaps[0] += 1
                    r.enter_context(nc.sbuf_tensor(f"gap{gaps[0]}", [P, start_kb * 256], F32))
                for name, shape, dt in specs:
                    got.append(r.enter_context(nc.sbuf_tensor(name, shape, dt)))
            return got

        def flow(name):
            f = Flow(ctx.enter_context(nc.semaphore(name)))
            flows.append(f)
            return f

        def sem(name):
            return ctx.enter_context(nc.semaphore(name))

        flows = []

        ident = sb("ident", [P, P])
        ones = sb("ones", [P, VDIM])
        minus_half = sb("minus_half", [P, 2])
        consts = sb("consts", [P, 4])
        cols = sb("cols", [P, 48])
        dw_cols = sb("dw_cols", [P, NK, 32])
        stats = sb("stats", [P, NT, 12])
        mean_var = sb("mean_var", [P, NT, 2])
        rstd = sb("rstd", [P, NT, 2])
        negmax = sb("negmax", [P, NQT])
        sums = sb("sums", [P, NQT])
        rsums = sb("rsums", [P, NQT])
        gb = sb("gb", [P, 2, D])
        C_GQ, C_BIN, C_DWB, C_LNG, C_LNB = 0, 5, 21, 29, 37
        N_COLS = 45

        actT_hi, actT_lo = region(32, ("actT_hi", [P, NK, SEQ], F32R), ("actT_lo", [P, NK, SEQ], F32R))
        [resid] = region(0, ("resid", [P, NT, D], F32))
        [x_stage] = region(0, ("x_stage", [P, 4, D], F32))
        [vec_rows, dw_rows, pos_i, ang, turns, cosv, sinv, absr] = region(
            16, ("vec_rows", [P, P], F32), ("dw_rows", [P, D], F32), ("pos_i", [P, CHUNK], I32),
            ("ang", [P, CHUNK], F32), ("turns", [P, CHUNK], F32), ("cosv", [P, CHUNK], F32),
            ("sinv", [P, CHUNK], F32), ("absr", [P, CHUNK], F32))
        cT_hi, cT_lo, tab, kr_f = region(96, ("cT_hi", [P, 5, SEQ], F32R), ("cT_lo", [P, 5, SEQ], F32R),
                                         ("tab", [P, SEQ], F32), ("kr_f", [P, SEQ], F32))
        [wd_hi, wd_lo] = region(144, ("wd_hi", [P, NK, DOWN], F32R), ("wd_lo", [P, NK, DOWN], F32R))
        wd_raw, c_tok = region(187, ("wd_raw", [P, 2, DOWN], F32), ("c_tok", [P, DOWN + ROPE], F32))
        [pt_hi, pt_lo] = region(0, ("pt_hi", [P, 2, NK, CHUNK], F32R), ("pt_lo", [P, 2, NK, CHUNK], F32R))
        q_hi, q_lo, k_hi, k_lo = region(
            32, ("q_hi", [P, 2, SEQ], F32R), ("q_lo", [P, 2, SEQ], F32R),
            ("k_hi", [P, 2, SEQ], F32R), ("k_lo", [P, 2, SEQ], F32R))
        [oT_f] = region(64, ("oT_f", [P, NK, SEQ], F32))
        (v2, p_f, rope_a, rope_b, wq_hi, wq_lo, wkv_hi, wkv_lo, wq_raw, wkv_raw, o_first, o_both,
         diag) = region(
            144, ("v2", [P, NT, 2, 2 * VDIM], F32R), ("p_f", [P, 2, SEQ], F32),
            ("rope_a", [P, 2, SEQ], F32), ("rope_b", [P, 2, SEQ], F32),
            ("wq_hi", [P, NQ, 2 * P], F32R), ("wq_lo", [P, NQ, 2 * P], F32R),
            ("wkv_hi", [P, NKV, 2 * P], F32R), ("wkv_lo", [P, NKV, 2 * P], F32R),
            ("wq_raw", [P, NQ, 2 * QK], F32), ("wkv_raw", [P, NKV, 2 * P], F32),
            ("o_first", [P, 2, CHUNK], F32), ("o_both", [P, CHUNK], F32), ("diag", [P, 2, CHUNK], F32))
        wo_hi, wo_lo, wo_raw = region(96, ("wo_hi", [P, NK, D], F32R), ("wo_lo", [P, NK, D], F32R),
                                      ("wo_raw", [P, D], F32))
        wx_hi, wx_lo, wx_raw = region(128, ("wx_hi", [P, NK, D], F32R), ("wx_lo", [P, NK, D], F32R),
                                      ("wx_raw", [P, D], F32))
        (hid_hi, hid_lo, w13_hi, w13_lo, w2_hi, w2_lo, w13_raw, w2_raw, gate, hid_f) = region(
            96, ("hid_hi", [P, 2, SEQ], F32R), ("hid_lo", [P, 2, SEQ], F32R),
            ("w13_hi", [P, 2, 2, NK, P], F32R), ("w13_lo", [P, 2, 2, NK, P], F32R),
            ("w2_hi", [P, 2, D], F32R), ("w2_lo", [P, 2, D], F32R),
            ("w13_raw", [P, 2, NK, P], F32), ("w2_raw", [P, D], F32),
            ("gate", [P, SEQ], F32), ("hid_f", [P, SEQ], F32))
        [bout_b] = region(186, ("bout_b", [P, D], F32))
        convT, win_hi, win_lo, win_raw, glu, sig, conv_acc, dw_now, bias_now = region(
            96, ("convT", [P, NK, SEQ], F32), ("win_hi", [P, 2, 2, NK, P], F32R),
            ("win_lo", [P, 2, 2, NK, P], F32R), ("win_raw", [P, 2, NK, P], F32),
            ("glu", [P, 2, SEQ + 2 * PAD], F32), ("sig", [P, SEQ], F32),
            ("conv_acc", [P, SEQ], F32), ("dw_now", [P, 2, 32], F32), ("bias_now", [P, 2], F32))

        ps = [ctx.enter_context(nc.psum_tensor(f"ps{i}", [P, 2 * HALF], F32)) for i in range(4)]

        started = sem("started")
        x_in = [sem(f"x_in{i}") for i in range(4)]
        small_in = sem("small_in")
        cols_in = sem("cols_in")
        wd_in = [sem(f"wd_in{i}") for i in range(2)]
        made_consts = sem("made_consts")
        cols_ps, cols_done = sem("cols_ps"), sem("cols_done")
        ang_done, tab_done = sem("ang_done"), sem("tab_done")
        tp_ps, tp_hi, tp_lo = flow("tp_ps"), flow("tp_hi"), flow("tp_lo")
        wd_hi_done, wd_lo_done = flow("wd_hi_done"), flow("wd_lo_done")
        c_ps, c_sq, c_ms, c_rstd, c_tok_done = (flow(n) for n in ("c_ps", "c_sq", "c_ms", "c_rstd", "c_tok_done"))
        ct_ps, ct_hi, ct_lo = flow("ct_ps"), flow("ct_hi"), flow("ct_lo")
        krope_done, krope_hi, krope_lo = sem("krope_done"), sem("krope_hi"), sem("krope_lo")
        wq_in, wkv_in = sem("wq_in"), sem("wkv_in")
        wa_hi_done, wa_lo_done = flow("wa_hi_done"), flow("wa_lo_done")
        k_ps, qn_ps, qr_ps, v_ps = flow("k_ps"), flow("qn_ps"), flow("qr_ps"), flow("v_ps")
        k_hi_done, k_lo_done, qn_hi_done, qn_lo_done = (flow(n) for n in (
            "k_hi_done", "k_lo_done", "qn_hi_done", "qn_lo_done"))
        v_hi_done, v_lo_done = flow("v_hi_done"), flow("v_lo_done")
        qr_parts, qr_sum, qr_hi_done, qr_lo_done = (flow(n) for n in (
            "qr_parts", "qr_sum", "qr_hi_done", "qr_lo_done"))
        s_ps, s_max, p_done = flow("s_ps"), flow("s_max"), flow("p_done")
        pt_ps, pt_hi_done, pt_lo_done = flow("pt_ps"), flow("pt_hi_done"), flow("pt_lo_done")
        rsum_done, diag_done, o_ps, o_first_done, o_sum_done, o_done = (flow(n) for n in (
            "rsum_done", "diag_done", "o_ps", "o_first_done", "o_sum_done", "o_done"))
        xr_in = [sem(f"xr_in{i}") for i in range(NT)]
        oT_hi_done, oT_lo_done = flow("oT_hi_done"), flow("oT_lo_done")
        wsq_in = sem("wsq_in")
        wsq_hi_done, wsq_lo_done = flow("wsq_hi_done"), flow("wsq_lo_done")
        pr_ps, pr_add = flow("pr_ps"), flow("pr_add")
        gb_in = sem("gb_in")
        bout_in = sem("bout_in")
        ln_var, ln_rstd, ln_norm, ln_g_done, ln_done, ln_scaled, ln_bout = (flow(n) for n in (
            "ln_var", "ln_rstd", "ln_norm", "ln_g_done", "ln_done", "ln_scaled", "ln_bout"))
        w13_in, w2_in = sem("w13_in"), sem("w2_in")
        w13_hi_done, w13_lo_done, w2_hi_done, w2_lo_done = (flow(n) for n in (
            "w13_hi_done", "w13_lo_done", "w2_hi_done", "w2_lo_done"))
        up_ps, gate_done, hid_f_done, hid_hi_done, hid_lo_done, down_ps, acc_done = (flow(n) for n in (
            "up_ps", "gate_done", "hid_f_done", "hid_hi_done", "hid_lo_done", "down_ps", "acc_done"))
        win_in = sem("win_in")
        win_hi_done, win_lo_done, in_ps, sig_done, glu_done, dw_now_done, bias_now_done, tap_done = (flow(n) for n in (
            "win_hi_done", "win_lo_done", "in_ps", "sig_done", "glu_done", "dw_now_done", "bias_now_done", "tap_done"))
        pads_done = sem("pads_done")
        cl_ps, cl_var, cl_rstd, cl_norm, cb_ps, silu_done, sT_hi_done, sT_lo_done = (flow(n) for n in (
            "cl_ps", "cl_var", "cl_rstd", "cl_norm", "cb_ps", "silu_done", "sT_hi_done", "sT_lo_done"))
        stored = sem("stored")
        dve_steps, act_steps, pool_steps = sem("dve_steps"), sem("act_steps"), sem("pool_steps")

        block = ctx.enter_context(nc.Block())
        tok = [slice(t * P, (t + 1) * P) for t in range(NT)]
        halves = [slice(0, HALF), slice(HALF, 2 * HALF)]

        def bank(m):
            return ps[2 + m % 4 // 2][:, halves[m % 2]]

        @block.sync
        def _(sp):
            with nc.allow_non_contiguous_dma(reason="vectors of a few hundred elements"):
                sp.dma_start(consts[:, 0:3], rope_const).then_inc(small_in, 16)
                for q in range(4):
                    sp.dma_start(pos_i[32 * q:32 * q + 32, :],
                                 positions[:, CHUNK * q:CHUNK * (q + 1)].to_broadcast([32, CHUNK])
                                 ).then_inc(small_in, 16)
                for t in range(4):
                    sp.dma_start(x_stage[:, t, :], x_v[t]).then_inc(x_in[t], 16)
                for row, v, n in ((C_GQ, q_norm, NQ), (C_GQ + NQ, kv_norm, NKV), (C_BIN, b_in, 2 * NK),
                                  (C_DWB, conv_dw_b, NK), (C_LNG, conv_ln_g, NK), (C_LNB, conv_ln_b, NK)):
                    sp.dma_start(vec_rows[row:row + n, :], v[0].rearrange("(r p) -> r p", p=P)).then_inc(cols_in, 16)
                sp.dma_start(dw_rows[0:TAPS, :], conv_dw[0]).then_inc(cols_in, 16)
            def load_wd(k):
                if k >= 2:
                    sp.wait_ge(wd_lo_done.sem, wd_lo_done.free(k, 2))
                sp.dma_start(wd_raw[:, k % 2, 0:Q_RANK], dq_v[:, k, :]).then_inc(wd_in[k % 2], 16)
                sp.dma_start(wd_raw[:, k % 2, Q_RANK:DOWN], dkv_v[:, k, :]).then_inc(wd_in[k % 2], 16)

            sp.wait_ge(started, 1)
            load_wd(0)
            load_wd(1)
            for t in range(4, NT):
                sp.wait_ge(tp_ps.sem, tp_ps.ready(t - 4))
                sp.dma_start(x_stage[:, t % 4, :], x_v[t]).then_inc(x_in[t % 4], 16)
                load_wd(2 + t - 4)
            for k in range(6, NK):
                load_wd(k)

            sp.wait_ge(ct_ps.sem, ct_ps.ready(NT - 1))
            sp.wait_ge(c_tok_done.sem, c_tok_done.ready(NT - 1))

            def load_pair(i):
                sp.dma_start(wq_raw[:], uq_v[:, :, bass.ds(i * (2 * QK), 2 * QK)]).then_inc(wq_in, 16)
                sp.dma_start(wkv_raw[:], ukv_v[:, :, bass.ds(i * (2 * P), 2 * P)]).then_inc(wkv_in, 16)

            load_pair(0)
            with sp.Fori(1, PAIRS) as i:
                sp.wait_ge(wa_lo_done.sem, wa_lo_done.ready(i - 1))
                load_pair(i)

            def load_ln(u):
                if u:
                    sp.wait_ge(ln_done.sem, ln_done.ready(u * NT - 1))
                for n, v in enumerate((ln_g, ln_b)):
                    sp.dma_start(gb[:, n, :], v[u // 2, u % 2:u % 2 + 1, :].to_broadcast([P, D])).then_inc(gb_in, 16)

            def load_square(use, raw, view):
                for k in range(NK):
                    if k:
                        sp.wait_ge(wsq_lo_done.sem, wsq_lo_done.ready(use * NK + k - 1))
                    sp.dma_start(raw[:], view[k]).then_inc(wsq_in, 16)

            load_ln(0)
            sp.wait_ge(o_done.sem, o_done.ready(8 * PAIRS - 1))
            for t in range(NT):
                sp.dma_start(resid[:, t, :], x_v[t]).then_inc(xr_in[t], 16)
            load_square(0, wo_raw, wo_v)

            def load_ffn(l):
                def load_13(f, first=False):
                    if not first:
                        sp.wait_ge(w13_lo_done.sem, w13_lo_done.ready(f - 1 + l * NF))
                    for n, v in enumerate((w1_v[l], w3_v[l])):
                        sp.dma_start(w13_raw[:, n], v[:, :, bass.ds(f * P, P)]).then_inc(w13_in, 16)

                def load_2(f, first=False):
                    if not first:
                        sp.wait_ge(w2_lo_done.sem, w2_lo_done.ready(f - 1 + l * NF))
                    sp.dma_start(w2_raw[:], w2_v[l][:, bass.ds(f, 1), :].rearrange("p o n -> p (o n)")
                                 ).then_inc(w2_in, 16)

                load_13(0, True)
                load_13(1)
                load_2(0, True)
                with sp.Fori(0, NF - 2) as f:
                    load_13(f + 2)
                    load_2(f + 1)
                load_2(NF - 1)

            sp.wait_ge(pr_ps.sem, pr_ps.ready(NT - 1))
            sp.dma_start(bout_b[:], b_out[0:1, :].to_broadcast([P, D])).then_inc(bout_in, 16)
            load_ffn(0)
            load_ln(1)
            sp.wait_ge(acc_done.sem, acc_done.ready(NF * 16 - 1))

            def load_win(c, first=False):
                if not first:
                    sp.wait_ge(win_lo_done.sem, win_lo_done.ready(c - 1))
                for g in range(2):
                    sp.dma_start(win_raw[:, g], win_v[:, g, :, bass.ds(c * P, P)]).then_inc(win_in, 16)

            load_win(0, True)
            with sp.Fori(1, NK) as c:
                load_win(c)
            load_ln(2)
            sp.wait_ge(tap_done.sem, tap_done.ready(2 * NK * TAPS - 1))
            sp.wait_ge(ln_bout.sem, ln_bout.ready(NT - 1))
            load_square(1, wx_raw, wout_v)
            sp.wait_ge(pr_ps.sem, pr_ps.ready(2 * NT - 1))
            load_ffn(1)
            load_ln(3)
            for t in range(NT):
                sp.wait_ge(ln_done.sem, ln_done.ready(3 * NT + t))
                sp.dma_start(out_v[t], resid[:, t, :]).then_inc(stored, 16)
            sp.wait_ge(stored, 16 * NT)

        @block.tensor
        def _(pe):
            mm = nc.tensor.matmul

            def product(dst, terms, last_inc=None):
                n = len(terms)
                for m, ((a_hi, a_lo), (b_hi, b_lo)) in enumerate(terms):
                    mm(dst, a_hi, b_hi, start=m == 0, stop=False)
                    mm(dst, a_hi, b_lo, start=False, stop=False)
                    ins = mm(dst, a_lo, b_hi, start=False, stop=m == n - 1)
                return ins

            def transpose_tile(src, use, t):
                for k in range(NK):
                    ins = nc.tensor.transpose(ps[t % 2][:, tok[k]], src(k), ident[:])
                ins.then_inc(tp_ps.sem, 1)

            pe.wait_ge(started, 1)
            pe.wait_ge(made_consts, 1)
            pe.wait_ge(cols_in, 7 * 16)
            nc.tensor.transpose(ps[2][:, 0:N_COLS], vec_rows[0:N_COLS, :], ident[0:N_COLS, 0:N_COLS])
            for k in range(NK):
                ins = nc.tensor.transpose(ps[2][:, 64 + 32 * k:64 + 32 * k + TAPS], dw_rows[0:TAPS, tok[k]],
                                          ident[0:TAPS, 0:TAPS])
            ins.then_inc(cols_ps, 1)
            for t in range(NT):
                pe.wait_ge(x_in[t % 4], 16 * (t // 4 + 1))
                pe.wait_ge(tp_lo.sem, tp_lo.free(t, 2))
                transpose_tile(lambda k: x_stage[:, t % 4, tok[k]], 0, t)

            def transpose_c(t):
                pe.wait_ge(c_tok_done.sem, c_tok_done.ready(t))
                pe.wait_ge(ct_lo.sem, ct_lo.free(t, 2))
                dst = ps[t % 2]
                for j in range(5):
                    nc.tensor.transpose(dst[:, tok[j]], c_tok[:, tok[j]], ident[:])
                nc.tensor.transpose(dst[0:2 * ROPE, tok[5]], c_tok[:, 5 * P:5 * P + 2 * ROPE], ident[:]
                                    ).then_inc(ct_ps.sem, 1)

            pe.wait_ge(cols_done, 1)
            pe.wait_ge(tp_lo.sem, tp_lo.ready(NT - 1))
            for t in range(NT):
                pe.wait_ge(c_tok_done.sem, c_tok_done.free(t, 2))
                dst = ps[2 + t % 2]
                parts = ((dst[:, 0:Q_RANK], slice(0, Q_RANK)), (dst[:, HALF:HALF + DOWN - Q_RANK], slice(Q_RANK, DOWN)))
                for k in range(NK):
                    if t == 0:
                        pe.wait_ge(wd_lo_done.sem, wd_lo_done.ready(k))
                    for d, s in parts:
                        mm(d, actT_hi[:, k, tok[t]], wd_hi[:, k, s], start=k == 0, stop=False)
                        mm(d, actT_hi[:, k, tok[t]], wd_lo[:, k, s], start=False, stop=False)
                        ins = mm(d, actT_lo[:, k, tok[t]], wd_hi[:, k, s], start=False, stop=k == NK - 1)
                ins.then_inc(c_ps.sem, 1)
                if t:
                    transpose_c(t - 1)
            transpose_c(NT - 1)

            cq = [(cT_hi[:, k, :], cT_lo[:, k, :]) for k in range(NQ)]
            ckv = [(cT_hi[:, NQ + k, :], cT_lo[:, NQ + k, :]) for k in range(NKV)]

            def project(dst, w_hi, w_lo, s, c):
                for h in halves:
                    ins = product(dst[:, h], [((w_hi[:, k, s], w_lo[:, k, s]), (c_hi[:, h], c_lo[:, h]))
                                              for k, (c_hi, c_lo) in enumerate(c)])
                return ins

            def keys(i):
                pe.wait_ge(wa_lo_done.sem, wa_lo_done.ready(i))
                project(ps[0], wkv_hi, wkv_lo, slice(0, P), ckv).then_inc(k_ps.sem, 1)

            def queries(i):
                project(ps[1], wq_hi, wq_lo, slice(0, P), cq).then_inc(qn_ps.sem, 1)
                project(ps[2], wq_hi, wq_lo, slice(P, 2 * P), cq).then_inc(qr_ps.sem, 1)

            def values(i):
                pe.wait_ge(k_lo_done.sem, k_lo_done.ready(i))
                for t in range(NT):
                    ins = product(ps[0][:, tok[t]],
                                  [((c_hi[:, tok[t]], c_lo[:, tok[t]]), (wkv_hi[:, k, P:2 * P], wkv_lo[:, k, P:2 * P]))
                                   for k, (c_hi, c_lo) in enumerate(ckv)])
                ins.then_inc(v_ps.sem, 1)

            def scores(i, n):
                j, t = divmod(n, NT)
                pe.wait_ge(p_done.sem, p_done.free(i * NQT + n, 2))
                q = (q_hi[0:QK, j, tok[t]], q_lo[0:QK, j, tok[t]])
                for h in halves:
                    ins = product(ps[n % 2][:, h], [(q, (k_hi[0:QK, j, h], k_lo[0:QK, j, h]))])
                ins.then_inc(s_ps.sem, 1)

            def transposed(i, n):
                pe.wait_ge(p_done.sem, p_done.ready(i * NQT + n))
                for a in range(2):
                    pe.wait_ge(pt_lo_done.sem, pt_lo_done.free((i * NQT + n) * 2 + a, 2))
                    for kk in range(4):
                        ins = nc.tensor.transpose(ps[2][:, tok[4 * a + kk]], p_f[:, n % 2, tok[4 * a + kk]], ident[:])
                    ins.then_inc(pt_ps.sem, 1)

            def times_v(i, c):
                item = i * 8 + c
                pe.wait_ge(pt_lo_done.sem, pt_lo_done.ready(item * 4 + 3))
                pe.wait_ge(o_done.sem, o_done.free(item, 2))
                o = ps[3][:, HALF * (c % 2):HALF * (c % 2) + CHUNK]
                for k in range(NK):
                    v = v2[:, k, c // 4, :]
                    mm(o, v, pt_hi[:, c % 2, k, :], start=k == 0, stop=False)
                    mm(o, v, pt_lo[:, c % 2, k, :], start=False, stop=k == NK - 1)
                pe.wait_ge(diag_done.sem, diag_done.ready(item))
                mm(ps[3][0:VDIM, HALF * (c % 2) + CHUNK:HALF * (c % 2) + 2 * CHUNK], ones[:], diag[:, c % 2, :],
                   start=True, stop=True).then_inc(o_ps.sem, 1)

            def attend(i, more):
                pe.wait_ge(k_lo_done.sem, k_lo_done.ready(i))
                pe.wait_ge(qn_lo_done.sem, qn_lo_done.ready(i))
                pe.wait_ge(qr_lo_done.sem, qr_lo_done.ready(i))
                pe.wait_ge(v_lo_done.sem, v_lo_done.ready(i))
                scores(i, 0)
                for n in range(NQT):
                    if n + 1 < NQT:
                        scores(i, n + 1)
                    transposed(i, n)
                    if n % 2 == 0 and n:
                        times_v(i, n // 2 - 1)
                if more:
                    keys(i + 1)
                    pe.wait_ge(pt_lo_done.sem, pt_lo_done.ready((i * NQT + NQT) * 2 - 1))
                    queries(i + 1)
                times_v(i, 7)
                if more:
                    values(i + 1)

            pe.wait_ge(ct_lo.sem, ct_lo.ready(NT - 1))
            keys(0)
            queries(0)
            values(0)
            with pe.Fori(0, PAIRS - 1) as i:
                attend(i, True)
            attend(PAIRS - 1, False)

            def transpose_resid(use, t):
                pe.wait_ge(ln_done.sem, ln_done.ready((use - 1) * NT + t))
                pe.wait_ge(tp_lo.sem, tp_lo.free(use * NT + t, 2))
                transpose_tile(lambda k: resid[:, t, tok[k]], use, t)

            def square(use, ln, w_hi, w_lo):
                for t in range(NT):
                    pe.wait_ge(pr_add.sem, pr_add.free(use * NT + t, 2))
                    dst = ps[2 + t % 2]
                    for k in range(NK):
                        if t == 0:
                            pe.wait_ge(wsq_lo_done.sem, wsq_lo_done.ready(use * NK + k))
                        a_hi, a_lo = actT_hi[:, k, tok[t]], actT_lo[:, k, tok[t]]
                        for h in halves:
                            mm(dst[:, h], a_hi, w_hi[:, k, h], start=k == 0, stop=False)
                            mm(dst[:, h], a_hi, w_lo[:, k, h], start=False, stop=False)
                            ins = mm(dst[:, h], a_lo, w_hi[:, k, h], start=False, stop=k == NK - 1)
                    ins.then_inc(pr_ps.sem, 1)
                    if t:
                        transpose_resid(ln, t - 1)
                transpose_resid(ln, NT - 1)

            pe.wait_ge(oT_lo_done.sem, oT_lo_done.ready(NK - 1))
            pe.wait_ge(o_done.sem, o_done.ready(8 * PAIRS - 1))
            square(0, 1, wo_hi, wo_lo)

            def up(l, f, slot):
                item = f + l * NF
                pe.wait_ge(w13_lo_done.sem, w13_lo_done.ready(item))
                for n, h in enumerate(halves):
                    pe.wait_ge(hid_f_done.sem, hid_f_done.free(item * 2 + n, 2))
                    for g in range(2):
                        ins = product(ps[g][:, h], [((w13_hi[:, slot, g, k, :], w13_lo[:, slot, g, k, :]),
                                                     (actT_hi[:, k, h], actT_lo[:, k, h])) for k in range(NK)])
                    ins.then_inc(up_ps.sem, 1)

            def down(l, f, slot):
                item = f + l * NF
                pe.wait_ge(w2_lo_done.sem, w2_lo_done.ready(item))
                pe.wait_ge(hid_lo_done.sem, hid_lo_done.ready(item * 2 + 1))
                for m in range(2 * NT):
                    t, h = divmod(m, 2)
                    pe.wait_ge(acc_done.sem, acc_done.free(item * 16 + m, 4))
                    product(bank(m), [((hid_hi[:, slot, tok[t]], hid_lo[:, slot, tok[t]]),
                                       (w2_hi[:, slot, halves[h]], w2_lo[:, slot, halves[h]]))]
                            ).then_inc(down_ps.sem, 1)

            def ffn(l):
                up(l, 0, 0)
                with pe.Fori(0, NF // 2 - 1) as i:
                    up(l, i * 2 + 1, 1)
                    down(l, i * 2, 0)
                    up(l, i * 2 + 2, 0)
                    down(l, i * 2 + 1, 1)
                up(l, NF - 1, 1)
                down(l, NF - 2, 0)
                down(l, NF - 1, 1)

            pe.wait_ge(tp_lo.sem, tp_lo.ready(2 * NT - 1))
            pe.wait_ge(pr_add.sem, pr_add.ready(NT - 1))
            ffn(0)
            for t in range(NT):
                transpose_resid(2, t)

            def conv_in(c, slot):
                pe.wait_ge(win_lo_done.sem, win_lo_done.ready(c))
                for n, h in enumerate(halves):
                    pe.wait_ge(glu_done.sem, glu_done.free(c * 2 + n, 4))
                    for g in range(2):
                        ins = product(ps[2 * slot + g][:, h],
                                      [((win_hi[:, slot, g, k, :], win_lo[:, slot, g, k, :]),
                                        (actT_hi[:, k, h], actT_lo[:, k, h])) for k in range(NK)])
                    ins.then_inc(in_ps.sem, 1)

            pe.wait_ge(tp_lo.sem, tp_lo.ready(3 * NT - 1))
            with pe.Fori(0, NK // 2) as i:
                conv_in(i * 2, 0)
                conv_in(i * 2 + 1, 1)

            pe.wait_ge(tap_done.sem, tap_done.ready(2 * NK * TAPS - 1))

            def to_tokens(t):
                pe.wait_ge(cl_norm.sem, cl_norm.free(t, 2))
                for k in range(NK):
                    ins = nc.tensor.transpose(ps[t % 2][:, tok[k]], convT[:, k, tok[t]], ident[:])
                ins.then_inc(cl_ps.sem, 1)

            def to_channels(t):
                pe.wait_ge(cl_norm.sem, cl_norm.ready(t))
                pe.wait_ge(silu_done.sem, silu_done.free(t, 2))
                for k in range(NK):
                    ins = nc.tensor.transpose(ps[2 + t % 2][:, tok[k]], convT[:, k, tok[t]], ident[:])
                ins.then_inc(cb_ps.sem, 1)

            for t in range(NT):
                to_tokens(t)
                if t:
                    to_channels(t - 1)
            to_channels(NT - 1)
            pe.wait_ge(sT_lo_done.sem, sT_lo_done.ready(NT - 1))
            square(1, 3, wx_hi, wx_lo)
            pe.wait_ge(tp_lo.sem, tp_lo.ready(4 * NT - 1))
            pe.wait_ge(pr_add.sem, pr_add.ready(2 * NT - 1))
            ffn(1)

        @block.scalar
        def _(act):
            copy, activate = nc.scalar.copy, nc.scalar.activation

            def split_tile(use, t):
                act.wait_ge(tp_ps.sem, tp_ps.ready(use * NT + t))
                copy(actT_hi[:, :, tok[t]], ps[t % 2][:].rearrange("p (k n) -> p k n", k=NK)
                     ).then_inc(tp_hi.sem, 1)

            def split_wd(k):
                act.wait_ge(wd_in[k % 2], 32 * (k // 2 + 1))
                copy(wd_hi[:, k, :], wd_raw[:, k % 2, :]).then_inc(wd_hi_done.sem, 1)

            act.wait_ge(started, 1)
            act.wait_ge(ang_done, 1)
            activate(absr[:], ang[:], ACT.Abs).then_inc(act_steps, 1)
            activate(sinv[:], ang[:], ACT.Sin, scale=consts[:, 1:2]).then_inc(act_steps, 1)
            act.wait_ge(act_steps, 1)
            activate(cosv[:], absr[:], ACT.Sin, bias=consts[:, 2:3], scale=-1.0).then_inc(act_steps, 1)
            act.wait_ge(act_steps, 3)
            for q in range(4):
                rows, cs = slice(32 * q, 32 * q + 32), slice(CHUNK * q, CHUNK * (q + 1))
                copy(tab[0:32, cs], cosv[rows, :])
                ins = copy(tab[32:64, cs], sinv[rows, :])
            ins.then_inc(tab_done, 1)
            act.wait_ge(cols_ps, 1)
            copy(cols[:, 0:N_COLS], ps[2][:, 0:N_COLS])
            copy(dw_cols[:, :, 0:TAPS], ps[2][:, 64:64 + 32 * NK].rearrange("p (k j) -> p k j", k=NK)[:, :, 0:TAPS]
                 ).then_inc(cols_done, 1)
            for t in range(4):
                split_tile(0, t)
            split_wd(0)
            split_wd(1)
            for t in range(4, NT):
                split_tile(0, t)
                split_wd(t - 2)
            split_wd(6)
            split_wd(7)

            def squares(t):
                act.wait_ge(c_ps.sem, c_ps.ready(t))
                activate(x_stage[:, t % 2, 0:Q_RANK], ps[2 + t % 2][:, 0:Q_RANK], ACT.Square, accum_out=stats[:, t, 0:1])
                activate(x_stage[:, t % 2, HALF:HALF + KV_RANK], ps[2 + t % 2][:, HALF:HALF + KV_RANK], ACT.Square,
                         accum_out=stats[:, t, 1:2]).then_inc(c_sq.sem, 1)

            def split_c(t):
                act.wait_ge(ct_ps.sem, ct_ps.ready(t))
                for j in range(5):
                    ins = activate(cT_hi[:, j, tok[t]], ps[t % 2][:, tok[j]], ACT.Copy,
                                   scale=cols[:, C_GQ + j:C_GQ + j + 1])
                ins.then_inc(ct_hi.sem, 1)

            act.wait_ge(cols_done, 1)
            for t in range(NT):
                squares(t)
                if t:
                    split_c(t - 1)
            split_c(NT - 1)

            def split_pair(i, wait_used=True):
                if wait_used:
                    act.wait_ge(v_ps.sem, v_ps.ready(i - 1))
                act.wait_ge(wq_in, (i + 1) * 16)
                for dst, src in pair_views(wq_hi, wq_raw):
                    copy(dst, src)
                act.wait_ge(wkv_in, (i + 1) * 16)
                for dst, src in kv_views(wkv_hi, wkv_raw):
                    ins = copy(dst, src)
                ins.then_inc(wa_hi_done.sem, 1)

            def head_part(dst, src, j):
                return copy(dst[0:NOPE, j, :], src[NOPE * j:NOPE * (j + 1), :])

            def keys_queries(i):
                act.wait_ge(k_ps.sem, k_ps.ready(i))
                head_part(k_hi, ps[0], 0)
                head_part(k_hi, ps[0], 1).then_inc(k_hi_done.sem, 1)
                act.wait_ge(qn_ps.sem, qn_ps.ready(i))
                head_part(q_hi, ps[1], 0)
                head_part(q_hi, ps[1], 1).then_inc(qn_hi_done.sem, 1)
                act.wait_ge(qr_sum.sem, qr_sum.ready(i))
                copy(q_hi[NOPE:QK, :, :], rope_a[NOPE:QK, :, :]).then_inc(qr_hi_done.sem, 1)

            def values(i):
                act.wait_ge(v_ps.sem, v_ps.ready(i))
                copy(v2[:, :, :, 0:VDIM], ps[0][:].rearrange("p (t j d) -> p t j d", t=NT, j=2)
                     ).then_inc(v_hi_done.sem, 1)

            def exponentials(i, n):
                act.wait_ge(pt_ps.sem, pt_ps.free((i * NQT + n) * 2 + 1, 4))
                act.wait_ge(s_max.sem, s_max.ready(i * NQT + n))
                activate(p_f[:, n % 2, :], ps[n % 2][:], ACT.Exp, bias=negmax[:, n:n + 1], scale=SCALE,
                         accum_out=sums[:, n:n + 1]).then_inc(p_done.sem, 1)

            def split_probs(i, n):
                c = n // 2
                act.wait_ge(o_ps.sem, o_ps.free(i * 8 + c, 2))
                for a in range(2):
                    act.wait_ge(pt_ps.sem, pt_ps.ready((i * NQT + n) * 2 + a))
                    copy(pt_hi[:, c % 2, 4 * a:4 * a + 4, tok[n % 2]],
                         ps[2][:, halves[a]].rearrange("p (k n) -> p k n", k=4)).then_inc(pt_hi_done.sem, 1)

            def first_half(i, c):
                act.wait_ge(o_ps.sem, o_ps.ready(i * 8 + c))
                copy(o_first[0:VDIM, c % 2, :], ps[3][0:VDIM, HALF * (c % 2):HALF * (c % 2) + CHUNK]
                     ).then_inc(o_first_done.sem, 1)

            def attend(i, more):
                exponentials(i, 0)
                for n in range(NQT):
                    if n + 1 < NQT:
                        exponentials(i, n + 1)
                    split_probs(i, n)
                    if n % 2 == 0 and n:
                        first_half(i, n // 2 - 1)
                    if more and n == 3:
                        split_pair(i + 1)
                if more:
                    keys_queries(i + 1)
                first_half(i, 7)
                if more:
                    values(i + 1)

            split_pair(0, wait_used=False)
            act.wait_ge(ct_ps.sem, ct_ps.ready(NT - 1))
            act.wait_ge(krope_done, 1)
            for j in range(2):
                ins = copy(k_hi[NOPE:QK, j, :], rope_a[NOPE:QK, 0, :])
            ins.then_inc(krope_hi, 1)
            keys_queries(0)
            values(0)
            with act.Fori(0, PAIRS - 1) as i:
                attend(i, True)
            attend(PAIRS - 1, False)

            def split_square(use, w_hi, raw):
                for k in range(NK):
                    act.wait_ge(wsq_in, 16 * (use * NK + k + 1))
                    copy(w_hi[:, k, :], raw[:]).then_inc(wsq_hi_done.sem, 1)

            def rescale(use, t):
                act.wait_ge(tp_ps.sem, tp_ps.ready(use * NT + t))
                nc.scalar.mul(resid[:, t, :], resid[:, t, :], ALPHA).then_inc(ln_scaled.sem, 1)

            act.wait_ge(o_done.sem, o_done.ready(8 * PAIRS - 1))
            for k in range(NK):
                copy(actT_hi[:, k, :], oT_f[:, k, :]).then_inc(oT_hi_done.sem, 1)
            split_square(0, wo_hi, wo_raw)
            for t in range(NT):
                split_tile(1, t)
                rescale(1, t)

            def ffn(l):
                def split_13(f, slot, used=True):
                    item = f + l * NF
                    if used:
                        act.wait_ge(up_ps.sem, up_ps.ready((item - 2) * 2 + 1))
                    act.wait_ge(w13_in, (item + 1) * 32)
                    copy(w13_hi[:, slot], w13_raw[:]).then_inc(w13_hi_done.sem, 1)

                def split_2(f, slot, used=True):
                    item = f + l * NF
                    if used:
                        act.wait_ge(down_ps.sem, down_ps.ready((item - 2) * 16 + 15))
                    act.wait_ge(w2_in, (item + 1) * 16)
                    copy(w2_hi[:, slot, :], w2_raw[:]).then_inc(w2_hi_done.sem, 1)

                def hidden(f, slot, used=True):
                    item = f + l * NF
                    for n, h in enumerate(halves):
                        act.wait_ge(up_ps.sem, up_ps.ready(item * 2 + n))
                        act.wait_ge(hid_f_done.sem, hid_f_done.free(item * 2 + n, 2))
                        activate(gate[:, h], ps[0][:, h], ACT.Silu).then_inc(gate_done.sem, 1)
                    if used:
                        act.wait_ge(down_ps.sem, down_ps.ready((item - 2) * 16 + 15))
                    for n, h in enumerate(halves):
                        act.wait_ge(hid_f_done.sem, hid_f_done.ready(item * 2 + n))
                        copy(hid_hi[:, slot, h], hid_f[:, h]).then_inc(hid_hi_done.sem, 1)

                split_13(0, 0, False)
                split_13(1, 1, False)
                split_2(0, 0, False)
                hidden(0, 0, False)
                split_13(2, 0)
                split_2(1, 1, False)
                hidden(1, 1, False)
                split_13(3, 1)
                split_2(2, 0)
                with act.Fori(1, NF // 2 - 1) as i:
                    for b in range(2):
                        hidden(i * 2 + b, b)
                        split_13(i * 2 + b + 2, b)
                        split_2(i * 2 + b + 1, 1 - b)
                hidden(NF - 2, 0)
                split_2(NF - 1, 1)
                hidden(NF - 1, 1)

            act.wait_ge(pr_ps.sem, pr_ps.ready(NT - 1))
            ffn(0)
            for t in range(NT):
                split_tile(2, t)
                rescale(2, t)

            def split_win(c, slot, used=True):
                if used:
                    act.wait_ge(in_ps.sem, in_ps.ready((c - 2) * 2 + 1))
                act.wait_ge(win_in, (c + 1) * 32)
                copy(win_hi[:, slot], win_raw[:]).then_inc(win_hi_done.sem, 1)

            def sigmoids(c, slot):
                copy(bias_now[:, slot:slot + 1], cols[:, bass.ds(c + (C_BIN + NK), 1)]).then_inc(bias_now_done.sem, 1)
                for n, h in enumerate(halves):
                    act.wait_ge(bias_now_done.sem, bias_now_done.ready(c))
                    act.wait_ge(glu_done.sem, glu_done.free(c * 2 + n, 2))
                    act.wait_ge(in_ps.sem, in_ps.ready(c * 2 + n))
                    activate(sig[:, h], ps[2 * slot + 1][:, h], ACT.Sigmoid, bias=bias_now[:, slot:slot + 1]
                             ).then_inc(sig_done.sem, 1)

            act.wait_ge(acc_done.sem, acc_done.ready(NF * 16 - 1))
            split_win(0, 0, False)
            split_win(1, 1, False)
            with act.Fori(0, NK // 2 - 1) as i:
                for b in range(2):
                    sigmoids(i * 2 + b, b)
                    split_win(i * 2 + b + 2, b)
            sigmoids(NK - 2, 0)
            sigmoids(NK - 1, 1)

            act.wait_ge(tap_done.sem, tap_done.ready(2 * NK * TAPS - 1))
            act.wait_ge(ln_bout.sem, ln_bout.ready(NT - 1))
            split_square(1, wx_hi, wx_raw)
            for t in range(NT):
                act.wait_ge(cb_ps.sem, cb_ps.ready(t))
                for k in range(NK):
                    ins = activate(convT[:, k, tok[t]], ps[2 + t % 2][:, tok[k]], ACT.Silu,
                                   bias=cols[:, C_LNB + k:C_LNB + k + 1], scale=cols[:, C_LNG + k:C_LNG + k + 1])
                ins.then_inc(silu_done.sem, 1)
                act.wait_ge(silu_done.sem, silu_done.ready(t))
                copy(actT_hi[:, :, tok[t]], convT[:, :, tok[t]]).then_inc(sT_hi_done.sem, 1)
            for t in range(NT):
                split_tile(3, t)
                rescale(3, t)
            act.wait_ge(pr_ps.sem, pr_ps.ready(2 * NT - 1))
            ffn(1)

        @block.vector
        def _(v):
            V = nc.vector
            own = Chain(dve_steps, v)
            tt, sub = V.tensor_tensor, ALU.subtract

            v.wait_ge(started, 1)
            v.wait_ge(small_in, 5 * 16)
            own.link(V.tensor_scalar(ang[:], pos_i[:], consts[:, 0:1], None, ALU.mult))
            for size, count in ((2.0 ** 20, 4), (2.0 ** 10, 4), (1.0, 4)):
                own.link(V.tensor_scalar(turns[:], ang[:], 1.0 / (2 * math.pi * size), MAGIC, ALU.mult, ALU.add))
                own.link(V.tensor_scalar(turns[:], turns[:], MAGIC, None, ALU.subtract))
                for piece in turn_pieces(size, count):
                    own.link(V.scalar_tensor_tensor(out=ang[:], in0=turns[:], scalar=-piece, in1=ang[:],
                                                    op0=ALU.mult, op1=ALU.add))
            V.tensor_scalar(ang[:], ang[:], 3.1415925, -3.1415925, ALU.min, ALU.max).then_inc(ang_done, 1)

            def split_tile(use, t):
                v.wait_ge(tp_hi.sem, tp_hi.ready(use * NT + t))
                tt(actT_lo[:, :, tok[t]], ps[t % 2][:].rearrange("p (k n) -> p k n", k=NK),
                   actT_hi[:, :, tok[t]], sub).then_inc(tp_lo.sem, 1)

            for t in range(NT):
                split_tile(0, t)

            def norm_c(t):
                src = ps[2 + t % 2]
                v.wait_ge(c_sq.sem, c_sq.ready(t))
                V.tensor_scalar(mean_var[:, t, 0:1], stats[:, t, 0:1], 1.0 / Q_RANK, RMS_EPS, ALU.mult, ALU.add)
                V.tensor_scalar(mean_var[:, t, 1:2], stats[:, t, 1:2], 1.0 / KV_RANK, RMS_EPS, ALU.mult, ALU.add
                                ).then_inc(c_ms.sem, 1)
                v.wait_ge(c_rstd.sem, c_rstd.ready(t))
                v.wait_ge(ct_ps.sem, ct_ps.free(t, 1))
                V.tensor_scalar(c_tok[:, 0:Q_RANK], src[:, 0:Q_RANK], rstd[:, t, 0:1], None, ALU.mult)
                V.tensor_scalar(c_tok[:, Q_RANK:Q_RANK + KV_RANK], src[:, HALF:HALF + KV_RANK], rstd[:, t, 1:2],
                                None, ALU.mult)
                r0, h = HALF + KV_RANK, ROPE // 2
                V.tensor_copy(c_tok[:, 5 * P:5 * P + ROPE], src[:, r0:r0 + ROPE])
                V.tensor_copy(c_tok[:, 5 * P + ROPE:5 * P + ROPE + h], src[:, r0 + h:r0 + ROPE])
                V.tensor_copy(c_tok[:, 5 * P + ROPE + h:5 * P + 2 * ROPE], src[:, r0:r0 + h]
                              ).then_inc(c_tok_done.sem, 1)

            def split_c(t):
                v.wait_ge(ct_hi.sem, ct_hi.ready(t))
                for j in range(5):
                    V.scalar_tensor_tensor(out=cT_lo[:, j, tok[t]], in0=ps[t % 2][:, tok[j]],
                                           scalar=cols[:, C_GQ + j:C_GQ + j + 1], in1=cT_hi[:, j, tok[t]],
                                           op0=ALU.mult, op1=sub)
                V.tensor_copy(kr_f[0:2 * ROPE, tok[t]], ps[t % 2][0:2 * ROPE, tok[5]]).then_inc(ct_lo.sem, 1)

            v.wait_ge(cols_done, 1)
            for t in range(NT):
                norm_c(t)
                split_c(t)

            v.wait_ge(tab_done, 1)
            v.wait_ge(ct_lo.sem, ct_lo.ready(NT - 1))
            v.wait_ge(ct_ps.sem, ct_ps.ready(NT - 1))
            tt(rope_a[NOPE:QK, 0, :], kr_f[0:ROPE, :], tab[0:ROPE, :], ALU.mult)
            own.link(tt(rope_b[NOPE:QK, 0, :], kr_f[ROPE:2 * ROPE, :], tab[ROPE:2 * ROPE, :], ALU.mult))
            tt(rope_a[NOPE:QK, 0, :], rope_a[NOPE:QK, 0, :], rope_b[NOPE:QK, 0, :], ALU.add).then_inc(krope_done, 1)
            v.wait_ge(krope_hi, 1)
            for j in range(2):
                ins = tt(k_lo[NOPE:QK, j, :], rope_a[NOPE:QK, 0, :], k_hi[NOPE:QK, j, :], sub)
            ins.then_inc(krope_lo, 1)
            v.wait_ge(krope_lo, 1)

            def head_part(lo, hi, src, j):
                return tt(lo[0:NOPE, j, :], src[NOPE * j:NOPE * (j + 1), :], hi[0:NOPE, j, :], sub)

            def keys_queries(i):
                v.wait_ge(k_hi_done.sem, k_hi_done.ready(i))
                head_part(k_lo, k_hi, ps[0], 0)
                head_part(k_lo, k_hi, ps[0], 1).then_inc(k_lo_done.sem, 1)
                v.wait_ge(qr_ps.sem, qr_ps.ready(i))
                v.wait_ge(qr_lo_done.sem, qr_lo_done.free(i, 1))
                for j in range(2):
                    tt(rope_a[NOPE:QK, j, :], ps[2][ROPE * j:ROPE * (j + 1), :], tab[0:ROPE, :], ALU.mult)
                    ins = tt(rope_b[NOPE:QK, j, :], ps[2][ROPE * (2 + j):ROPE * (3 + j), :],
                             tab[ROPE:2 * ROPE, :], ALU.mult)
                ins.then_inc(qr_parts.sem, 1)
                v.wait_ge(qn_hi_done.sem, qn_hi_done.ready(i))
                head_part(q_lo, q_hi, ps[1], 0)
                head_part(q_lo, q_hi, ps[1], 1).then_inc(qn_lo_done.sem, 1)

            def values(i):
                v.wait_ge(v_hi_done.sem, v_hi_done.ready(i))
                tt(v2[:, :, :, VDIM:2 * VDIM], ps[0][:].rearrange("p (t j d) -> p t j d", t=NT, j=2),
                   v2[:, :, :, 0:VDIM], sub).then_inc(v_lo_done.sem, 1)

            def row_max(i, n):
                v.wait_ge(s_ps.sem, s_ps.ready(i * NQT + n))
                V.tensor_scalar(rope_b[:, n % 2, :], ps[n % 2][:], -SCALE, None, ALU.mult, ALU.min,
                                accum_out=negmax[:, n:n + 1]).then_inc(s_max.sem, 1)

            def split_probs(i, n):
                c = n // 2
                for a in range(2):
                    v.wait_ge(pt_hi_done.sem, pt_hi_done.ready((i * NQT + n) * 2 + a))
                    tt(pt_lo[:, c % 2, 4 * a:4 * a + 4, tok[n % 2]],
                       ps[2][:, halves[a]].rearrange("p (k n) -> p k n", k=4),
                       pt_hi[:, c % 2, 4 * a:4 * a + 4, tok[n % 2]], sub).then_inc(pt_lo_done.sem, 1)

            def inverse_sums(i, c):
                v.wait_ge(p_done.sem, p_done.ready(i * NQT + 2 * c + 1))
                V.reciprocal(rsums[:, 2 * c:2 * c + 2], sums[:, 2 * c:2 * c + 2]).then_inc(rsum_done.sem, 1)

            def outputs(i, c):
                item, b, j = i * 8 + c, HALF * (c % 2), c // 4
                v.wait_ge(o_first_done.sem, o_first_done.ready(item))
                tt(o_both[0:VDIM, :], ps[3][VDIM:P, b:b + CHUNK], o_first[0:VDIM, c % 2, :], ALU.add
                   ).then_inc(o_sum_done.sem, 1)
                v.wait_ge(o_sum_done.sem, o_sum_done.ready(item))
                q0 = (c % 4) * CHUNK
                dst = oT_f[VDIM * j:VDIM * (j + 1), bass.ds(i, 1), q0:q0 + CHUNK].rearrange("p o n -> p (o n)")
                tt(dst, ps[3][0:VDIM, b + CHUNK:b + 2 * CHUNK], o_both[0:VDIM, :], ALU.mult
                   ).then_inc(o_done.sem, 1)

            def attend(i, more):
                row_max(i, 0)
                for n in range(NQT):
                    if n + 1 < NQT:
                        row_max(i, n + 1)
                    split_probs(i, n)
                    if n % 2:
                        inverse_sums(i, n // 2)
                    if n % 2 == 0 and n:
                        outputs(i, n // 2 - 1)
                if more:
                    keys_queries(i + 1)
                outputs(i, 7)
                if more:
                    values(i + 1)

            keys_queries(0)
            values(0)
            with v.Fori(0, PAIRS - 1) as i:
                attend(i, True)
            attend(PAIRS - 1, False)

            def norm_tile(u, t):
                item = u * NT + t
                V.bn_stats(stats[:, t, 0:6], resid[:, t, halves[0]])
                own.link(V.bn_stats(stats[:, t, 6:12], resid[:, t, halves[1]]))
                own.link(V.bn_aggr(mean_var[:, t, :], stats[:, t, :]))
                V.tensor_scalar_add(mean_var[:, t, 1:2], mean_var[:, t, 1:2], LN_EPS).then_inc(ln_var.sem, 1)
                v.wait_ge(ln_rstd.sem, ln_rstd.ready(item))
                V.tensor_scalar(resid[:, t, :], resid[:, t, :], mean_var[:, t, 0:1], rstd[:, t, 0:1],
                                sub, ALU.mult).then_inc(ln_norm.sem, 1)

            def square(use, u, scale):
                for t in range(NT):
                    if use == 0:
                        v.wait_ge(xr_in[t], 16)
                    else:
                        v.wait_ge(ln_bout.sem, ln_bout.ready(t))
                    v.wait_ge(pr_ps.sem, pr_ps.ready(use * NT + t))
                    V.scalar_tensor_tensor(out=resid[:, t, :], in0=resid[:, t, :], scalar=scale,
                                           in1=ps[2 + t % 2][:], op0=ALU.mult, op1=ALU.add).then_inc(pr_add.sem, 1)
                    v.wait_ge(pr_add.sem, pr_add.ready(use * NT + t))
                    norm_tile(u, t)
                    if t:
                        split_tile(u + 1, t - 1)
                split_tile(u + 1, NT - 1)

            v.wait_ge(o_done.sem, o_done.ready(8 * PAIRS - 1))
            for k in range(NK):
                v.wait_ge(oT_hi_done.sem, oT_hi_done.ready(k))
                tt(actT_lo[:, k, :], oT_f[:, k, :], actT_hi[:, k, :], sub).then_inc(oT_lo_done.sem, 1)
            square(0, 0, ALPHA)

            def ffn(l):
                def hidden(f, slot):
                    item = f + l * NF
                    for n, h in enumerate(halves):
                        v.wait_ge(gate_done.sem, gate_done.ready(item * 2 + n))
                        v.wait_ge(hid_lo_done.sem, hid_lo_done.free(item * 2 + n, 2))
                        tt(hid_f[:, h], ps[1][:, h], gate[:, h], ALU.mult).then_inc(hid_f_done.sem, 1)
                    for n, h in enumerate(halves):
                        v.wait_ge(hid_hi_done.sem, hid_hi_done.ready(item * 2 + n))
                        tt(hid_lo[:, slot, h], hid_f[:, h], hid_hi[:, slot, h], sub).then_inc(hid_lo_done.sem, 1)

                def accumulate(f):
                    item = f + l * NF
                    for m in range(2 * NT):
                        t, h = divmod(m, 2)
                        v.wait_ge(down_ps.sem, down_ps.ready(item * 16 + m))
                        r = resid[:, t, halves[h]]
                        tt(r, bank(m), r, ALU.add).then_inc(acc_done.sem, 1)

                hidden(0, 0)
                with v.Fori(0, NF // 2 - 1) as i:
                    hidden(i * 2 + 1, 1)
                    accumulate(i * 2)
                    hidden(i * 2 + 2, 0)
                    accumulate(i * 2 + 1)
                hidden(NF - 1, 1)
                accumulate(NF - 2)
                accumulate(NF - 1)

            def ffn_norm(l, u, use):
                for t in range(NT):
                    v.wait_ge(acc_done.sem, acc_done.ready(((l + 1) * NF - 1) * 16 + 2 * t + 1))
                    norm_tile(u, t)
                    if t and use:
                        split_tile(use, t - 1)
                if use:
                    split_tile(use, NT - 1)

            v.wait_ge(ln_scaled.sem, ln_scaled.ready(NT - 1))
            ffn(0)
            ffn_norm(0, 1, 2)

            v.wait_ge(pads_done, 1)

            def gated(c, slot, column):
                for n, h in enumerate(halves):
                    v.wait_ge(sig_done.sem, sig_done.ready(c * 2 + n))
                    V.scalar_tensor_tensor(out=glu[:, slot, PAD + HALF * n:PAD + HALF * (n + 1)],
                                           in0=ps[2 * slot][:, h], scalar=column, in1=sig[:, h],
                                           op0=ALU.add, op1=ALU.mult).then_inc(glu_done.sem, 1)

            def taps(c, slot):
                V.tensor_copy(dw_now[:, slot, 0:TAPS], dw_cols[:, bass.ds(c, 1), 0:TAPS].rearrange("p o n -> p (o n)"))
                V.tensor_copy(dw_now[:, slot, TAPS:TAPS + 1], cols[:, bass.ds(c + C_DWB, 1)]
                              ).then_inc(dw_now_done.sem, 1)
                v.wait_ge(dw_now_done.sem, dw_now_done.ready(c))
                v.wait_ge(glu_done.sem, glu_done.ready(c * 2 + 1))
                for j in range(TAPS):
                    w = dw_now[:, slot, j:j + 1]
                    for n in range(2):
                        src = glu[:, slot, HALF * n + j:HALF * (n + 1) + j]
                        acc = conv_acc[:, halves[n]]
                        if j == 0:
                            ins = V.tensor_scalar(acc, src, w, dw_now[:, slot, TAPS:TAPS + 1], ALU.mult, ALU.add)
                        else:
                            v.wait_ge(tap_done.sem, tap_done.ready((c * TAPS + j - 1) * 2 + n))
                            dst = acc if j < TAPS - 1 else (
                                convT[:, bass.ds(c, 1), halves[n]].rearrange("p o n -> p (o n)"))
                            ins = V.scalar_tensor_tensor(out=dst, in0=src, scalar=w, in1=acc,
                                                         op0=ALU.mult, op1=ALU.add)
                        ins.then_inc(tap_done.sem, 1)

            with v.Fori(0, NK // 2) as i:
                for b in range(2):
                    gated(i * 2 + b, b, cols[:, bass.ds(i * 2 + (b + C_BIN), 1)])
                    taps(i * 2 + b, b)
            v.wait_ge(tap_done.sem, tap_done.ready(NK * TAPS * 2 - 1))

            for t in range(NT):
                src = ps[t % 2]
                v.wait_ge(cl_ps.sem, cl_ps.ready(t))
                V.bn_stats(stats[:, t, 0:6], src[:, halves[0]])
                own.link(V.bn_stats(stats[:, t, 6:12], src[:, halves[1]]))
                own.link(V.bn_aggr(mean_var[:, t, :], stats[:, t, :]))
                V.tensor_scalar_add(mean_var[:, t, 1:2], mean_var[:, t, 1:2], LN_EPS).then_inc(cl_var.sem, 1)
                v.wait_ge(cl_rstd.sem, cl_rstd.ready(t))
                V.tensor_scalar(convT[:, :, tok[t]], src[:].rearrange("p (k n) -> p k n", k=NK),
                                mean_var[:, t, 0:1], rstd[:, t, 0:1], sub, ALU.mult).then_inc(cl_norm.sem, 1)
                if t:
                    v.wait_ge(sT_hi_done.sem, sT_hi_done.ready(t - 1))
                    tt(actT_lo[:, :, tok[t - 1]], convT[:, :, tok[t - 1]], actT_hi[:, :, tok[t - 1]], sub
                       ).then_inc(sT_lo_done.sem, 1)
            v.wait_ge(sT_hi_done.sem, sT_hi_done.ready(NT - 1))
            tt(actT_lo[:, :, tok[NT - 1]], convT[:, :, tok[NT - 1]], actT_hi[:, :, tok[NT - 1]], sub
               ).then_inc(sT_lo_done.sem, 1)
            square(1, 2, 1.0)
            v.wait_ge(ln_scaled.sem, ln_scaled.ready(3 * NT - 1))
            ffn(1)
            ffn_norm(1, 3, 0)

        @block.gpsimd
        def _(pool):
            G = nc.gpsimd
            sub = ALU.subtract
            for f in flows:
                pool.sem_inc(f.sem, CREDIT)
            pool.sem_inc(started, 1)
            G.memset(ones[:], 1.0)
            G.memset(minus_half[:], -0.5).then_inc(pool_steps, 1)
            G.memset(ident[:], 0.0).then_inc(pool_steps, 1)
            pool.wait_ge(pool_steps, 2)
            G.affine_select(out=ident[:], in_=ident[:], compare_op=ALU.not_equal, fill=1.0, base=0,
                            pattern=[[-1, P]], channel_multiplier=1).then_inc(made_consts, 1)
            pool.wait_ge(made_consts, 1)
            for k in range(NK):
                pool.wait_ge(wd_hi_done.sem, wd_hi_done.ready(k))
                G.tensor_tensor(wd_lo[:, k, :], wd_raw[:, k % 2, :], wd_hi[:, k, :], sub).then_inc(wd_lo_done.sem, 1)
            for t in range(NT):
                pool.wait_ge(c_ms.sem, c_ms.ready(t))
                G.tensor_tensor(rstd[:, t, :], mean_var[:, t, :], minus_half[:], ALU.pow).then_inc(c_rstd.sem, 1)

            def split_pair(i):
                pool.wait_ge(wa_hi_done.sem, wa_hi_done.ready(i))
                for (lo, raw), (hi, _) in zip(pair_views(wq_lo, wq_raw) + kv_views(wkv_lo, wkv_raw),
                                              pair_views(wq_hi, wq_raw) + kv_views(wkv_hi, wkv_raw)):
                    ins = G.tensor_tensor(lo, raw, hi, sub)
                ins.then_inc(wa_lo_done.sem, 1)

            def rotate(i):
                a, b = rope_a[NOPE:QK, :, :], rope_b[NOPE:QK, :, :]
                pool.wait_ge(qr_parts.sem, qr_parts.ready(i))
                G.tensor_tensor(a, a, b, ALU.add).then_inc(qr_sum.sem, 1)
                pool.wait_ge(qr_hi_done.sem, qr_hi_done.ready(i))
                G.tensor_tensor(q_lo[NOPE:QK, :, :], a, q_hi[NOPE:QK, :, :], sub).then_inc(qr_lo_done.sem, 1)

            def inverse_diagonal(i, c):
                item = i * 8 + c
                pool.wait_ge(o_ps.sem, o_ps.free(item, 2))
                pool.wait_ge(rsum_done.sem, rsum_done.ready(item))
                for b in range(2):
                    n = 2 * c + b
                    ins = G.tensor_tensor(diag[:, c % 2, tok[b]], ident[:], rsums[:, n:n + 1].to_broadcast([P, P]),
                                          ALU.mult)
                ins.then_inc(diag_done.sem, 1)

            def attend(i, more):
                pool.wait_ge(qr_lo_done.sem, qr_lo_done.ready(i))
                for c in range(8):
                    inverse_diagonal(i, c)
                    if more and c == 1:
                        split_pair(i + 1)
                if more:
                    pool.wait_ge(diag_done.sem, diag_done.ready(i * 8 + 7))
                    rotate(i + 1)

            split_pair(0)
            pool.wait_ge(wa_lo_done.sem, wa_lo_done.ready(0))
            rotate(0)
            with pool.Fori(0, PAIRS - 1) as i:
                attend(i, True)
            attend(PAIRS - 1, False)

            def split_square(use, w_hi, w_lo, raw):
                for k in range(NK):
                    pool.wait_ge(wsq_hi_done.sem, wsq_hi_done.ready(use * NK + k))
                    G.tensor_tensor(w_lo[:, k, :], raw[:], w_hi[:, k, :], sub).then_inc(wsq_lo_done.sem, 1)

            def norm_tile(u, t):
                item = u * NT + t
                pool.wait_ge(ln_var.sem, ln_var.ready(item))
                G.tensor_tensor(rstd[:, t, 0:1], mean_var[:, t, 1:2], minus_half[:, 0:1], ALU.pow
                                ).then_inc(ln_rstd.sem, 1)
                pool.wait_ge(gb_in, (u + 1) * 32)
                pool.wait_ge(ln_norm.sem, ln_norm.ready(item))
                G.tensor_tensor(resid[:, t, :], resid[:, t, :], gb[:, 0, :], ALU.mult).then_inc(ln_g_done.sem, 1)
                pool.wait_ge(ln_g_done.sem, ln_g_done.ready(item))
                G.tensor_tensor(resid[:, t, :], resid[:, t, :], gb[:, 1, :], ALU.add).then_inc(ln_done.sem, 1)

            split_square(0, wo_hi, wo_lo, wo_raw)
            for t in range(NT):
                norm_tile(0, t)

            def ffn(l):
                def split_13(f, slot):
                    pool.wait_ge(w13_hi_done.sem, w13_hi_done.ready(f + l * NF))
                    G.tensor_tensor(w13_lo[:, slot], w13_raw[:], w13_hi[:, slot], sub).then_inc(w13_lo_done.sem, 1)

                def split_2(f, slot):
                    pool.wait_ge(w2_hi_done.sem, w2_hi_done.ready(f + l * NF))
                    G.tensor_tensor(w2_lo[:, slot, :], w2_raw[:], w2_hi[:, slot, :], sub).then_inc(w2_lo_done.sem, 1)

                split_13(0, 0)
                split_13(1, 1)
                split_2(0, 0)
                with pool.Fori(0, NF // 2 - 1) as i:
                    for b in range(2):
                        split_13(i * 2 + b + 2, b)
                        split_2(i * 2 + b + 1, 1 - b)
                split_2(NF - 1, 1)

            ffn(0)
            for t in range(NT):
                norm_tile(1, t)
                if t == 0:
                    pool.wait_ge(bout_in, 16)
                pool.wait_ge(ln_scaled.sem, ln_scaled.ready(NT + t))
                G.tensor_tensor(resid[:, t, :], resid[:, t, :], bout_b[:], ALU.add).then_inc(ln_bout.sem, 1)

            pool.wait_ge(acc_done.sem, acc_done.ready(NF * 16 - 1))
            G.memset(glu[:, :, 0:PAD], 0.0)
            G.memset(glu[:, :, PAD + SEQ:], 0.0).then_inc(pads_done, 1)
            def split_win(c, slot):
                pool.wait_ge(win_hi_done.sem, win_hi_done.ready(c))
                G.tensor_tensor(win_lo[:, slot], win_raw[:], win_hi[:, slot], sub).then_inc(win_lo_done.sem, 1)

            with pool.Fori(0, NK // 2) as i:
                split_win(i * 2, 0)
                split_win(i * 2 + 1, 1)
            split_square(1, wx_hi, wx_lo, wx_raw)
            for t in range(NT):
                pool.wait_ge(cl_var.sem, cl_var.ready(t))
                G.tensor_tensor(rstd[:, t, 0:1], mean_var[:, t, 1:2], minus_half[:, 0:1], ALU.pow
                                ).then_inc(cl_rstd.sem, 1)
            for t in range(NT):
                norm_tile(2, t)
            ffn(1)
            for t in range(NT):
                norm_tile(3, t)


_INS = ['x', 'positions', 'ln_g', 'ln_b', 'mla_w_dq', 'mla_q_norm', 'mla_w_uq', 'mla_w_dkv', 'mla_kv_norm',
        'mla_w_ukv', 'mla_w_o', 'conv_w_in', 'conv_b_in', 'conv_dw', 'conv_dw_b', 'conv_ln_g', 'conv_ln_b',
        'conv_w_out', 'conv_b_out', 'ffn_w1', 'ffn_w3', 'ffn_w2']


def kernel(**inputs):
    import concourse.bacc as bacc
    from concourse.bass_utils import run_bass_kernel_spmd as run

    nc = bacc.Bacc("TRN2", target_bir_lowering=False, num_devices=1)
    arrays, args = {}, []

    def add(name, a):
        arrays[name] = a
        args.append(nc.dram_tensor(name, a.shape, mybir.dt.from_np(a.dtype), kind="ExternalInput").ap())

    for name in _INS:
        add(f"in_{name}_dram", np.ascontiguousarray(inputs[name]))
    j = np.arange(P) % ROPE
    exponent = (-2.0 * (j % (ROPE // 2)) / ROPE).astype(np.float32)
    inv_freq = np.float32(10000.0) ** exponent
    rope_const = np.stack([inv_freq, np.where(j < ROPE // 2, -1.0, 1.0), np.full(P, math.pi / 2)], axis=1)
    add("rope_const_dram", np.ascontiguousarray(rope_const.astype(np.float32)))
    args.append(nc.dram_tensor("out_0_dram", (1, SEQ, D), F32, kind="ExternalOutput").ap())
    trunk(nc, *args)
    r = run(nc, [arrays], core_ids=[0])
    return r.results[0]["out_0_dram"]
```

```python
import math
from contextlib import ExitStack

import numpy as np
import concourse.bass as bass
from concourse import mybir

F32 = mybir.dt.float32
F32R = mybir.dt.float32r
I32 = mybir.dt.int32
ALU = mybir.AluOpType
ACT = mybir.ActivationFunctionType

P = 128
D = 1024
SEQ = 1024
NK = D // P
NT = SEQ // P
HALF = 512
HEADS, NOPE, ROPE, VDIM = 16, 64, 32, 64
QK = NOPE + ROPE
PAIRS = HEADS // 2
Q_RANK, KV_RANK = 384, 256
NQ, NKV = Q_RANK // P, KV_RANK // P
DOWN = Q_RANK + KV_RANK + ROPE
D_FF = 2816
NF = D_FF // P
TAPS = 31
PAD = TAPS // 2
PE_TAPS = 8
ALPHA = float(4 ** 0.25)
LN_EPS, RMS_EPS = 1e-5, 1e-6
SCALE = 1.0 / math.sqrt(QK)
QUARTER = SEQ // 4
CHUNK = 4 * P
NQT = 2 * NT
NC = NQT * P // CHUNK
CREDIT = 4
MAGIC = 1.5 * 2.0 ** 23


class Flow:

    def __init__(self, sem):
        self.sem = sem

    def ready(self, item):
        return item + (1 + CREDIT)

    def free(self, item, slots):
        return item + (1 - slots + CREDIT)


class Chain:

    def __init__(self, sem, eng):
        self.sem, self.eng, self.count = sem, eng, 0

    def link(self, ins):
        ins.then_inc(self.sem, 1)
        self.count += 1
        self.eng.wait_ge(self.sem, self.count)


def turn_pieces(turns, count):
    rest, out = 2 * math.pi * turns, []
    for _ in range(count):
        unit = 2.0 ** (math.floor(math.log2(rest)) - 11)
        out.append(math.floor(rest / unit) * unit)
        rest -= out[-1]
    return out


def pair_views(w, raw):
    src = raw[:].rearrange("p k (j d) -> p k j d", j=2)
    h = ROPE // 2

    def dst(a, d):
        return w[:, :, a:a + 2 * d].rearrange("p k (j d) -> p k j d", j=2)

    swapped = dst(P + 2 * ROPE, ROPE)
    return [(dst(0, NOPE), src[:, :, :, 0:NOPE]), (dst(P, ROPE), src[:, :, :, NOPE:QK]),
            (swapped[:, :, :, 0:h], src[:, :, :, NOPE + h:QK]), (swapped[:, :, :, h:ROPE], src[:, :, :, NOPE:NOPE + h])]


def kv_views(w, raw):
    src = raw[:].rearrange("p k (j d) -> p k j d", j=2)
    return [(w[:, :, a:a + P].rearrange("p k (j d) -> p k j d", j=2), src[:, :, :, b:b + NOPE])
            for a, b in ((0, 0), (P, NOPE))]


def trunk(nc, x, positions, ln_g, ln_b, w_dq, q_norm, w_uq, w_dkv, kv_norm, w_ukv, w_o, w_in, b_in,
          conv_dw, conv_dw_b, conv_ln_g, conv_ln_b, w_out, b_out, ffn_w1, ffn_w3, ffn_w2, rope_const, out):
    x_v = x[0].rearrange("(t p) d -> t p d", p=P)
    out_v = out[0].rearrange("(t p) d -> t p d", p=P)
    dq_v = w_dq[0].rearrange("(k p) n -> p k n", p=P)
    dkv_v = w_dkv[0].rearrange("(k p) n -> p k n", p=P)
    uq_v = w_uq[0].rearrange("(k p) n -> p k n", p=P)
    ukv_v = w_ukv[0].rearrange("(k p) n -> p k n", p=P)
    wo_v = w_o[0].rearrange("(k p) n -> k p n", p=P)
    wout_v = w_out[0].rearrange("(k p) n -> k p n", p=P)
    win_v = w_in[0].rearrange("(k p) (g n) -> p g k n", p=P, g=2)
    w1_v = [ffn_w1[l].rearrange("(k p) n -> p k n", p=P) for l in range(2)]
    w3_v = [ffn_w3[l].rearrange("(k p) n -> p k n", p=P) for l in range(2)]
    w2_v = [ffn_w2[l].rearrange("(f p) n -> p f n", p=P) for l in range(2)]

    ctx = ExitStack()
    with ctx:
        def sb(name, shape, dt=F32):
            return ctx.enter_context(nc.sbuf_tensor(name, shape, dt))

        gaps = [0]
        KEPT = 8

        def region(start_kb, *specs):
            got = []
            with ExitStack() as r:
                if start_kb > -KEPT:
                    gaps[0] += 1
                    r.enter_context(nc.sbuf_tensor(f"gap{gaps[0]}", [P, (KEPT + start_kb) * 256], F32))
                for name, shape, dt in specs:
                    got.append(r.enter_context(nc.sbuf_tensor(name, shape, dt)))
            return got

        def flow(name):
            f = Flow(ctx.enter_context(nc.semaphore(name)))
            flows.append(f)
            return f

        def sem(name):
            return ctx.enter_context(nc.semaphore(name))

        flows = []

        ident = sb("ident", [P, P])
        minus_half = sb("minus_half", [P, 2])
        consts = sb("consts", [P, 4])
        cols = sb("cols", [P, 48])
        conv_cols = sb("conv_cols", [P, NK, 50])
        conv_now = sb("conv_now", [P, 2, 50])
        dw_hi = sb("dw_hi", [P, NK, PE_TAPS], F32R)
        stats = sb("stats", [P, NT, 12])
        mean_var = sb("mean_var", [P, NT, 2])
        rstd = sb("rstd", [P, NT, 2])
        negmax = sb("negmax", [P, NQT])
        sums = sb("sums", [P, NQT])
        rsums = sb("rsums", [P, NQT])
        C_GQ, C_BIN, C_DWB, C_LNG, C_LNB = 0, 5, 21, 29, 37
        N_COLS = 45
        CC_DW, CC_BIAS, CC_VALUE, CC_GATE, CC_HI, CC_LO = 0, 31, 32, 33, 34, 42

        [gb] = region(-KEPT, ("gb", [P, 2, D], F32))
        diag_hi, diag_lo = region(-KEPT, ("diag_hi", [P, PE_TAPS, P], F32R), ("diag_lo", [P, PE_TAPS, P], F32R))
        actT_hi, actT_lo = region(32, ("actT_hi", [P, NK, SEQ], F32R), ("actT_lo", [P, NK, SEQ], F32R))
        [resid] = region(0, ("resid", [P, NT, D], F32))
        [x_stage] = region(0, ("x_stage", [P, 4, D], F32))
        [vec_rows, dw_rows, pos_i, ang, turns, cosv, sinv, absr] = region(
            16, ("vec_rows", [P, P], F32), ("dw_rows", [P, D], F32), ("pos_i", [P, QUARTER], I32),
            ("ang", [P, QUARTER], F32), ("turns", [P, QUARTER], F32), ("cosv", [P, QUARTER], F32),
            ("sinv", [P, QUARTER], F32), ("absr", [P, QUARTER], F32))
        cT_hi, cT_lo, tab, kr_f = region(96, ("cT_hi", [P, 5, SEQ], F32R), ("cT_lo", [P, 5, SEQ], F32R),
                                         ("tab", [P, SEQ], F32), ("kr_f", [P, SEQ], F32))
        [wd_hi, wd_lo] = region(144, ("wd_hi", [P, NK, DOWN], F32R), ("wd_lo", [P, NK, DOWN], F32R))
        wd_raw, c_tok = region(187, ("wd_raw", [P, 2, DOWN], F32), ("c_tok", [P, DOWN + ROPE], F32))
        [pt_hi, pt_lo] = region(0, ("pt_hi", [P, 2, NK, CHUNK], F32R), ("pt_lo", [P, 2, NK, CHUNK], F32R))
        q_hi, q_lo, k_hi, k_lo = region(
            64, ("q_hi", [P, 2, SEQ], F32R), ("q_lo", [P, 2, SEQ], F32R),
            ("k_hi", [P, 2, SEQ], F32R), ("k_lo", [P, 2, SEQ], F32R))
        [oT_f] = region(64, ("oT_f", [P, NK, SEQ], F32))
        (v2, p_f, rope_m, wq_hi, wq_lo, wkv_hi, wkv_lo, wq_raw, wkv_raw, o_sum, vT) = region(
            140, ("v2", [P, NT, 2, 2 * VDIM], F32R), ("p_f", [P, 3, SEQ], F32), ("rope_m", [P, 2, SEQ], F32),
            ("wq_hi", [P, NQ, 2 * P], F32R), ("wq_lo", [P, NQ, 2 * P], F32R),
            ("wkv_hi", [P, NKV, 2 * P], F32R), ("wkv_lo", [P, NKV, 2 * P], F32R),
            ("wq_raw", [P, NQ, 2 * QK], F32), ("wkv_raw", [P, NKV, 2 * P], F32),
            ("o_sum", [P, 2, CHUNK], F32), ("vT", [P, SEQ], F32))
        oT_dram = nc.dram_tensor("oT_dram", (NK, P, SEQ), F32, kind="Internal").ap()
        wo_lo, wo_hi = region(96, ("wo_lo", [P, NK, D], F32R), ("wo_hi", [P, NK, D], F32R))
        [wo_raw] = region(96, ("wo_raw", [P, NK, D], F32))
        wx_hi, wx_lo = region(128, ("wx_hi", [P, NK, D], F32R), ("wx_lo", [P, NK, D], F32R))
        [wx_raw] = region(160, ("wx_raw", [P, NK, D], F32))

        def up_weights(start, tag):
            hi, lo = region(start, (f"w13_hi{tag}", [P, 2, 2, NK, P], F32R), (f"w13_lo{tag}", [P, 2, 2, NK, P], F32R))
            [raw] = region(start + 16, (f"w13_raw{tag}", [P, 2, 2, NK, P], F32))
            return hi, lo, raw

        def ffn_memory(start, tag):
            hid_hi, hid_lo, w2_hi, w2_lo, gate, hid_f = region(
                start, (f"hid_hi{tag}", [P, 2, SEQ], F32R), (f"hid_lo{tag}", [P, 2, SEQ], F32R),
                (f"w2_hi{tag}", [P, 2, D], F32R), (f"w2_lo{tag}", [P, 2, D], F32R),
                (f"gate{tag}", [P, SEQ], F32), (f"hid_f{tag}", [P, SEQ], F32))
            [w2_raw] = region(start + 24, (f"w2_raw{tag}", [P, 2, D], F32))
            return hid_hi, hid_lo, w2_hi, w2_lo, w2_raw, gate, hid_f

        win_hi, win_lo, win_raw = up_weights(161, 0)
        up_w = [(win_hi, win_lo, win_raw), up_weights(96, 1)]
        ffn_m = [ffn_memory(96, 0), ffn_memory(128, 1)]
        [bout_b] = region(136, ("bout_b", [P, D], F32))
        convT, glu, glu_hi, glu_lo, sig, conv_acc = region(
            96, ("convT", [P, NK, SEQ], F32), ("glu", [P, 2, SEQ + 2 * PAD], F32),
            ("glu_hi", [P, 2, SEQ + 2 * PAD], F32R), ("glu_lo", [P, 2, SEQ + 2 * PAD], F32R),
            ("sig", [P, SEQ], F32), ("conv_acc", [P, SEQ], F32))

        ps = [ctx.enter_context(nc.psum_tensor(f"ps{i}", [P, 2 * HALF], F32)) for i in range(4)]

        started = sem("started")
        x_in = [sem(f"x_in{i}") for i in range(4)]
        small_in = sem("small_in")
        cols_in = sem("cols_in")
        wd_in = [sem(f"wd_in{i}") for i in range(2)]
        made_consts = sem("made_consts")
        cols_ps, cols_done = sem("cols_ps"), sem("cols_done")
        ang_done, tab_done = sem("ang_done"), sem("tab_done")
        tp_ps, tp_hi, tp_lo = flow("tp_ps"), flow("tp_hi"), flow("tp_lo")
        wd_hi_done, wd_lo_done = flow("wd_hi_done"), flow("wd_lo_done")
        c_ps, c_sq, c_ms, c_rstd, c_tok_done = (flow(n) for n in ("c_ps", "c_sq", "c_ms", "c_rstd", "c_tok_done"))
        ct_ps, ct_hi, ct_lo = flow("ct_ps"), flow("ct_hi"), flow("ct_lo")
        krope_done, krope_hi, krope_lo = sem("krope_done"), sem("krope_hi"), sem("krope_lo")
        wq_in, wkv_in = sem("wq_in"), sem("wkv_in")
        wa_hi_done, wa_lo_done = flow("wa_hi_done"), flow("wa_lo_done")
        k_ps, qn_ps, qr_ps, vt_ps, v_ps, vt_done = (flow(n) for n in ("k_ps", "qn_ps", "qr_ps", "vt_ps", "v_ps", "vt_done"))
        o_stored = [flow(f"o_stored{b}") for b in range(2)]
        oT_in = [sem(f"oT_in{k}") for k in range(NK)]
        k_hi_done, k_lo_done, qn_hi_done, qn_lo_done = (flow(n) for n in (
            "k_hi_done", "k_lo_done", "qn_hi_done", "qn_lo_done"))
        v_hi_done, v_lo_done = flow("v_hi_done"), flow("v_lo_done")
        qr_parts, qr_sum, qr_hi_done, qr_lo_done = (flow(n) for n in (
            "qr_parts", "qr_sum", "qr_hi_done", "qr_lo_done"))
        s_ps, s_max, p_done = flow("s_ps"), flow("s_max"), flow("p_done")
        pt_ps, pt_hi_done, pt_lo_done = flow("pt_ps"), flow("pt_hi_done"), flow("pt_lo_done")
        rsum_done, p_normed, o_ps, o_first_done, o_done = (flow(n) for n in (
            "rsum_done", "p_normed", "o_ps", "o_first_done", "o_done"))
        xr_in = [sem(f"xr_in{i}") for i in range(NT)]
        oT_hi_done, oT_lo_done = flow("oT_hi_done"), flow("oT_lo_done")
        wsq_in = [sem(f"wsq_in{k}") for k in range(NK)]
        wsq_hi_done, wsq_even_lo, wsq_odd_lo = flow("wsq_hi_done"), flow("wsq_even_lo"), flow("wsq_odd_lo")
        pr_ps, pr_add = flow("pr_ps"), flow("pr_add")
        gb_in = sem("gb_in")
        bout_in = sem("bout_in")
        ln_var, ln_rstd, ln_centred, ln_unit, ln_done, ln_scaled, ln_bout = (flow(n) for n in (
            "ln_var", "ln_rstd", "ln_centred", "ln_unit", "ln_done", "ln_scaled", "ln_bout"))
        w13_in, w2_in = [sem(f"w13_in{b}") for b in range(2)], [sem(f"w2_in{b}") for b in range(2)]
        w13_hi_done, w13_lo_done, w2_hi_done, w2_lo_done = (flow(n) for n in (
            "w13_hi_done", "w13_lo_done", "w2_hi_done", "w2_lo_done"))
        up_ps, gate_done, hid_f_done, hid_hi_done, hid_lo_done, down_ps, acc_done = (flow(n) for n in (
            "up_ps", "gate_done", "hid_f_done", "hid_hi_done", "hid_lo_done", "down_ps", "acc_done"))
        win_in = [sem(f"win_in{b}") for b in range(2)]
        (win_hi_done, win_lo_done, in_ps, sig_done, glu_done, glu_hi_done, glu_lo_done, now_done, diag_done, conv_ps,
         conv_out, tap_done) = (flow(n) for n in (
            "win_hi_done", "win_lo_done", "in_ps", "sig_done", "glu_done", "glu_hi_done", "glu_lo_done", "now_done",
            "diag_done", "conv_ps", "conv_out", "tap_done"))
        cc_done = sem("cc_done")
        pads_done = sem("pads_done")
        cl_ps, cl_var, cl_rstd, cl_norm, cb_ps, silu_done, sT_hi_done, sT_lo_done = (flow(n) for n in (
            "cl_ps", "cl_var", "cl_rstd", "cl_norm", "cb_ps", "silu_done", "sT_hi_done", "sT_lo_done"))
        stored = sem("stored")
        dve_steps, act_steps, pool_steps = sem("dve_steps"), sem("act_steps"), sem("pool_steps")

        block = ctx.enter_context(nc.Block())
        tok = [slice(t * P, (t + 1) * P) for t in range(NT)]
        halves = [slice(0, HALF), slice(HALF, 2 * HALF)]

        def bank(m):
            return ps[2 + m % 4 // 2][:, halves[m % 2]]

        def turned(use, t):
            if use == 2 and t >= 4:
                return ps[2 + t % 2]
            return ps[2] if use in (1, 3) and t == NT - 1 else ps[t % 2]

        @block.sync
        def _(sp):
            with nc.allow_non_contiguous_dma(reason="vectors of a few hundred elements"):
                sp.dma_start(consts[:, 0:3], rope_const).then_inc(small_in, 16)
                for q in range(4):
                    sp.dma_start(pos_i[32 * q:32 * q + 32, :],
                                 positions[:, QUARTER * q:QUARTER * (q + 1)].to_broadcast([32, QUARTER])
                                 ).then_inc(small_in, 16)
                for t in range(4):
                    sp.dma_start(x_stage[:, t, :], x_v[t]).then_inc(x_in[t], 16)
                for row, v, n in ((C_GQ, q_norm, NQ), (C_GQ + NQ, kv_norm, NKV), (C_BIN, b_in, 2 * NK),
                                  (C_DWB, conv_dw_b, NK), (C_LNG, conv_ln_g, NK), (C_LNB, conv_ln_b, NK)):
                    sp.dma_start(vec_rows[row:row + n, :], v[0].rearrange("(r p) -> r p", p=P)).then_inc(cols_in, 16)
                sp.dma_start(dw_rows[0:TAPS, :], conv_dw[0]).then_inc(cols_in, 16)
            def load_wd(k):
                if k >= 2:
                    sp.wait_ge(wd_lo_done.sem, wd_lo_done.free(k, 2))
                sp.dma_start(wd_raw[:, k % 2, 0:Q_RANK], dq_v[:, k, :]).then_inc(wd_in[k % 2], 16)
                sp.dma_start(wd_raw[:, k % 2, Q_RANK:DOWN], dkv_v[:, k, :]).then_inc(wd_in[k % 2], 16)

            sp.wait_ge(started, 1)
            load_wd(0)
            load_wd(1)
            for t in range(4, NT):
                sp.wait_ge(tp_ps.sem, tp_ps.ready(t - 4))
                sp.dma_start(x_stage[:, t % 4, :], x_v[t]).then_inc(x_in[t % 4], 16)
                load_wd(2 + t - 4)
            for k in range(6, NK):
                load_wd(k)

            sp.wait_ge(ct_ps.sem, ct_ps.ready(NT - 1))
            sp.wait_ge(c_tok_done.sem, c_tok_done.ready(NT - 1))

            def load_pair(i):
                sp.dma_start(wq_raw[:], uq_v[:, :, bass.ds(i * (2 * QK), 2 * QK)]).then_inc(wq_in, 16)
                sp.dma_start(wkv_raw[:], ukv_v[:, :, bass.ds(i * (2 * P), 2 * P)]).then_inc(wkv_in, 16)

            def store_outputs(i):
                for c in range(NC):
                    sp.wait_ge(o_done.sem, o_done.ready(i * NC + c))
                    rows, q0 = slice(VDIM * (c // 2), VDIM * (c // 2 + 1)), CHUNK * (c % 2)
                    sp.dma_start(oT_dram[bass.ds(i, 1), rows, q0:q0 + CHUNK].rearrange("o p n -> (o p) n"),
                                 o_sum[0:VDIM, c % 2, :]).then_inc(o_stored[c % 2].sem, 16)

            load_pair(0)
            with sp.Fori(0, PAIRS - 1) as i:
                sp.wait_ge(wa_lo_done.sem, wa_lo_done.ready(i))
                load_pair(i + 1)
                store_outputs(i)

            def load_ln(u):
                if u:
                    sp.wait_ge(ln_done.sem, ln_done.ready(u * NT - 1))
                for n, v in enumerate((ln_g, ln_b)):
                    sp.dma_start(gb[:, n, :], v[u // 2, u % 2:u % 2 + 1, :].to_broadcast([P, D])).then_inc(gb_in, 16)

            load_ln(0)
            sp.wait_ge(vt_ps.sem, vt_ps.ready(PAIRS - 1))
            for k in range(NK):
                sp.dma_start(wo_raw[:, k, :], wo_v[k]).then_inc(wsq_in[k], 16)
            store_outputs(PAIRS - 1)
            for k in range(NK):
                if k in (0, NK - 1):
                    for slot in o_stored:
                        sp.wait_ge(slot.sem, 16 * 2 * (PAIRS if k else PAIRS - 1) + CREDIT)
                sp.dma_start(oT_f[:, k, :], oT_dram[k]).then_inc(oT_in[k], 16)
            for t in range(NT):
                sp.dma_start(resid[:, t, :], x_v[t]).then_inc(xr_in[t], 16)

            def ffn_loads(l):
                def load_13(f, slot, used=True):
                    if used:
                        sp.wait_ge(up_ps.sem, up_ps.ready((f - 2 + l * NF) * 2 + 1))
                    for n, v in enumerate((w1_v[l], w3_v[l])):
                        sp.dma_start(up_w[l][2][:, slot, n], v[:, :, bass.ds(f * P, P)]).then_inc(w13_in[slot], 16)

                def load_2(f, slot, used=True):
                    if used:
                        sp.wait_ge(down_ps.sem, down_ps.ready((f - 2 + l * NF) * 16 + 15))
                    sp.dma_start(ffn_m[l][4][:, slot, :], w2_v[l][:, bass.ds(f, 1), :].rearrange("p o n -> p (o n)")
                                 ).then_inc(w2_in[slot], 16)
                return load_13, load_2

            def load_ffn(l):
                load_13, load_2 = ffn_loads(l)
                load_2(0, 0, False)
                load_2(1, 1, False)
                with sp.Fori(1, NF // 2) as i:
                    for b in range(2):
                        load_13(i * 2 + b, b)
                        load_2(i * 2 + b, b)

            for b in range(2):
                ffn_loads(0)[0](b, b, False)
            sp.wait_ge(pr_ps.sem, pr_ps.ready(NT - 1))
            sp.dma_start(bout_b[:], b_out[0:1, :].to_broadcast([P, D])).then_inc(bout_in, 16)
            load_ffn(0)
            load_ln(1)

            def load_win(c, slot):
                for g in range(2):
                    sp.dma_start(win_raw[:, slot, g], win_v[:, g, :, bass.ds(c * P, P)]).then_inc(win_in[slot], 16)

            for b in range(2):
                sp.wait_ge(up_ps.sem, up_ps.ready((NF - 2 + b) * 2 + 1))
                load_win(b, b)
            with sp.Fori(1, NK // 2) as i:
                for b in range(2):
                    sp.wait_ge(in_ps.sem, in_ps.ready((i * 2 + (b - 2)) * 2 + 1))
                    load_win(i * 2 + b, b)
            sp.wait_ge(conv_ps.sem, conv_ps.ready(NK - 1))
            load_ln(2)
            sp.wait_ge(tap_done.sem, tap_done.ready(2 * NK * (TAPS - PE_TAPS) - 1))
            for k in range(NK):
                sp.dma_start(wx_raw[:, k, :], wout_v[k]).then_inc(wsq_in[k], 16)
            sp.wait_ge(sT_lo_done.sem, sT_lo_done.ready(NT - 1))
            for b in range(2):
                ffn_loads(1)[0](b, b, False)
            sp.wait_ge(pr_ps.sem, pr_ps.ready(2 * NT - 1))
            load_ffn(1)
            load_ln(3)
            for t in range(NT):
                sp.wait_ge(ln_done.sem, ln_done.ready(3 * NT + t))
                sp.dma_start(out_v[t], resid[:, t, :]).then_inc(stored, 16)
            sp.wait_ge(stored, 16 * NT)

        @block.tensor
        def _(pe):
            mm = nc.tensor.matmul

            def product(dst, terms, last_inc=None):
                n = len(terms)
                for m, ((a_hi, a_lo), (b_hi, b_lo)) in enumerate(terms):
                    mm(dst, a_hi, b_hi, start=m == 0, stop=False)
                    mm(dst, a_hi, b_lo, start=False, stop=False)
                    ins = mm(dst, a_lo, b_hi, start=False, stop=m == n - 1)
                return ins

            def transpose_tile(src, use, t):
                for k in range(NK):
                    ins = nc.tensor.transpose(turned(use, t)[:, tok[k]], src(k), ident[:])
                ins.then_inc(tp_ps.sem, 1)

            pe.wait_ge(started, 1)
            pe.wait_ge(made_consts, 1)
            pe.wait_ge(cols_in, 7 * 16)
            nc.tensor.transpose(ps[2][:, 0:N_COLS], vec_rows[0:N_COLS, :], ident[0:N_COLS, 0:N_COLS])
            for k in range(NK):
                ins = nc.tensor.transpose(ps[2][:, 64 + 32 * k:64 + 32 * k + TAPS], dw_rows[0:TAPS, tok[k]],
                                          ident[0:TAPS, 0:TAPS])
            ins.then_inc(cols_ps, 1)
            for t in range(NT):
                pe.wait_ge(x_in[t % 4], 16 * (t // 4 + 1))
                pe.wait_ge(tp_lo.sem, tp_lo.free(t, 2))
                transpose_tile(lambda k: x_stage[:, t % 4, tok[k]], 0, t)

            def transpose_c(t):
                pe.wait_ge(c_tok_done.sem, c_tok_done.ready(t))
                pe.wait_ge(ct_lo.sem, ct_lo.free(t, 2))
                dst = ps[t % 2]
                for j in range(5):
                    nc.tensor.transpose(dst[:, tok[j]], c_tok[:, tok[j]], ident[:])
                nc.tensor.transpose(dst[0:2 * ROPE, tok[5]], c_tok[:, 5 * P:5 * P + 2 * ROPE], ident[:]
                                    ).then_inc(ct_ps.sem, 1)

            pe.wait_ge(cols_done, 1)
            pe.wait_ge(tp_lo.sem, tp_lo.ready(NT - 1))
            for t in range(NT):
                pe.wait_ge(c_tok_done.sem, c_tok_done.free(t, 2))
                dst = ps[2 + t % 2]
                parts = ((dst[:, 0:Q_RANK], slice(0, Q_RANK)), (dst[:, HALF:HALF + DOWN - Q_RANK], slice(Q_RANK, DOWN)))
                for k in range(NK):
                    if t == 0:
                        pe.wait_ge(wd_lo_done.sem, wd_lo_done.ready(k))
                    for d, s in parts:
                        mm(d, actT_hi[:, k, tok[t]], wd_hi[:, k, s], start=k == 0, stop=False)
                        mm(d, actT_hi[:, k, tok[t]], wd_lo[:, k, s], start=False, stop=False)
                        ins = mm(d, actT_lo[:, k, tok[t]], wd_hi[:, k, s], start=False, stop=k == NK - 1)
                ins.then_inc(c_ps.sem, 1)
                if t:
                    transpose_c(t - 1)
            transpose_c(NT - 1)

            cq = [(cT_hi[:, k, :], cT_lo[:, k, :]) for k in range(NQ)]
            ckv = [(cT_hi[:, NQ + k, :], cT_lo[:, NQ + k, :]) for k in range(NKV)]

            def project(dst, w_hi, w_lo, s, c):
                for h in halves:
                    ins = product(dst[:, h], [((w_hi[:, k, s], w_lo[:, k, s]), (c_hi[:, h], c_lo[:, h]))
                                              for k, (c_hi, c_lo) in enumerate(c)])
                return ins

            def rotary_queries(i):
                pe.wait_ge(wa_lo_done.sem, wa_lo_done.ready(i))
                project(ps[0], wq_hi, wq_lo, slice(P, 2 * P), cq).then_inc(qr_ps.sem, 1)

            def keys(i):
                project(ps[1], wkv_hi, wkv_lo, slice(0, P), ckv).then_inc(k_ps.sem, 1)

            def plain_queries(i):
                pe.wait_ge(qr_parts.sem, qr_parts.ready(i))
                project(ps[0], wq_hi, wq_lo, slice(0, P), cq).then_inc(qn_ps.sem, 1)

            def values_transposed(i):
                pe.wait_ge(k_lo_done.sem, k_lo_done.ready(i))
                project(ps[1], wkv_hi, wkv_lo, slice(P, 2 * P), ckv).then_inc(vt_ps.sem, 1)

            def values(i):
                pe.wait_ge(pt_lo_done.sem, pt_lo_done.free(i * NQT * 2, 1))
                for t in range(NT):
                    ins = nc.tensor.transpose(ps[2][:, tok[t]], vT[:, tok[t]], ident[:])
                ins.then_inc(v_ps.sem, 1)

            def scores(i, n):
                j, t = divmod(n, NT)
                if n > 1:
                    pe.wait_ge(p_done.sem, p_done.ready(i * NQT + n - 2))
                q = (q_hi[0:QK, j, tok[t]], q_lo[0:QK, j, tok[t]])
                for h in halves:
                    ins = product(ps[n % 2][:, h], [(q, (k_hi[0:QK, j, h], k_lo[0:QK, j, h]))])
                ins.then_inc(s_ps.sem, 1)

            def transposed(i, n):
                pe.wait_ge(p_normed.sem, p_normed.ready(i * NQT + n))
                for a in range(2):
                    pe.wait_ge(pt_lo_done.sem, pt_lo_done.free((i * NQT + n) * 2 + a, 2))
                    for kk in range(4):
                        ins = nc.tensor.transpose(ps[2][:, tok[4 * a + kk]], p_f[:, n % 3, tok[4 * a + kk]], ident[:])
                    ins.then_inc(pt_ps.sem, 1)

            def times_v(i, c, part):
                item = i * NC + c
                if part == 0:
                    pe.wait_ge(pt_lo_done.sem, pt_lo_done.ready((i * NQT + 4 * c + 3) * 2 + 1))
                    pe.wait_ge(o_done.sem, o_done.free(item, 2))
                o = ps[3][:, halves[c % 2]]
                for k in range(2 * part, 2 * part + 2):
                    v = v2[:, k, c // 2, :]
                    mm(o, v, pt_hi[:, c % 2, k, :], start=k == 0, stop=False)
                    ins = mm(o, v, pt_lo[:, c % 2, k, :], start=False, stop=k == NK - 1)
                if part == 3:
                    ins.then_inc(o_ps.sem, 1)

            def attend(i, more):
                pe.wait_ge(k_lo_done.sem, k_lo_done.ready(i))
                pe.wait_ge(qn_lo_done.sem, qn_lo_done.ready(i))
                pe.wait_ge(qr_lo_done.sem, qr_lo_done.ready(i))
                scores(i, 0)
                pe.wait_ge(vt_done.sem, vt_done.ready(i))
                scores(i, 1)
                values(i)
                for n in range(1, NQT):
                    if n + 1 < NQT:
                        scores(i, n + 1)
                    if n >= 7:
                        times_v(i, *divmod(n - 7, 4))
                    if n == 2:
                        pe.wait_ge(v_lo_done.sem, v_lo_done.ready(i))
                    if n >= 2:
                        transposed(i, n - 2)
                if more:
                    pe.wait_ge(p_done.sem, p_done.ready(i * NQT + NQT - 2))
                    rotary_queries(i + 1)
                times_v(i, 2, 1)
                transposed(i, NQT - 2)
                if more:
                    pe.wait_ge(p_done.sem, p_done.ready(i * NQT + NQT - 1))
                    keys(i + 1)
                times_v(i, 2, 2)
                transposed(i, NQT - 1)
                times_v(i, 2, 3)
                if more:
                    plain_queries(i + 1)
                    values_transposed(i + 1)
                for part in range(4):
                    times_v(i, 3, part)

            pe.wait_ge(ct_lo.sem, ct_lo.ready(NT - 1))
            rotary_queries(0)
            keys(0)
            plain_queries(0)
            values_transposed(0)
            with pe.Fori(0, PAIRS - 1) as i:
                attend(i, True)
            attend(PAIRS - 1, False)

            def transpose_resid(use, t):
                pe.wait_ge(ln_done.sem, ln_done.ready((use - 1) * NT + t))
                pe.wait_ge(tp_lo.sem, tp_lo.free(use * NT + t, 2))
                transpose_tile(lambda k: resid[:, t, tok[k]], use, t)

            def square(use, ln, w_hi, w_lo):
                for t in range(NT):
                    pe.wait_ge(pr_add.sem, pr_add.free(use * NT + t, 2))
                    dst = ps[2 + t % 2]
                    for k in range(NK):
                        if t == 0:
                            lo_done = wsq_odd_lo if k % 2 else wsq_even_lo
                            pe.wait_ge(lo_done.sem, lo_done.ready(use * NK // 2 + k // 2))
                            if use == 0:
                                pe.wait_ge(oT_lo_done.sem, oT_lo_done.ready(k))
                        a_hi, a_lo = actT_hi[:, k, tok[t]], actT_lo[:, k, tok[t]]
                        for h in halves:
                            mm(dst[:, h], a_hi, w_hi[:, k, h], start=k == 0, stop=False)
                            mm(dst[:, h], a_hi, w_lo[:, k, h], start=False, stop=False)
                            ins = mm(dst[:, h], a_lo, w_hi[:, k, h], start=False, stop=k == NK - 1)
                    ins.then_inc(pr_ps.sem, 1)
                    if t:
                        transpose_resid(ln, t - 1)

            def last_tile(ln):
                transpose_resid(ln, NT - 1)
                pe.wait_ge(tp_lo.sem, tp_lo.ready((ln + 1) * NT - 1))

            square(0, 1, wo_hi, wo_lo)

            def up(l, f, slot, between=None):
                item = f + l * NF
                w_hi, w_lo, _ = up_w[l]
                pe.wait_ge(w13_lo_done.sem, w13_lo_done.ready(item))
                for n, h in enumerate(halves):
                    if n and between:
                        between()
                    pe.wait_ge(hid_f_done.sem, hid_f_done.free(item * 2 + n, 2))
                    for g in range(2):
                        ins = product(ps[g][:, h], [((w_hi[:, slot, g, k, :], w_lo[:, slot, g, k, :]),
                                                     (actT_hi[:, k, h], actT_lo[:, k, h])) for k in range(NK)])
                    ins.then_inc(up_ps.sem, 1)

            def down(l, f, slot, behind=None):
                item = f + l * NF
                hid_hi, hid_lo, w2_hi, w2_lo = ffn_m[l][0:4]
                pe.wait_ge(w2_lo_done.sem, w2_lo_done.ready(item))
                pe.wait_ge(hid_lo_done.sem, hid_lo_done.ready(item * 2 + 1))
                for m in range(2 * NT):
                    t, h = divmod(m, 2)
                    pe.wait_ge(acc_done.sem, acc_done.free(item * 16 + m, 4))
                    product(bank(m), [((hid_hi[:, slot, tok[t]], hid_lo[:, slot, tok[t]]),
                                       (w2_hi[:, slot, halves[h]], w2_lo[:, slot, halves[h]]))]
                            ).then_inc(down_ps.sem, 1)
                    if h and behind:
                        behind(t)

            def ffn(l, between, behind=None):
                up(l, 0, 0, between)
                with pe.Fori(0, NF // 2 - 1) as i:
                    up(l, i * 2 + 1, 1)
                    down(l, i * 2, 0)
                    up(l, i * 2 + 2, 0)
                    down(l, i * 2 + 1, 1)
                up(l, NF - 1, 1)
                down(l, NF - 2, 0)
                down(l, NF - 1, 1, behind)

            def first_tiles(t):
                if 2 <= t < 6:
                    transpose_resid(2, t - 2)

            def last_tiles():
                pe.wait_ge(acc_done.sem, acc_done.ready(NF * 16 - 1))
                for t in range(4, NT):
                    transpose_resid(2, t)
                pe.wait_ge(tp_lo.sem, tp_lo.ready(3 * NT - 1))

            pe.wait_ge(tp_lo.sem, tp_lo.ready(2 * NT - 2))
            ffn(0, lambda: last_tile(1), first_tiles)

            def conv_in(c, slot, between=None):
                pe.wait_ge(win_lo_done.sem, win_lo_done.ready(c))
                for n, h in enumerate(halves):
                    if n and between:
                        between()
                    pe.wait_ge(glu_done.sem, glu_done.free(c * 2 + n, 2))
                    for g in range(2):
                        ins = product(ps[g][:, h],
                                      [((win_hi[:, slot, g, k, :], win_lo[:, slot, g, k, :]),
                                        (actT_hi[:, k, h], actT_lo[:, k, h])) for k in range(NK)])
                    ins.then_inc(in_ps.sem, 1)

            def conv_taps(c, slot):
                pe.wait_ge(glu_lo_done.sem, glu_lo_done.ready(c))
                pe.wait_ge(diag_done.sem, diag_done.ready(c))
                pe.wait_ge(conv_out.sem, conv_out.free(c, 2))
                for n, h in enumerate(halves):
                    ins = product(ps[2 + slot][:, h],
                                  [((diag_hi[:, j, :], diag_lo[:, j, :]),
                                    (glu_hi[:, slot, HALF * n + j:HALF * (n + 1) + j],
                                     glu_lo[:, slot, HALF * n + j:HALF * (n + 1) + j])) for j in range(PE_TAPS)])
                ins.then_inc(conv_ps.sem, 1)

            pe.wait_ge(tp_lo.sem, tp_lo.ready(2 * NT + 3))
            conv_in(0, 0, last_tiles)
            conv_in(1, 1)
            with pe.Fori(0, NK // 2 - 1) as i:
                for b in range(2):
                    conv_taps(i * 2 + b, b)
                    conv_in(i * 2 + b + 2, b)
            conv_taps(NK - 2, 0)
            conv_taps(NK - 1, 1)

            pe.wait_ge(tap_done.sem, tap_done.ready(2 * NK * (TAPS - PE_TAPS) - 1))

            def to_tokens(t):
                pe.wait_ge(cl_norm.sem, cl_norm.free(t, 2))
                for k in range(NK):
                    ins = nc.tensor.transpose(ps[t % 2][:, tok[k]], convT[:, k, tok[t]], ident[:])
                ins.then_inc(cl_ps.sem, 1)

            def to_channels(t):
                pe.wait_ge(cl_norm.sem, cl_norm.ready(t))
                pe.wait_ge(silu_done.sem, silu_done.free(t, 2))
                for k in range(NK):
                    ins = nc.tensor.transpose(ps[2 + t % 2][:, tok[k]], convT[:, k, tok[t]], ident[:])
                ins.then_inc(cb_ps.sem, 1)

            for t in range(NT):
                to_tokens(t)
                if t:
                    to_channels(t - 1)
            to_channels(NT - 1)
            pe.wait_ge(sT_lo_done.sem, sT_lo_done.ready(NT - 1))
            square(1, 3, wx_hi, wx_lo)
            pe.wait_ge(tp_lo.sem, tp_lo.ready(4 * NT - 2))
            ffn(1, lambda: last_tile(3))

        @block.scalar
        def _(act):
            copy, activate = nc.scalar.copy, nc.scalar.activation

            def split_tile(use, t):
                act.wait_ge(tp_ps.sem, tp_ps.ready(use * NT + t))
                copy(actT_hi[:, :, tok[t]], turned(use, t)[:].rearrange("p (k n) -> p k n", k=NK)
                     ).then_inc(tp_hi.sem, 1)

            def split_wd(k):
                act.wait_ge(wd_in[k % 2], 32 * (k // 2 + 1))
                copy(wd_hi[:, k, :], wd_raw[:, k % 2, :]).then_inc(wd_hi_done.sem, 1)

            act.wait_ge(started, 1)
            act.wait_ge(ang_done, 1)
            activate(absr[:], ang[:], ACT.Abs).then_inc(act_steps, 1)
            activate(sinv[:], ang[:], ACT.Sin, scale=consts[:, 1:2]).then_inc(act_steps, 1)
            act.wait_ge(act_steps, 1)
            activate(cosv[:], absr[:], ACT.Sin, bias=consts[:, 2:3], scale=-1.0).then_inc(act_steps, 1)
            act.wait_ge(act_steps, 3)
            for q in range(4):
                rows, cs = slice(32 * q, 32 * q + 32), slice(QUARTER * q, QUARTER * (q + 1))
                for j in range(2):
                    copy(tab[32 * j:32 * j + 32, cs], cosv[rows, :])
                    ins = copy(tab[64 + 32 * j:96 + 32 * j, cs], sinv[rows, :])
            ins.then_inc(tab_done, 1)
            act.wait_ge(cols_ps, 1)
            copy(cols[:, 0:N_COLS], ps[2][:, 0:N_COLS])
            taps_ps = ps[2][:, 64:64 + 32 * NK].rearrange("p (k j) -> p k j", k=NK)
            copy(conv_cols[:, :, CC_DW:CC_DW + TAPS], taps_ps[:, :, 0:TAPS])
            copy(dw_hi[:], taps_ps[:, :, 0:PE_TAPS])
            for k in range(NK):
                for dst, src in ((CC_BIAS, C_DWB), (CC_VALUE, C_BIN), (CC_GATE, C_BIN + NK)):
                    ins = copy(conv_cols[:, k, dst:dst + 1], ps[2][:, src + k:src + k + 1])
            ins.then_inc(cols_done, 1)
            for t in range(4):
                split_tile(0, t)
            split_wd(0)
            split_wd(1)
            for t in range(4, NT):
                split_tile(0, t)
                split_wd(t - 2)
            split_wd(6)
            split_wd(7)

            def squares(t):
                act.wait_ge(c_ps.sem, c_ps.ready(t))
                activate(x_stage[:, t % 2, 0:Q_RANK], ps[2 + t % 2][:, 0:Q_RANK], ACT.Square, accum_out=stats[:, t, 0:1])
                activate(x_stage[:, t % 2, HALF:HALF + KV_RANK], ps[2 + t % 2][:, HALF:HALF + KV_RANK], ACT.Square,
                         accum_out=stats[:, t, 1:2]).then_inc(c_sq.sem, 1)

            def split_c(t):
                act.wait_ge(ct_ps.sem, ct_ps.ready(t))
                for j in range(5):
                    ins = activate(cT_hi[:, j, tok[t]], ps[t % 2][:, tok[j]], ACT.Copy,
                                   scale=cols[:, C_GQ + j:C_GQ + j + 1])
                ins.then_inc(ct_hi.sem, 1)

            act.wait_ge(cols_done, 1)
            for t in range(NT):
                squares(t)
                if t:
                    split_c(t - 1)
            split_c(NT - 1)

            def split_pair(i, wait_used=True):
                if wait_used:
                    act.wait_ge(vt_ps.sem, vt_ps.ready(i - 1))
                act.wait_ge(wq_in, (i + 1) * 16)
                for dst, src in pair_views(wq_hi, wq_raw):
                    copy(dst, src)
                act.wait_ge(wkv_in, (i + 1) * 16)
                for dst, src in kv_views(wkv_hi, wkv_raw):
                    ins = copy(dst, src)
                ins.then_inc(wa_hi_done.sem, 1)

            def head_part(dst, src, j):
                return copy(dst[0:NOPE, j, :], src[NOPE * j:NOPE * (j + 1), :])

            def split_keys(i):
                act.wait_ge(k_ps.sem, k_ps.ready(i))
                head_part(k_hi, ps[1], 0)
                head_part(k_hi, ps[1], 1).then_inc(k_hi_done.sem, 1)

            def split_rotary(i):
                act.wait_ge(qr_sum.sem, qr_sum.ready(i))
                copy(q_hi[NOPE:QK, :, :], rope_m[NOPE:QK, :, :]).then_inc(qr_hi_done.sem, 1)

            def split_plain(i):
                act.wait_ge(qn_ps.sem, qn_ps.ready(i))
                head_part(q_hi, ps[0], 0)
                head_part(q_hi, ps[0], 1).then_inc(qn_hi_done.sem, 1)

            def values_transposed(i):
                act.wait_ge(vt_ps.sem, vt_ps.ready(i))
                copy(vT[:], ps[1][:]).then_inc(vt_done.sem, 1)

            def values(i):
                act.wait_ge(v_ps.sem, v_ps.ready(i))
                copy(v2[:, :, :, 0:VDIM], ps[2][:].rearrange("p (t j d) -> p t j d", t=NT, j=2)
                     ).then_inc(v_hi_done.sem, 1)

            def exponentials(i, n):
                item = i * NQT + n
                act.wait_ge(pt_ps.sem, pt_ps.free(item * 2, 1) if n == 0 else pt_ps.ready((item - 3) * 2 + 1) if n > 2
                            else pt_ps.free(item * 2 + 1, 4))
                act.wait_ge(s_max.sem, s_max.ready(item))
                activate(p_f[:, n % 3, :], ps[n % 2][:], ACT.Exp, bias=negmax[:, n:n + 1], scale=-1.0,
                         accum_out=sums[:, n:n + 1]).then_inc(p_done.sem, 1)

            def split_probs(i, n):
                c = n // 4
                act.wait_ge(o_ps.sem, o_ps.free(i * NC + c, 2))
                for a in range(2):
                    act.wait_ge(pt_ps.sem, pt_ps.ready((i * NQT + n) * 2 + a))
                    copy(pt_hi[:, c % 2, 4 * a:4 * a + 4, tok[n % 4]],
                         ps[2][:, halves[a]].rearrange("p (k n) -> p k n", k=4)).then_inc(pt_hi_done.sem, 1)

            def first_half(i, c):
                act.wait_ge(o_stored[c % 2].sem, (i * 2 + c // 2) * 16 + CREDIT)
                act.wait_ge(o_ps.sem, o_ps.ready(i * NC + c))
                copy(o_sum[0:VDIM, c % 2, :], ps[3][0:VDIM, halves[c % 2]]).then_inc(o_first_done.sem, 1)

            def attend(i, more):
                for n in range(NQT):
                    if n >= 3:
                        split_probs(i, n - 3)
                    exponentials(i, n)
                    if n == 0:
                        values(i)
                    if n >= 11 and (n - 11) % 4 == 0:
                        first_half(i, (n - 11) // 4)
                    if more and n == 4:
                        split_pair(i + 1)
                split_probs(i, NQT - 3)
                split_probs(i, NQT - 2)
                if more:
                    split_keys(i + 1)
                    split_rotary(i + 1)
                split_probs(i, NQT - 1)
                first_half(i, 2)
                if more:
                    split_plain(i + 1)
                    values_transposed(i + 1)
                first_half(i, 3)

            split_pair(0, wait_used=False)
            act.wait_ge(ct_ps.sem, ct_ps.ready(NT - 1))
            act.wait_ge(krope_done, 1)
            for j in range(2):
                ins = copy(k_hi[NOPE:QK, j, :], rope_m[NOPE:QK, 0, :])
            ins.then_inc(krope_hi, 1)
            split_rotary(0)
            split_keys(0)
            split_plain(0)
            values_transposed(0)
            with act.Fori(0, PAIRS - 1) as i:
                attend(i, True)
            attend(PAIRS - 1, False)

            def square_hi(use, w_hi, raw, k):
                act.wait_ge(wsq_in[k], 16 * (use + 1))
                copy(w_hi[:, k, :], raw[:, k, :]).then_inc(wsq_hi_done.sem, 1)

            def unit_tile(u, t):
                act.wait_ge(ln_rstd.sem, ln_rstd.ready(u * NT + t))
                act.wait_ge(ln_centred.sem, ln_centred.ready(u * NT + t))
                activate(resid[:, t, :], resid[:, t, :], ACT.Copy, scale=rstd[:, t, 0:1]).then_inc(ln_unit.sem, 1)

            def rescale(use, t):
                act.wait_ge(tp_ps.sem, tp_ps.ready(use * NT + t))
                nc.scalar.mul(resid[:, t, :], resid[:, t, :], ALPHA).then_inc(ln_scaled.sem, 1)

            act.wait_ge(o_done.sem, o_done.ready(NC * PAIRS - 1))
            for k in range(NK):
                act.wait_ge(oT_in[k], 16)
                copy(actT_hi[:, k, :], oT_f[:, k, :]).then_inc(oT_hi_done.sem, 1)
                square_hi(0, wo_hi, wo_raw, k)

            def split_13(l, f, slot):
                w13_hi, _, w13_raw = up_w[l]
                item = f + l * NF
                act.wait_ge(w13_in[slot], (item - slot) * 16 + 32)
                copy(w13_hi[:, slot], w13_raw[:, slot]).then_inc(w13_hi_done.sem, 1)

            def square(use, ln):
                for t in range(NT):
                    if t in (3, 5):
                        split_13(use, t // 4, t // 4)
                    unit_tile(ln - 1, t)
                    if t:
                        split_tile(ln, t - 1)
                        rescale(ln, t - 1)

            square(0, 1)

            def ffn(l):
                hid_hi, _, w2_hi, _, w2_raw, gate, hid_f = ffn_m[l]

                def split_2(f, slot):
                    item = f + l * NF
                    act.wait_ge(w2_in[slot], (item - slot) * 8 + 16)
                    copy(w2_hi[:, slot, :], w2_raw[:, slot, :]).then_inc(w2_hi_done.sem, 1)

                def hidden(f, slot, used=True):
                    item = f + l * NF
                    for n, h in enumerate(halves):
                        act.wait_ge(up_ps.sem, up_ps.ready(item * 2 + n))
                        act.wait_ge(hid_f_done.sem, hid_f_done.free(item * 2 + n, 2))
                        activate(gate[:, h], ps[0][:, h], ACT.Silu).then_inc(gate_done.sem, 1)
                    if used:
                        act.wait_ge(down_ps.sem, down_ps.ready((item - 2) * 16 + 15))
                    for n, h in enumerate(halves):
                        act.wait_ge(hid_f_done.sem, hid_f_done.ready(item * 2 + n))
                        copy(hid_hi[:, slot, h], hid_f[:, h]).then_inc(hid_hi_done.sem, 1)

                split_tile(2 * l + 1, NT - 1)
                rescale(2 * l + 1, NT - 1)
                split_2(0, 0)
                hidden(0, 0, False)
                split_13(l, 2, 0)
                split_2(1, 1)
                hidden(1, 1, False)
                split_13(l, 3, 1)
                split_2(2, 0)
                with act.Fori(1, NF // 2 - 1) as i:
                    for b in range(2):
                        hidden(i * 2 + b, b)
                        split_13(l, i * 2 + b + 2, b)
                        split_2(i * 2 + b + 1, 1 - b)
                hidden(NF - 2, 0)
                split_2(NF - 1, 1)
                hidden(NF - 1, 1)

            ffn(0)

            def split_win(c, slot, loads):
                act.wait_ge(win_in[slot], loads)
                copy(win_hi[:, slot], win_raw[:, slot]).then_inc(win_hi_done.sem, 1)

            split_win(0, 0, 32)
            for t in range(NT):
                unit_tile(1, t)
                if 2 <= t < 6:
                    split_tile(2, t - 2)
                    rescale(2, t - 2)
            split_win(1, 1, 32)
            for t in range(4, NT):
                split_tile(2, t)
                rescale(2, t)

            def sigmoids(c, slot):
                act.wait_ge(now_done.sem, now_done.ready(c))
                for n, h in enumerate(halves):
                    act.wait_ge(glu_done.sem, glu_done.free(c * 2 + n, 2))
                    act.wait_ge(in_ps.sem, in_ps.ready(c * 2 + n))
                    activate(sig[:, h], ps[1][:, h], ACT.Sigmoid, bias=conv_now[:, slot, CC_GATE:CC_GATE + 1]
                             ).then_inc(sig_done.sem, 1)

            def split_glu(c, slot):
                act.wait_ge(glu_done.sem, glu_done.ready(c * 2 + 1))
                act.wait_ge(conv_ps.sem, conv_ps.free(c, 2))
                copy(glu_hi[:, slot, :], glu[:, slot, :]).then_inc(glu_hi_done.sem, 1)

            def conv_start(c, slot):
                act.wait_ge(conv_ps.sem, conv_ps.ready(c))
                act.wait_ge(tap_done.sem, tap_done.free(c * (TAPS - PE_TAPS) * 2, 1))
                activate(conv_acc[:], ps[2 + slot][:], ACT.Identity, bias=conv_now[:, slot, CC_BIAS:CC_BIAS + 1]
                         ).then_inc(conv_out.sem, 1)

            act.wait_ge(ln_bout.sem, ln_bout.ready(NT - 1))
            for b in range(2):
                sigmoids(b, b)
                split_glu(b, b)
            with act.Fori(0, NK // 2 - 1) as i:
                for b in range(2):
                    split_win(i * 2 + b + 2, b, i * 32 + 64)
                    conv_start(i * 2 + b, b)
                    sigmoids(i * 2 + b + 2, b)
                    split_glu(i * 2 + b + 2, b)
            conv_start(NK - 2, 0)
            conv_start(NK - 1, 1)

            act.wait_ge(tap_done.sem, tap_done.ready(2 * NK * (TAPS - PE_TAPS) - 1))
            for t in range(NT):
                square_hi(1, wx_hi, wx_raw, t)
                act.wait_ge(cb_ps.sem, cb_ps.ready(t))
                for k in range(NK):
                    ins = activate(convT[:, k, tok[t]], ps[2 + t % 2][:, tok[k]], ACT.Silu,
                                   bias=cols[:, C_LNB + k:C_LNB + k + 1], scale=cols[:, C_LNG + k:C_LNG + k + 1])
                ins.then_inc(silu_done.sem, 1)
                act.wait_ge(silu_done.sem, silu_done.ready(t))
                copy(actT_hi[:, :, tok[t]], convT[:, :, tok[t]]).then_inc(sT_hi_done.sem, 1)
            square(1, 3)
            ffn(1)
            for t in range(NT):
                unit_tile(3, t)

        @block.vector
        def _(v):
            V = nc.vector
            own = Chain(dve_steps, v)
            tt, sub = V.tensor_tensor, ALU.subtract

            v.wait_ge(started, 1)
            v.wait_ge(small_in, 5 * 16)
            own.link(V.tensor_scalar(ang[:], pos_i[:], consts[:, 0:1], None, ALU.mult))
            for size, count in ((2.0 ** 20, 4), (2.0 ** 10, 4), (1.0, 4)):
                own.link(V.tensor_scalar(turns[:], ang[:], 1.0 / (2 * math.pi * size), MAGIC, ALU.mult, ALU.add))
                own.link(V.tensor_scalar(turns[:], turns[:], MAGIC, None, ALU.subtract))
                for piece in turn_pieces(size, count):
                    own.link(V.scalar_tensor_tensor(out=ang[:], in0=turns[:], scalar=-piece, in1=ang[:],
                                                    op0=ALU.mult, op1=ALU.add))
            V.tensor_scalar(ang[:], ang[:], 3.1415925, -3.1415925, ALU.min, ALU.max).then_inc(ang_done, 1)

            def split_tile(use, t):
                v.wait_ge(tp_hi.sem, tp_hi.ready(use * NT + t))
                tt(actT_lo[:, :, tok[t]], turned(use, t)[:].rearrange("p (k n) -> p k n", k=NK),
                   actT_hi[:, :, tok[t]], sub).then_inc(tp_lo.sem, 1)

            for t in range(NT):
                split_tile(0, t)

            def norm_c(t):
                src = ps[2 + t % 2]
                v.wait_ge(c_sq.sem, c_sq.ready(t))
                V.tensor_scalar(mean_var[:, t, 0:1], stats[:, t, 0:1], 1.0 / Q_RANK, RMS_EPS, ALU.mult, ALU.add)
                V.tensor_scalar(mean_var[:, t, 1:2], stats[:, t, 1:2], 1.0 / KV_RANK, RMS_EPS, ALU.mult, ALU.add
                                ).then_inc(c_ms.sem, 1)
                v.wait_ge(c_rstd.sem, c_rstd.ready(t))
                v.wait_ge(ct_ps.sem, ct_ps.free(t, 1))
                V.tensor_scalar(c_tok[:, 0:Q_RANK], src[:, 0:Q_RANK], rstd[:, t, 0:1], None, ALU.mult)
                V.tensor_scalar(c_tok[:, Q_RANK:Q_RANK + KV_RANK], src[:, HALF:HALF + KV_RANK], rstd[:, t, 1:2],
                                None, ALU.mult)
                r0, h = HALF + KV_RANK, ROPE // 2
                V.tensor_copy(c_tok[:, 5 * P:5 * P + ROPE], src[:, r0:r0 + ROPE])
                V.tensor_copy(c_tok[:, 5 * P + ROPE:5 * P + ROPE + h], src[:, r0 + h:r0 + ROPE])
                V.tensor_copy(c_tok[:, 5 * P + ROPE + h:5 * P + 2 * ROPE], src[:, r0:r0 + h]
                              ).then_inc(c_tok_done.sem, 1)

            def split_c(t):
                v.wait_ge(ct_hi.sem, ct_hi.ready(t))
                for j in range(5):
                    V.scalar_tensor_tensor(out=cT_lo[:, j, tok[t]], in0=ps[t % 2][:, tok[j]],
                                           scalar=cols[:, C_GQ + j:C_GQ + j + 1], in1=cT_hi[:, j, tok[t]],
                                           op0=ALU.mult, op1=sub)
                V.tensor_copy(kr_f[0:ROPE, tok[t]], ps[t % 2][0:ROPE, tok[5]])
                V.tensor_copy(kr_f[2 * ROPE:3 * ROPE, tok[t]], ps[t % 2][ROPE:2 * ROPE, tok[5]]).then_inc(ct_lo.sem, 1)

            v.wait_ge(cols_done, 1)
            for t in range(NT):
                norm_c(t)
                split_c(t)

            v.wait_ge(tab_done, 1)
            v.wait_ge(ct_lo.sem, ct_lo.ready(NT - 1))
            v.wait_ge(ct_ps.sem, ct_ps.ready(NT - 1))
            tt(rope_m[0:ROPE, 0, :], kr_f[0:ROPE, :], tab[0:ROPE, :], ALU.mult)
            own.link(tt(rope_m[0:ROPE, 1, :], kr_f[2 * ROPE:3 * ROPE, :], tab[2 * ROPE:3 * ROPE, :], ALU.mult))
            tt(rope_m[NOPE:QK, 0, :], rope_m[0:ROPE, 0, :], rope_m[0:ROPE, 1, :], ALU.add).then_inc(krope_done, 1)
            v.wait_ge(krope_hi, 1)
            for j in range(2):
                ins = tt(k_lo[NOPE:QK, j, :], rope_m[NOPE:QK, 0, :], k_hi[NOPE:QK, j, :], sub)
            ins.then_inc(krope_lo, 1)
            v.wait_ge(krope_lo, 1)

            def head_part(lo, hi, src, j):
                return tt(lo[0:NOPE, j, :], src[NOPE * j:NOPE * (j + 1), :], hi[0:NOPE, j, :], sub)

            def split_keys(i):
                v.wait_ge(k_hi_done.sem, k_hi_done.ready(i))
                head_part(k_lo, k_hi, ps[1], 0)
                head_part(k_lo, k_hi, ps[1], 1).then_inc(k_lo_done.sem, 1)

            def rotary_parts(i):
                v.wait_ge(qr_ps.sem, qr_ps.ready(i))
                tt(rope_m[0:2 * ROPE, 0, :], ps[0][0:2 * ROPE, :], tab[0:2 * ROPE, :], ALU.mult)
                tt(rope_m[0:2 * ROPE, 1, :], ps[0][2 * ROPE:P, :], tab[2 * ROPE:P, :], ALU.mult
                   ).then_inc(qr_parts.sem, 1)

            def rotary_sums(i):
                v.wait_ge(qr_parts.sem, qr_parts.ready(i))
                for j in range(2):
                    rows = slice(ROPE * j, ROPE * (j + 1))
                    ins = tt(rope_m[NOPE:QK, j, :], rope_m[rows, 0, :], rope_m[rows, 1, :], ALU.add)
                ins.then_inc(qr_sum.sem, 1)

            def split_rotary(i):
                v.wait_ge(qr_sum.sem, qr_sum.ready(i))
                v.wait_ge(qr_hi_done.sem, qr_hi_done.ready(i))
                tt(q_lo[NOPE:QK, :, :], rope_m[NOPE:QK, :, :], q_hi[NOPE:QK, :, :], sub).then_inc(qr_lo_done.sem, 1)

            def split_plain(i):
                v.wait_ge(qn_hi_done.sem, qn_hi_done.ready(i))
                head_part(q_lo, q_hi, ps[0], 0)
                head_part(q_lo, q_hi, ps[0], 1).then_inc(qn_lo_done.sem, 1)

            def values(i):
                v.wait_ge(v_hi_done.sem, v_hi_done.ready(i))
                tt(v2[:, :, :, VDIM:2 * VDIM], ps[2][:].rearrange("p (t j d) -> p t j d", t=NT, j=2),
                   v2[:, :, :, 0:VDIM], sub).then_inc(v_lo_done.sem, 1)

            def row_max(i, n):
                v.wait_ge(s_ps.sem, s_ps.ready(i * NQT + n))
                V.tensor_scalar(ps[n % 2][:], ps[n % 2][:], -SCALE, None, ALU.mult, ALU.min,
                                accum_out=negmax[:, n:n + 1]).then_inc(s_max.sem, 1)

            def split_probs(i, n):
                c = n // 4
                for a in range(2):
                    v.wait_ge(pt_hi_done.sem, pt_hi_done.ready((i * NQT + n) * 2 + a))
                    tt(pt_lo[:, c % 2, 4 * a:4 * a + 4, tok[n % 4]],
                       ps[2][:, halves[a]].rearrange("p (k n) -> p k n", k=4),
                       pt_hi[:, c % 2, 4 * a:4 * a + 4, tok[n % 4]], sub).then_inc(pt_lo_done.sem, 1)

            def inverse_sum(i, n):
                v.wait_ge(p_done.sem, p_done.ready(i * NQT + n))
                V.reciprocal(rsums[:, n:n + 1], sums[:, n:n + 1]).then_inc(rsum_done.sem, 1)

            def outputs(i, c):
                v.wait_ge(o_first_done.sem, o_first_done.ready(i * NC + c))
                o = o_sum[0:VDIM, c % 2, :]
                tt(o, ps[3][VDIM:P, halves[c % 2]], o, ALU.add).then_inc(o_done.sem, 1)

            def attend(i, more):
                for n in range(NQT):
                    if n:
                        inverse_sum(i, n - 1)
                    row_max(i, n)
                    if n == 1:
                        values(i)
                    if n >= 3:
                        split_probs(i, n - 3)
                    if n >= 11 and (n - 11) % 4 == 0:
                        outputs(i, (n - 11) // 4)
                inverse_sum(i, NQT - 1)
                split_probs(i, NQT - 3)
                if more:
                    rotary_parts(i + 1)
                split_probs(i, NQT - 2)
                if more:
                    rotary_sums(i + 1)
                    split_keys(i + 1)
                split_probs(i, NQT - 1)
                outputs(i, 2)
                if more:
                    split_rotary(i + 1)
                    split_plain(i + 1)
                outputs(i, 3)

            rotary_parts(0)
            rotary_sums(0)
            split_keys(0)
            split_rotary(0)
            split_plain(0)
            with v.Fori(0, PAIRS - 1) as i:
                attend(i, True)
            attend(PAIRS - 1, False)

            def norm_tile(u, t):
                item = u * NT + t
                V.bn_stats(stats[:, t, 0:6], resid[:, t, halves[0]])
                own.link(V.bn_stats(stats[:, t, 6:12], resid[:, t, halves[1]]))
                own.link(V.bn_aggr(mean_var[:, t, :], stats[:, t, :]))
                V.tensor_scalar_add(mean_var[:, t, 1:2], mean_var[:, t, 1:2], LN_EPS).then_inc(ln_var.sem, 1)
                v.wait_ge(gb_in, (u + 1) * 32)
                V.scalar_tensor_tensor(out=resid[:, t, :], in0=resid[:, t, :], scalar=mean_var[:, t, 0:1],
                                       in1=gb[:, 0, :], op0=sub, op1=ALU.mult).then_inc(ln_centred.sem, 1)

            def square(use, u, scale):
                for t in range(NT):
                    if use == 0:
                        v.wait_ge(xr_in[t], 16)
                    else:
                        v.wait_ge(ln_bout.sem, ln_bout.ready(t))
                    v.wait_ge(pr_ps.sem, pr_ps.ready(use * NT + t))
                    V.scalar_tensor_tensor(out=resid[:, t, :], in0=resid[:, t, :], scalar=scale,
                                           in1=ps[2 + t % 2][:], op0=ALU.mult, op1=ALU.add).then_inc(pr_add.sem, 1)
                    v.wait_ge(pr_add.sem, pr_add.ready(use * NT + t))
                    norm_tile(u, t)
                    if t:
                        split_tile(u + 1, t - 1)
                split_tile(u + 1, NT - 1)

            def square_lo(use, w_hi, w_lo, raw, k):
                v.wait_ge(wsq_hi_done.sem, wsq_hi_done.ready(use * NK + k))
                tt(w_lo[:, k, :], raw[:, k, :], w_hi[:, k, :], sub).then_inc(wsq_odd_lo.sem, 1)

            for k in range(NK):
                v.wait_ge(oT_hi_done.sem, oT_hi_done.ready(k))
                tt(actT_lo[:, k, :], oT_f[:, k, :], actT_hi[:, k, :], sub).then_inc(oT_lo_done.sem, 1)
                if k % 2:
                    square_lo(0, wo_hi, wo_lo, wo_raw, k)
            square(0, 0, ALPHA)

            def ffn(l, behind):
                hid_hi, hid_lo, _, _, _, gate, hid_f = ffn_m[l]

                def hidden(f, slot):
                    item = f + l * NF
                    for n, h in enumerate(halves):
                        v.wait_ge(gate_done.sem, gate_done.ready(item * 2 + n))
                        v.wait_ge(hid_lo_done.sem, hid_lo_done.free(item * 2 + n, 2))
                        tt(hid_f[:, h], ps[1][:, h], gate[:, h], ALU.mult).then_inc(hid_f_done.sem, 1)
                    for n, h in enumerate(halves):
                        v.wait_ge(hid_hi_done.sem, hid_hi_done.ready(item * 2 + n))
                        tt(hid_lo[:, slot, h], hid_f[:, h], hid_hi[:, slot, h], sub).then_inc(hid_lo_done.sem, 1)

                def accumulate(f, behind=None):
                    item = f + l * NF
                    for m in range(2 * NT):
                        t, h = divmod(m, 2)
                        v.wait_ge(down_ps.sem, down_ps.ready(item * 16 + m))
                        r = resid[:, t, halves[h]]
                        tt(r, bank(m), r, ALU.add).then_inc(acc_done.sem, 1)
                        if h and behind:
                            behind(t)

                hidden(0, 0)
                with v.Fori(0, NF // 2 - 1) as i:
                    hidden(i * 2 + 1, 1)
                    accumulate(i * 2)
                    hidden(i * 2 + 2, 0)
                    accumulate(i * 2 + 1)
                hidden(NF - 1, 1)
                accumulate(NF - 2)
                accumulate(NF - 1, behind)

            def first_norm(t):
                v.wait_ge(acc_done.sem, acc_done.ready((NF - 1) * 16 + 2 * t + 1))
                norm_tile(1, t)
                if 2 <= t < 6:
                    split_tile(2, t - 2)

            def last_norm(t):
                v.wait_ge(acc_done.sem, acc_done.ready((2 * NF - 1) * 16 + 2 * t + 1))
                norm_tile(3, t)

            v.wait_ge(ln_scaled.sem, ln_scaled.ready(NT - 1))
            ffn(0, first_norm)

            V.tensor_copy(conv_cols[:, :, CC_HI:CC_HI + PE_TAPS], dw_hi[:])
            tt(conv_cols[:, :, CC_LO:CC_LO + PE_TAPS], conv_cols[:, :, CC_DW:CC_DW + PE_TAPS], dw_hi[:], sub
               ).then_inc(cc_done, 1)
            v.wait_ge(cc_done, 1)

            def columns(c, slot, used=True):
                if used:
                    v.wait_ge(tap_done.sem, tap_done.ready((c - 1) * (TAPS - PE_TAPS) * 2 - 1))
                V.tensor_copy(conv_now[:, slot, :], conv_cols[:, bass.ds(c, 1), :].rearrange("p o n -> p (o n)")
                              ).then_inc(now_done.sem, 1)

            def gated(c, slot):
                v.wait_ge(now_done.sem, now_done.ready(c))
                for n, h in enumerate(halves):
                    v.wait_ge(sig_done.sem, sig_done.ready(c * 2 + n))
                    V.scalar_tensor_tensor(out=glu[:, slot, PAD + HALF * n:PAD + HALF * (n + 1)],
                                           in0=ps[0][:, h], scalar=conv_now[:, slot, CC_VALUE:CC_VALUE + 1],
                                           in1=sig[:, h], op0=ALU.add, op1=ALU.mult).then_inc(glu_done.sem, 1)
                v.wait_ge(glu_hi_done.sem, glu_hi_done.ready(c))
                tt(glu_lo[:, slot, :], glu[:, slot, :], glu_hi[:, slot, :], sub).then_inc(glu_lo_done.sem, 1)

            def taps(c, slot):
                count = TAPS - PE_TAPS
                v.wait_ge(conv_out.sem, conv_out.ready(c))
                for j in range(count):
                    w = conv_now[:, slot, CC_DW + PE_TAPS + j:CC_DW + PE_TAPS + j + 1]
                    for n in range(2):
                        start = HALF * n + PE_TAPS + j
                        acc = conv_acc[:, halves[n]]
                        if j:
                            v.wait_ge(tap_done.sem, tap_done.ready((c * count + j - 1) * 2 + n))
                        dst = acc if j < count - 1 else (
                            convT[:, bass.ds(c, 1), halves[n]].rearrange("p o n -> p (o n)"))
                        V.scalar_tensor_tensor(out=dst, in0=glu[:, slot, start:start + HALF], scalar=w, in1=acc,
                                               op0=ALU.mult, op1=ALU.add).then_inc(tap_done.sem, 1)

            columns(0, 0, False)
            columns(1, 1, False)
            for t in range(4, NT):
                split_tile(2, t)
            v.wait_ge(pads_done, 1)
            gated(0, 0)
            gated(1, 1)
            with v.Fori(0, NK // 2 - 1) as i:
                for b in range(2):
                    taps(i * 2 + b, b)
                    columns(i * 2 + b + 2, b)
                    gated(i * 2 + b + 2, b)
            taps(NK - 2, 0)
            taps(NK - 1, 1)
            v.wait_ge(tap_done.sem, tap_done.ready(2 * NK * (TAPS - PE_TAPS) - 1))

            for t in range(NT):
                src = ps[t % 2]
                v.wait_ge(cl_ps.sem, cl_ps.ready(t))
                V.bn_stats(stats[:, t, 0:6], src[:, halves[0]])
                own.link(V.bn_stats(stats[:, t, 6:12], src[:, halves[1]]))
                own.link(V.bn_aggr(mean_var[:, t, :], stats[:, t, :]))
                V.tensor_scalar_add(mean_var[:, t, 1:2], mean_var[:, t, 1:2], LN_EPS).then_inc(cl_var.sem, 1)
                v.wait_ge(cl_rstd.sem, cl_rstd.ready(t))
                V.tensor_scalar(convT[:, :, tok[t]], src[:].rearrange("p (k n) -> p k n", k=NK),
                                mean_var[:, t, 0:1], rstd[:, t, 0:1], sub, ALU.mult).then_inc(cl_norm.sem, 1)
                if t % 2:
                    square_lo(1, wx_hi, wx_lo, wx_raw, t)
                if t:
                    v.wait_ge(sT_hi_done.sem, sT_hi_done.ready(t - 1))
                    tt(actT_lo[:, :, tok[t - 1]], convT[:, :, tok[t - 1]], actT_hi[:, :, tok[t - 1]], sub
                       ).then_inc(sT_lo_done.sem, 1)
            v.wait_ge(sT_hi_done.sem, sT_hi_done.ready(NT - 1))
            tt(actT_lo[:, :, tok[NT - 1]], convT[:, :, tok[NT - 1]], actT_hi[:, :, tok[NT - 1]], sub
               ).then_inc(sT_lo_done.sem, 1)
            square(1, 2, 1.0)
            v.wait_ge(ln_scaled.sem, ln_scaled.ready(3 * NT - 1))
            ffn(1, last_norm)

        @block.gpsimd
        def _(pool):
            G = nc.gpsimd
            sub = ALU.subtract
            for f in flows:
                pool.sem_inc(f.sem, CREDIT)
            pool.sem_inc(started, 1)
            G.memset(minus_half[:], -0.5).then_inc(pool_steps, 1)
            G.memset(ident[:], 0.0).then_inc(pool_steps, 1)
            pool.wait_ge(pool_steps, 2)
            G.affine_select(out=ident[:], in_=ident[:], compare_op=ALU.not_equal, fill=1.0, base=0,
                            pattern=[[-1, P]], channel_multiplier=1).then_inc(made_consts, 1)
            pool.wait_ge(made_consts, 1)
            for k in range(NK):
                pool.wait_ge(wd_hi_done.sem, wd_hi_done.ready(k))
                G.tensor_tensor(wd_lo[:, k, :], wd_raw[:, k % 2, :], wd_hi[:, k, :], sub).then_inc(wd_lo_done.sem, 1)
            for t in range(NT):
                pool.wait_ge(c_ms.sem, c_ms.ready(t))
                G.tensor_tensor(rstd[:, t, :], mean_var[:, t, :], minus_half[:], ALU.pow).then_inc(c_rstd.sem, 1)

            weight_parts = list(zip(pair_views(wq_lo, wq_raw) + kv_views(wkv_lo, wkv_raw),
                                    pair_views(wq_hi, wq_raw) + kv_views(wkv_hi, wkv_raw)))

            def split_pair(i, part):
                if part == 0:
                    pool.wait_ge(wa_hi_done.sem, wa_hi_done.ready(i))
                (lo, raw), (hi, _) = weight_parts[part]
                ins = G.tensor_tensor(lo, raw, hi, sub)
                if part == len(weight_parts) - 1:
                    ins.then_inc(wa_lo_done.sem, 1)

            def normalise(i, n):
                pool.wait_ge(rsum_done.sem, rsum_done.ready(i * NQT + n))
                G.tensor_tensor(p_f[:, n % 3, :], p_f[:, n % 3, :], rsums[:, n:n + 1].to_broadcast([P, SEQ]),
                                ALU.mult).then_inc(p_normed.sem, 1)

            def attend(i, more):
                for n in range(NQT):
                    normalise(i, n)
                    if more and 6 <= n < 6 + len(weight_parts):
                        split_pair(i + 1, n - 6)

            for part in range(len(weight_parts)):
                split_pair(0, part)
            with pool.Fori(0, PAIRS - 1) as i:
                attend(i, True)
            attend(PAIRS - 1, False)

            def square_lo(use, w_hi, w_lo, raw, k):
                pool.wait_ge(wsq_hi_done.sem, wsq_hi_done.ready(use * NK + k))
                G.tensor_tensor(w_lo[:, k, :], raw[:, k, :], w_hi[:, k, :], sub).then_inc(wsq_even_lo.sem, 1)

            def norm_tile(u, t):
                item = u * NT + t
                pool.wait_ge(ln_var.sem, ln_var.ready(item))
                G.tensor_tensor(rstd[:, t, 0:1], mean_var[:, t, 1:2], minus_half[:, 0:1], ALU.pow
                                ).then_inc(ln_rstd.sem, 1)
                pool.wait_ge(gb_in, (u + 1) * 32)
                pool.wait_ge(ln_unit.sem, ln_unit.ready(item))
                G.tensor_tensor(resid[:, t, :], resid[:, t, :], gb[:, 1, :], ALU.add).then_inc(ln_done.sem, 1)

            def split_13(l, f, slot):
                w13_hi, w13_lo, w13_raw = up_w[l]
                pool.wait_ge(w13_hi_done.sem, w13_hi_done.ready(f + l * NF))
                G.tensor_tensor(w13_lo[:, slot], w13_raw[:, slot], w13_hi[:, slot], sub).then_inc(w13_lo_done.sem, 1)

            for k in range(0, NK, 2):
                square_lo(0, wo_hi, wo_lo, wo_raw, k)
            def norm_square(u, l):
                for t in range(NT):
                    norm_tile(u, t)
                    if t in (3, 5):
                        split_13(l, t // 4, t // 4)

            norm_square(0, 0)

            def ffn(l):
                w2_hi, w2_lo, w2_raw = ffn_m[l][2:5]

                def split_2(f, slot):
                    pool.wait_ge(w2_hi_done.sem, w2_hi_done.ready(f + l * NF))
                    G.tensor_tensor(w2_lo[:, slot, :], w2_raw[:, slot, :], w2_hi[:, slot, :], sub
                                    ).then_inc(w2_lo_done.sem, 1)

                split_2(0, 0)
                with pool.Fori(0, NF // 2 - 1) as i:
                    for b in range(2):
                        split_13(l, i * 2 + b + 2, b)
                        split_2(i * 2 + b + 1, 1 - b)
                split_2(NF - 1, 1)

            ffn(0)

            def split_win(c, slot):
                pool.wait_ge(win_hi_done.sem, win_hi_done.ready(c))
                G.tensor_tensor(win_lo[:, slot], win_raw[:, slot], win_hi[:, slot], sub).then_inc(win_lo_done.sem, 1)

            def diagonals(c, slot):
                pool.wait_ge(now_done.sem, now_done.ready(c))
                pool.wait_ge(conv_ps.sem, conv_ps.free(c, 1))
                for dst, first in ((diag_hi, CC_HI), (diag_lo, CC_LO)):
                    for j in range(PE_TAPS):
                        w = conv_now[:, slot, first + j:first + j + 1]
                        ins = G.tensor_tensor(dst[:, j, :], ident[:], w.to_broadcast([P, P]), ALU.mult)
                ins.then_inc(diag_done.sem, 1)

            split_win(0, 0)
            for t in range(NT):
                norm_tile(1, t)
                if t == 0:
                    pool.wait_ge(bout_in, 16)
                if 2 <= t < 6:
                    pool.wait_ge(ln_scaled.sem, ln_scaled.ready(NT + t - 2))
                    G.tensor_tensor(resid[:, t - 2, :], resid[:, t - 2, :], bout_b[:], ALU.add).then_inc(ln_bout.sem, 1)
            split_win(1, 1)
            for t in range(4, NT):
                pool.wait_ge(ln_scaled.sem, ln_scaled.ready(NT + t))
                G.tensor_tensor(resid[:, t, :], resid[:, t, :], bout_b[:], ALU.add).then_inc(ln_bout.sem, 1)
            pool.wait_ge(ln_bout.sem, ln_bout.ready(NT - 1))
            G.memset(glu[:, :, 0:PAD], 0.0)
            G.memset(glu[:, :, PAD + SEQ:], 0.0).then_inc(pads_done, 1)
            pool.wait_ge(ln_done.sem, ln_done.ready(2 * NT - 1))
            diagonals(0, 0)
            with pool.Fori(0, NK // 2 - 1) as i:
                for b in range(2):
                    split_win(i * 2 + b + 2, b)
                    diagonals(i * 2 + b + 1, 1 - b)
            diagonals(NK - 1, 1)
            for t in range(NT):
                pool.wait_ge(cl_var.sem, cl_var.ready(t))
                G.tensor_tensor(rstd[:, t, 0:1], mean_var[:, t, 1:2], minus_half[:, 0:1], ALU.pow
                                ).then_inc(cl_rstd.sem, 1)
                if t % 2 == 0:
                    square_lo(1, wx_hi, wx_lo, wx_raw, t)
            norm_square(2, 1)
            ffn(1)
            for t in range(NT):
                norm_tile(3, t)


_INS = ['x', 'positions', 'ln_g', 'ln_b', 'mla_w_dq', 'mla_q_norm', 'mla_w_uq', 'mla_w_dkv', 'mla_kv_norm',
        'mla_w_ukv', 'mla_w_o', 'conv_w_in', 'conv_b_in', 'conv_dw', 'conv_dw_b', 'conv_ln_g', 'conv_ln_b',
        'conv_w_out', 'conv_b_out', 'ffn_w1', 'ffn_w3', 'ffn_w2']


def kernel(**inputs):
    import concourse.bacc as bacc
    from concourse.bass_utils import run_bass_kernel_spmd as run

    nc = bacc.Bacc("TRN2", target_bir_lowering=False, num_devices=1)
    arrays, args = {}, []

    def add(name, a):
        arrays[name] = a
        args.append(nc.dram_tensor(name, a.shape, mybir.dt.from_np(a.dtype), kind="ExternalInput").ap())

    for name in _INS:
        add(f"in_{name}_dram", np.ascontiguousarray(inputs[name]))
    j = np.arange(P) % ROPE
    exponent = (-2.0 * (j % (ROPE // 2)) / ROPE).astype(np.float32)
    inv_freq = np.float32(10000.0) ** exponent
    rope_const = np.stack([inv_freq, np.where(j < ROPE // 2, -1.0, 1.0), np.full(P, math.pi / 2)], axis=1)
    add("rope_const_dram", np.ascontiguousarray(rope_const.astype(np.float32)))
    args.append(nc.dram_tensor("out_0_dram", (1, SEQ, D), F32, kind="ExternalOutput").ap())
    trunk(nc, *args)
    r = run(nc, [arrays], core_ids=[0])
    return r.results[0]["out_0_dram"]
```

```python
import math
from contextlib import ExitStack

import numpy as np
import concourse.bass as bass
from concourse import mybir

F32 = mybir.dt.float32
F32R = mybir.dt.float32r
I32 = mybir.dt.int32
ALU = mybir.AluOpType
ACT = mybir.ActivationFunctionType

P = 128
D = 1024
SEQ = 1024
NK = D // P
NT = SEQ // P
HALF = 512
HEADS, NOPE, ROPE, VDIM = 16, 64, 32, 64
QK = NOPE + ROPE
PAIRS = HEADS // 2
Q_RANK, KV_RANK = 384, 256
NQ, NKV = Q_RANK // P, KV_RANK // P
DOWN = Q_RANK + KV_RANK + ROPE
D_FF = 2816
NF = D_FF // P
TAPS = 31
PAD = TAPS // 2
PE_TAPS = 9
MORE_TAPS = 15
TAP_STEPS = 2 * (NK * (TAPS - PE_TAPS) - MORE_TAPS + 1)
ALPHA = float(4 ** 0.25)
LN_EPS, RMS_EPS = 1e-5, 1e-6
SCALE = 1.0 / math.sqrt(QK)
QUARTER = SEQ // 4
CHUNK = 4 * P
NQT = 2 * NT
NC = NQT * P // CHUNK
CREDIT = 4
MAGIC = 1.5 * 2.0 ** 23


class Flow:

    def __init__(self, sem):
        self.sem = sem

    def ready(self, item):
        return item + (1 + CREDIT)

    def free(self, item, slots):
        return item + (1 - slots + CREDIT)


class Chain:

    def __init__(self, sem, eng):
        self.sem, self.eng, self.count = sem, eng, 0

    def link(self, ins):
        ins.then_inc(self.sem, 1)
        self.count += 1
        self.eng.wait_ge(self.sem, self.count)


def turn_pieces(turns, count):
    rest, out = 2 * math.pi * turns, []
    for _ in range(count):
        unit = 2.0 ** (math.floor(math.log2(rest)) - 11)
        out.append(math.floor(rest / unit) * unit)
        rest -= out[-1]
    return out


def pair_views(w, raw):
    src = raw[:].rearrange("p k (j d) -> p k j d", j=2)
    h = ROPE // 2

    def dst(a, d):
        return w[:, :, a:a + 2 * d].rearrange("p k (j d) -> p k j d", j=2)

    swapped = dst(P + 2 * ROPE, ROPE)
    return [(dst(0, NOPE), src[:, :, :, 0:NOPE]), (dst(P, ROPE), src[:, :, :, NOPE:QK]),
            (swapped[:, :, :, 0:h], src[:, :, :, NOPE + h:QK]), (swapped[:, :, :, h:ROPE], src[:, :, :, NOPE:NOPE + h])]


def kv_views(w, raw):
    src = raw[:].rearrange("p k (j d) -> p k j d", j=2)
    return [(w[:, :, a:a + P].rearrange("p k (j d) -> p k j d", j=2), src[:, :, :, b:b + NOPE])
            for a, b in ((0, 0), (P, NOPE))]


def trunk(nc, x, positions, ln_g, ln_b, w_dq, q_norm, w_uq, w_dkv, kv_norm, w_ukv, w_o, w_in, b_in,
          conv_dw, conv_dw_b, conv_ln_g, conv_ln_b, w_out, b_out, ffn_w1, ffn_w3, ffn_w2, rope_const, out):
    x_v = x[0].rearrange("(t p) d -> t p d", p=P)
    out_v = out[0].rearrange("(t p) d -> t p d", p=P)
    dq_v = w_dq[0].rearrange("(k p) n -> p k n", p=P)
    dkv_v = w_dkv[0].rearrange("(k p) n -> p k n", p=P)
    uq_v = w_uq[0].rearrange("(k p) n -> p k n", p=P)
    ukv_v = w_ukv[0].rearrange("(k p) n -> p k n", p=P)
    wo_v = w_o[0].rearrange("(k p) n -> k p n", p=P)
    wout_v = w_out[0].rearrange("(k p) n -> k p n", p=P)
    win_v = w_in[0].rearrange("(k p) (g n) -> p g k n", p=P, g=2)
    w1_v = [ffn_w1[l].rearrange("(k p) n -> p k n", p=P) for l in range(2)]
    w3_v = [ffn_w3[l].rearrange("(k p) n -> p k n", p=P) for l in range(2)]
    w2_v = [ffn_w2[l].rearrange("(f p) n -> p f n", p=P) for l in range(2)]

    ctx = ExitStack()
    with ctx:
        def sb(name, shape, dt=F32):
            return ctx.enter_context(nc.sbuf_tensor(name, shape, dt))

        gaps = [0]
        KEPT = 9

        def region(start_kb, *specs):
            got = []
            with ExitStack() as r:
                if start_kb > -KEPT:
                    gaps[0] += 1
                    r.enter_context(nc.sbuf_tensor(f"gap{gaps[0]}", [P, (KEPT + start_kb) * 256], F32))
                for name, shape, dt in specs:
                    got.append(r.enter_context(nc.sbuf_tensor(name, shape, dt)))
            return got

        def flow(name):
            f = Flow(ctx.enter_context(nc.semaphore(name)))
            flows.append(f)
            return f

        def sem(name):
            return ctx.enter_context(nc.semaphore(name))

        flows = []

        ident = sb("ident", [P, P])
        minus_half = sb("minus_half", [P, 2])
        consts = sb("consts", [P, 4])
        cols = sb("cols", [P, 48])
        CC_DW, CC_BIAS, CC_VALUE, CC_GATE, CC_HI, CC_LO, CC = 0, 31, 32, 33, 34, 34 + PE_TAPS, 34 + 2 * PE_TAPS
        conv_cols = sb("conv_cols", [P, NK, CC])
        conv_now = sb("conv_now", [P, 2, CC])
        dw_hi = sb("dw_hi", [P, NK, PE_TAPS], F32R)
        more_hi = sb("more_hi", [P, MORE_TAPS], F32R)
        more_cols = sb("more_cols", [P, 2, MORE_TAPS])
        stats = sb("stats", [P, NT, 12])
        mean_var = sb("mean_var", [P, NT, 2])
        rstd = sb("rstd", [P, NT, 2])
        negmax = sb("negmax", [P, NQT])
        sums = sb("sums", [P, NQT])
        rsums = sb("rsums", [P, NQT])
        C_GQ, C_BIN, C_DWB, C_LNG, C_LNB = 0, 5, 21, 29, 37
        N_COLS = 45

        [gb] = region(-KEPT, ("gb", [P, 2, D], F32))
        diag_hi, diag_lo = region(-KEPT, ("diag_hi", [P, PE_TAPS, P], F32R), ("diag_lo", [P, PE_TAPS, P], F32R))
        actT_hi, actT_lo = region(32, ("actT_hi", [P, NK, SEQ], F32R), ("actT_lo", [P, NK, SEQ], F32R))
        [resid] = region(0, ("resid", [P, NT, D], F32))
        [x_stage] = region(0, ("x_stage", [P, 4, D], F32))
        [x_stage2] = region(96, ("x_stage2", [P, 4, D], F32))
        [vec_rows, dw_rows, pos_i, ang, turns, cosv, sinv, absr] = region(
            16, ("vec_rows", [P, P], F32), ("dw_rows", [P, D], F32), ("pos_i", [P, QUARTER], I32),
            ("ang", [P, QUARTER], F32), ("turns", [P, QUARTER], F32), ("cosv", [P, QUARTER], F32),
            ("sinv", [P, QUARTER], F32), ("absr", [P, QUARTER], F32))
        cT_hi, cT_lo, tab, kr_f = region(96, ("cT_hi", [P, 5, SEQ], F32R), ("cT_lo", [P, 5, SEQ], F32R),
                                         ("tab", [P, SEQ], F32), ("kr_f", [P, SEQ], F32))
        [wd_hi, wd_lo] = region(144, ("wd_hi", [P, NK, DOWN], F32R), ("wd_lo", [P, NK, DOWN], F32R))
        [wd_raw] = region(165, ("wd_raw", [P, NK, DOWN], F32))
        [c_tok] = region(186, ("c_tok", [P, DOWN + ROPE], F32))
        [pt_hi, pt_lo] = region(0, ("pt_hi", [P, 2, NK, CHUNK], F32R), ("pt_lo", [P, 2, NK, CHUNK], F32R))
        q_hi, q_lo, k_hi, k_lo = region(
            64, ("q_hi", [P, 2, SEQ], F32R), ("q_lo", [P, 2, SEQ], F32R),
            ("k_hi", [P, 2, SEQ], F32R), ("k_lo", [P, 2, SEQ], F32R))
        [oT_f] = region(64, ("oT_f", [P, NK, SEQ], F32))
        (v2, p_f, rope_m, wq_hi, wq_lo, wkv_hi, wkv_lo, wq_raw, wkv_raw, o_sum, vT) = region(
            140, ("v2", [P, NT, 2, 2 * VDIM], F32R), ("p_f", [P, 3, SEQ], F32), ("rope_m", [P, 2, SEQ], F32),
            ("wq_hi", [P, NQ, 2 * P], F32R), ("wq_lo", [P, NQ, 2 * P], F32R),
            ("wkv_hi", [P, NKV, 2 * P], F32R), ("wkv_lo", [P, NKV, 2 * P], F32R),
            ("wq_raw", [P, NQ, 2 * QK], F32), ("wkv_raw", [P, NKV, 2 * P], F32),
            ("o_sum", [P, 2, CHUNK], F32), ("vT", [P, SEQ], F32))
        oT_dram = nc.dram_tensor("oT_dram", (NK, P, SEQ), F32, kind="Internal").ap()
        wo_lo, wo_hi = region(96, ("wo_lo", [P, NK, D], F32R), ("wo_hi", [P, NK, D], F32R))
        [wo_raw] = region(96, ("wo_raw", [P, NK, D], F32))
        [wx_hi] = region(128, ("wx_hi", [P, NK, D], F32R))
        [wx_lo] = region(161, ("wx_lo", [P, NK, D], F32R))
        [wx_raw] = region(161, ("wx_raw", [P, NK, D], F32))

        def up_weights(start, tag):
            hi, lo = region(start, (f"w13_hi{tag}", [P, 2, 2, NK, P], F32R), (f"w13_lo{tag}", [P, 2, 2, NK, P], F32R))
            [raw] = region(start + 16, (f"w13_raw{tag}", [P, 2, 2, NK, P], F32))
            return hi, lo, raw

        def ffn_memory(start, tag):
            hid_hi, hid_lo, w2_hi, w2_lo, gate, hid_f = region(
                start, (f"hid_hi{tag}", [P, 2, SEQ], F32R), (f"hid_lo{tag}", [P, 2, SEQ], F32R),
                (f"w2_hi{tag}", [P, 2, D], F32R), (f"w2_lo{tag}", [P, 2, D], F32R),
                (f"gate{tag}", [P, SEQ], F32), (f"hid_f{tag}", [P, SEQ], F32))
            [w2_raw] = region(start + 24, (f"w2_raw{tag}", [P, 2, D], F32))
            return hid_hi, hid_lo, w2_hi, w2_lo, w2_raw, gate, hid_f

        win_hi, win_lo, win_raw = up_weights(161, 0)
        up_w = [(win_hi, win_lo, win_raw), up_weights(96, 1)]
        ffn_m = [ffn_memory(96, 0), ffn_memory(128, 1)]
        [bout_b] = region(136, ("bout_b", [P, D], F32))
        [more_diag_hi] = region(161, ("more_diag_hi", [P, MORE_TAPS, P], F32R))
        [more_diag_lo] = region(177, ("more_diag_lo", [P, MORE_TAPS, P], F32R))
        convT, glu, glu_hi, glu_lo, sig, conv_acc = region(
            96, ("convT", [P, NK, SEQ], F32), ("glu", [P, 2, SEQ + 2 * PAD], F32),
            ("glu_hi", [P, 2, SEQ + 2 * PAD], F32R), ("glu_lo", [P, 2, SEQ + 2 * PAD], F32R),
            ("sig", [P, SEQ], F32), ("conv_acc", [P, SEQ], F32))

        ps = [ctx.enter_context(nc.psum_tensor(f"ps{i}", [P, 2 * HALF], F32)) for i in range(4)]

        started = sem("started")
        x_in = [sem(f"x_in{i}") for i in range(NT)]
        small_in = sem("small_in")
        cols_in = sem("cols_in")
        wd_in = [sem(f"wd_in{k}") for k in range(NK)]
        made_consts = sem("made_consts")
        cols_ps, cols_done = sem("cols_ps"), sem("cols_done")
        ang_done, tab_done = sem("ang_done"), sem("tab_done")
        tp_ps, tp_hi, tp_lo = flow("tp_ps"), flow("tp_hi"), flow("tp_lo")
        wd_hi_done, wd_lo_done = flow("wd_hi_done"), flow("wd_lo_done")
        c_ps, c_sq, c_ms, c_rstd, c_tok_done = (flow(n) for n in ("c_ps", "c_sq", "c_ms", "c_rstd", "c_tok_done"))
        ct_ps, ct_hi, ct_lo = flow("ct_ps"), flow("ct_hi"), flow("ct_lo")
        krope_done, krope_hi, krope_lo = sem("krope_done"), sem("krope_hi"), sem("krope_lo")
        wq_in, wkv_in = sem("wq_in"), sem("wkv_in")
        wa_hi_done, wa_lo_done = flow("wa_hi_done"), flow("wa_lo_done")
        k_ps, qn_ps, qr_ps, vt_ps, v_ps, vt_done = (flow(n) for n in ("k_ps", "qn_ps", "qr_ps", "vt_ps", "v_ps", "vt_done"))
        o_stored = [flow(f"o_stored{b}") for b in range(2)]
        oT_in = [sem(f"oT_in{k}") for k in range(NK)]
        k_hi_done, k_lo_done, qn_hi_done, qn_lo_done = (flow(n) for n in (
            "k_hi_done", "k_lo_done", "qn_hi_done", "qn_lo_done"))
        v_hi_done, v_lo_done = flow("v_hi_done"), flow("v_lo_done")
        qr_parts, qr_sum, qr_hi_done, qr_lo_done = (flow(n) for n in (
            "qr_parts", "qr_sum", "qr_hi_done", "qr_lo_done"))
        s_ps, s_max, p_done = flow("s_ps"), flow("s_max"), flow("p_done")
        pt_ps, pt_hi_done, pt_lo_done = flow("pt_ps"), flow("pt_hi_done"), flow("pt_lo_done")
        rsum_done, p_normed, o_ps, o_first_done, o_done = (flow(n) for n in (
            "rsum_done", "p_normed", "o_ps", "o_first_done", "o_done"))
        xr_in = [sem(f"xr_in{i}") for i in range(NT)]
        oT_hi_done, oT_lo_done = flow("oT_hi_done"), flow("oT_lo_done")
        wsq_in = [sem(f"wsq_in{k}") for k in range(NK)]
        wsq_hi_done, wsq_even_lo, wsq_odd_lo = flow("wsq_hi_done"), flow("wsq_even_lo"), flow("wsq_odd_lo")
        pr_ps, pr_add = flow("pr_ps"), flow("pr_add")
        gb_in = sem("gb_in")
        bout_in = sem("bout_in")
        ln_var, ln_rstd, ln_centred, ln_unit, ln_done, ln_scaled, ln_bout = (flow(n) for n in (
            "ln_var", "ln_rstd", "ln_centred", "ln_unit", "ln_done", "ln_scaled", "ln_bout"))
        w13_in, w2_in = [sem(f"w13_in{b}") for b in range(2)], [sem(f"w2_in{b}") for b in range(2)]
        w13_hi_done, w13_lo_done, w2_hi_done, w2_lo_done = (flow(n) for n in (
            "w13_hi_done", "w13_lo_done", "w2_hi_done", "w2_lo_done"))
        up_ps, gate_done, hid_f_done, hid_hi_done, hid_lo_done, down_ps, acc_done = (flow(n) for n in (
            "up_ps", "gate_done", "hid_f_done", "hid_hi_done", "hid_lo_done", "down_ps", "acc_done"))
        win_in = [sem(f"win_in{b}") for b in range(2)]
        (win_hi_done, win_lo_done, in_ps, sig_done, glu_done, glu_hi_done, glu_lo_done, now_done, diag_done, conv_ps,
         conv_out, tap_done) = (flow(n) for n in (
            "win_hi_done", "win_lo_done", "in_ps", "sig_done", "glu_done", "glu_hi_done", "glu_lo_done", "now_done",
            "diag_done", "conv_ps", "conv_out", "tap_done"))
        cc_done, more_diag_done = sem("cc_done"), sem("more_diag_done")
        pads_done = sem("pads_done")
        cl_ps, cl_var, cl_rstd, cl_norm, cb_ps, silu_done, sT_hi_done, sT_lo_done = (flow(n) for n in (
            "cl_ps", "cl_var", "cl_rstd", "cl_norm", "cb_ps", "silu_done", "sT_hi_done", "sT_lo_done"))
        stored = sem("stored")
        dve_steps, act_steps, pool_steps = sem("dve_steps"), sem("act_steps"), sem("pool_steps")

        block = ctx.enter_context(nc.Block())
        tok = [slice(t * P, (t + 1) * P) for t in range(NT)]
        halves = [slice(0, HALF), slice(HALF, 2 * HALF)]

        def bank(m):
            return ps[2 + m % 4 // 2][:, halves[m % 2]]

        def turned(use, t):
            if use == 2 and t >= 4:
                return ps[2 + t % 2]
            return ps[2] if use in (1, 3) and t == NT - 1 else ps[t % 2]

        @block.sync
        def _(sp):
            with nc.allow_non_contiguous_dma(reason="vectors of a few hundred elements"):
                for t in range(4):
                    sp.dma_start(x_stage[:, t, :], x_v[t]).then_inc(x_in[t], 16)
                sp.dma_start(consts[:, 0:3], rope_const).then_inc(small_in, 16)
                for q in range(4):
                    sp.dma_start(pos_i[32 * q:32 * q + 32, :],
                                 positions[:, QUARTER * q:QUARTER * (q + 1)].to_broadcast([32, QUARTER])
                                 ).then_inc(small_in, 16)
                for row, v, n in ((C_GQ, q_norm, NQ), (C_GQ + NQ, kv_norm, NKV), (C_BIN, b_in, 2 * NK),
                                  (C_DWB, conv_dw_b, NK), (C_LNG, conv_ln_g, NK), (C_LNB, conv_ln_b, NK)):
                    sp.dma_start(vec_rows[row:row + n, :], v[0].rearrange("(r p) -> r p", p=P)).then_inc(cols_in, 16)
                sp.dma_start(dw_rows[0:TAPS, :], conv_dw[0]).then_inc(cols_in, 16)
            for k in range(NK):
                sp.dma_start(wd_raw[:, k, 0:Q_RANK], dq_v[:, k, :]).then_inc(wd_in[k], 16)
                sp.dma_start(wd_raw[:, k, Q_RANK:DOWN], dkv_v[:, k, :]).then_inc(wd_in[k], 16)
                if k == 1:
                    for t in range(4, NT):
                        sp.dma_start(x_stage2[:, t - 4, :], x_v[t]).then_inc(x_in[t], 16)
            sp.wait_ge(started, 1)

            sp.wait_ge(c_ps.sem, c_ps.ready(NT - 1))

            def load_pair(i):
                sp.dma_start(wq_raw[:], uq_v[:, :, bass.ds(i * (2 * QK), 2 * QK)]).then_inc(wq_in, 16)
                sp.dma_start(wkv_raw[:], ukv_v[:, :, bass.ds(i * (2 * P), 2 * P)]).then_inc(wkv_in, 16)

            def store_outputs(i):
                for c in range(NC):
                    sp.wait_ge(o_done.sem, o_done.ready(i * NC + c))
                    rows, q0 = slice(VDIM * (c // 2), VDIM * (c // 2 + 1)), CHUNK * (c % 2)
                    sp.dma_start(oT_dram[bass.ds(i, 1), rows, q0:q0 + CHUNK].rearrange("o p n -> (o p) n"),
                                 o_sum[0:VDIM, c % 2, :]).then_inc(o_stored[c % 2].sem, 16)

            load_pair(0)
            with sp.Fori(0, PAIRS - 1) as i:
                sp.wait_ge(wa_lo_done.sem, wa_lo_done.ready(i))
                load_pair(i + 1)
                store_outputs(i)

            def load_ln(u):
                if u:
                    sp.wait_ge(ln_done.sem, ln_done.ready(u * NT - 1))
                for n, v in enumerate((ln_g, ln_b)):
                    sp.dma_start(gb[:, n, :], v[u // 2, u % 2:u % 2 + 1, :].to_broadcast([P, D])).then_inc(gb_in, 16)

            load_ln(0)
            sp.wait_ge(vt_ps.sem, vt_ps.ready(PAIRS - 1))
            for k in range(NK):
                sp.dma_start(wo_raw[:, k, :], wo_v[k]).then_inc(wsq_in[k], 16)
            store_outputs(PAIRS - 1)
            for k in range(NK):
                if k in (0, NK - 1):
                    for slot in o_stored:
                        sp.wait_ge(slot.sem, 16 * 2 * (PAIRS if k else PAIRS - 1) + CREDIT)
                sp.dma_start(oT_f[:, k, :], oT_dram[k]).then_inc(oT_in[k], 16)
            for t in range(NT):
                sp.dma_start(resid[:, t, :], x_v[t]).then_inc(xr_in[t], 16)

            def ffn_loads(l):
                def load_13(f, slot, used=True):
                    if used:
                        sp.wait_ge(up_ps.sem, up_ps.ready((f - 2 + l * NF) * 2 + 1))
                    for n, v in enumerate((w1_v[l], w3_v[l])):
                        sp.dma_start(up_w[l][2][:, slot, n], v[:, :, bass.ds(f * P, P)]).then_inc(w13_in[slot], 16)

                def load_2(f, slot, used=True):
                    if used:
                        sp.wait_ge(down_ps.sem, down_ps.ready((f - 2 + l * NF) * 16 + 15))
                    sp.dma_start(ffn_m[l][4][:, slot, :], w2_v[l][:, bass.ds(f, 1), :].rearrange("p o n -> p (o n)")
                                 ).then_inc(w2_in[slot], 16)
                return load_13, load_2

            def load_ffn(l):
                load_13, load_2 = ffn_loads(l)
                load_2(0, 0, False)
                load_2(1, 1, False)
                with sp.Fori(1, NF // 2) as i:
                    for b in range(2):
                        load_13(i * 2 + b, b)
                        load_2(i * 2 + b, b)

            for b in range(2):
                ffn_loads(0)[0](b, b, False)
            sp.wait_ge(pr_ps.sem, pr_ps.ready(NT - 1))
            sp.dma_start(bout_b[:], b_out[0:1, :].to_broadcast([P, D])).then_inc(bout_in, 16)
            load_ffn(0)
            load_ln(1)

            def load_win(c, slot):
                for g in range(2):
                    sp.dma_start(win_raw[:, slot, g], win_v[:, g, :, bass.ds(c * P, P)]).then_inc(win_in[slot], 16)

            for b in range(2):
                sp.wait_ge(up_ps.sem, up_ps.ready((NF - 2 + b) * 2 + 1))
                load_win(b, b)
            with sp.Fori(1, NK // 2) as i:
                for b in range(2):
                    sp.wait_ge(in_ps.sem, in_ps.ready((i * 2 + (b - 2)) * 2 + 1))
                    load_win(i * 2 + b, b)
            sp.wait_ge(in_ps.sem, in_ps.ready(2 * NK - 1))
            for k in (2, 3, 6, 7, 0, 1, 4, 5):
                if k == 0:
                    sp.wait_ge(conv_ps.sem, conv_ps.ready(NK - 1))
                sp.dma_start(wx_raw[:, k, :], wout_v[k]).then_inc(wsq_in[k], 16)
            load_ln(2)
            sp.wait_ge(sT_lo_done.sem, sT_lo_done.ready(NT - 1))
            for b in range(2):
                ffn_loads(1)[0](b, b, False)
            sp.wait_ge(pr_ps.sem, pr_ps.ready(2 * NT - 1))
            load_ffn(1)
            load_ln(3)
            for t in range(NT):
                sp.wait_ge(ln_done.sem, ln_done.ready(3 * NT + t))
                sp.dma_start(out_v[t], resid[:, t, :]).then_inc(stored, 16)
            sp.wait_ge(stored, 16 * NT)

        @block.tensor
        def _(pe):
            mm = nc.tensor.matmul

            def product(dst, terms, last_inc=None):
                n = len(terms)
                for m, ((a_hi, a_lo), (b_hi, b_lo)) in enumerate(terms):
                    mm(dst, a_hi, b_hi, start=m == 0, stop=False)
                    mm(dst, a_hi, b_lo, start=False, stop=False)
                    ins = mm(dst, a_lo, b_hi, start=False, stop=m == n - 1)
                return ins

            def transpose_tile(src, use, t):
                for k in range(NK):
                    ins = nc.tensor.transpose(turned(use, t)[:, tok[k]], src(k), ident[:])
                ins.then_inc(tp_ps.sem, 1)

            pe.wait_ge(started, 1)
            pe.wait_ge(made_consts, 1)
            for t in range(NT):
                pe.wait_ge(x_in[t], 16)
                pe.wait_ge(tp_lo.sem, tp_lo.free(t, 2))
                transpose_tile(lambda k: (x_stage2 if t >= 4 else x_stage)[:, t % 4, tok[k]], 0, t)

            pe.wait_ge(cols_in, 7 * 16)
            nc.tensor.transpose(ps[3][:, 0:N_COLS], vec_rows[0:N_COLS, :], ident[0:N_COLS, 0:N_COLS])
            for k in range(NK):
                ins = nc.tensor.transpose(ps[3][:, 64 + 32 * k:64 + 32 * k + TAPS], dw_rows[0:TAPS, tok[k]],
                                          ident[0:TAPS, 0:TAPS])
            ins.then_inc(cols_ps, 1)

            def transpose_c(t):
                pe.wait_ge(c_tok_done.sem, c_tok_done.ready(t))
                pe.wait_ge(ct_lo.sem, ct_lo.free(t, 2))
                dst = ps[t % 2]
                for j in range(5):
                    nc.tensor.transpose(dst[:, tok[j]], c_tok[:, tok[j]], ident[:])
                nc.tensor.transpose(dst[0:2 * ROPE, tok[5]], c_tok[:, 5 * P:5 * P + 2 * ROPE], ident[:]
                                    ).then_inc(ct_ps.sem, 1)

            pe.wait_ge(tp_lo.sem, tp_lo.ready(NT - 1))
            for t in range(NT):
                if t == 1:
                    pe.wait_ge(cols_done, 1)
                pe.wait_ge(c_tok_done.sem, c_tok_done.free(t, 2))
                dst = ps[2 + t % 2]
                parts = ((dst[:, 0:Q_RANK], slice(0, Q_RANK)), (dst[:, HALF:HALF + DOWN - Q_RANK], slice(Q_RANK, DOWN)))
                for k in range(NK):
                    if t == 0:
                        pe.wait_ge(wd_lo_done.sem, wd_lo_done.ready(k))
                    for d, s in parts:
                        mm(d, actT_hi[:, k, tok[t]], wd_hi[:, k, s], start=k == 0, stop=False)
                        mm(d, actT_hi[:, k, tok[t]], wd_lo[:, k, s], start=False, stop=False)
                        ins = mm(d, actT_lo[:, k, tok[t]], wd_hi[:, k, s], start=False, stop=k == NK - 1)
                ins.then_inc(c_ps.sem, 1)
                if t:
                    transpose_c(t - 1)
            transpose_c(NT - 1)

            cq = [(cT_hi[:, k, :], cT_lo[:, k, :]) for k in range(NQ)]
            ckv = [(cT_hi[:, NQ + k, :], cT_lo[:, NQ + k, :]) for k in range(NKV)]

            def project(dst, w_hi, w_lo, s, c):
                for h in halves:
                    ins = product(dst[:, h], [((w_hi[:, k, s], w_lo[:, k, s]), (c_hi[:, h], c_lo[:, h]))
                                              for k, (c_hi, c_lo) in enumerate(c)])
                return ins

            def rotary_queries(i):
                pe.wait_ge(wa_lo_done.sem, wa_lo_done.ready(i))
                project(ps[0], wq_hi, wq_lo, slice(P, 2 * P), cq).then_inc(qr_ps.sem, 1)

            def keys(i):
                project(ps[1], wkv_hi, wkv_lo, slice(0, P), ckv).then_inc(k_ps.sem, 1)

            def plain_queries(i):
                pe.wait_ge(qr_parts.sem, qr_parts.ready(i))
                project(ps[0], wq_hi, wq_lo, slice(0, P), cq).then_inc(qn_ps.sem, 1)

            def values_transposed(i):
                pe.wait_ge(k_lo_done.sem, k_lo_done.ready(i))
                project(ps[1], wkv_hi, wkv_lo, slice(P, 2 * P), ckv).then_inc(vt_ps.sem, 1)

            def values(i):
                pe.wait_ge(pt_lo_done.sem, pt_lo_done.free(i * NQT * 2, 1))
                for t in range(NT):
                    ins = nc.tensor.transpose(ps[2][:, tok[t]], vT[:, tok[t]], ident[:])
                ins.then_inc(v_ps.sem, 1)

            def scores(i, n):
                j, t = divmod(n, NT)
                if n > 1:
                    pe.wait_ge(p_done.sem, p_done.ready(i * NQT + n - 2))
                q = (q_hi[0:QK, j, tok[t]], q_lo[0:QK, j, tok[t]])
                for h in halves:
                    ins = product(ps[n % 2][:, h], [(q, (k_hi[0:QK, j, h], k_lo[0:QK, j, h]))])
                ins.then_inc(s_ps.sem, 1)

            def transposed(i, n):
                pe.wait_ge(p_normed.sem, p_normed.ready(i * NQT + n))
                for a in range(2):
                    pe.wait_ge(pt_lo_done.sem, pt_lo_done.free((i * NQT + n) * 2 + a, 2))
                    for kk in range(4):
                        ins = nc.tensor.transpose(ps[2][:, tok[4 * a + kk]], p_f[:, n % 3, tok[4 * a + kk]], ident[:])
                    ins.then_inc(pt_ps.sem, 1)

            def times_v(i, c, part):
                item = i * NC + c
                if part == 0:
                    pe.wait_ge(pt_lo_done.sem, pt_lo_done.ready((i * NQT + 4 * c + 3) * 2 + 1))
                    pe.wait_ge(o_done.sem, o_done.free(item, 2))
                o = ps[3][:, halves[c % 2]]
                for k in range(2 * part, 2 * part + 2):
                    v = v2[:, k, c // 2, :]
                    mm(o, v, pt_hi[:, c % 2, k, :], start=k == 0, stop=False)
                    ins = mm(o, v, pt_lo[:, c % 2, k, :], start=False, stop=k == NK - 1)
                if part == 3:
                    ins.then_inc(o_ps.sem, 1)

            def attend(i, more):
                pe.wait_ge(k_lo_done.sem, k_lo_done.ready(i))
                pe.wait_ge(qn_lo_done.sem, qn_lo_done.ready(i))
                pe.wait_ge(qr_lo_done.sem, qr_lo_done.ready(i))
                scores(i, 0)
                pe.wait_ge(vt_done.sem, vt_done.ready(i))
                scores(i, 1)
                values(i)
                for n in range(1, NQT):
                    if n + 1 < NQT:
                        scores(i, n + 1)
                    if n >= 7:
                        times_v(i, *divmod(n - 7, 4))
                    if n == 2:
                        pe.wait_ge(v_lo_done.sem, v_lo_done.ready(i))
                    if n >= 2:
                        transposed(i, n - 2)
                if more:
                    pe.wait_ge(p_done.sem, p_done.ready(i * NQT + NQT - 2))
                    rotary_queries(i + 1)
                times_v(i, 2, 1)
                transposed(i, NQT - 2)
                if more:
                    pe.wait_ge(p_done.sem, p_done.ready(i * NQT + NQT - 1))
                    keys(i + 1)
                times_v(i, 2, 2)
                transposed(i, NQT - 1)
                times_v(i, 2, 3)
                if more:
                    plain_queries(i + 1)
                    values_transposed(i + 1)
                for part in range(4):
                    times_v(i, 3, part)

            pe.wait_ge(ct_lo.sem, ct_lo.ready(NT - 1))
            rotary_queries(0)
            keys(0)
            plain_queries(0)
            values_transposed(0)
            with pe.Fori(0, PAIRS - 1) as i:
                attend(i, True)
            attend(PAIRS - 1, False)

            def transpose_resid(use, t):
                pe.wait_ge(ln_done.sem, ln_done.ready((use - 1) * NT + t))
                pe.wait_ge(tp_lo.sem, tp_lo.free(use * NT + t, 2))
                transpose_tile(lambda k: resid[:, t, tok[k]], use, t)

            def square_tile(use, t, w_hi, w_lo):
                pe.wait_ge(pr_add.sem, pr_add.free(use * NT + t, 2))
                dst = ps[2 + t % 2]
                for k in range(NK):
                    if t == 0:
                        lo_done = wsq_odd_lo if k % 2 else wsq_even_lo
                        pe.wait_ge(lo_done.sem, lo_done.ready(use * NK // 2 + k // 2))
                        if use == 0:
                            pe.wait_ge(oT_lo_done.sem, oT_lo_done.ready(k))
                    a_hi, a_lo = actT_hi[:, k, tok[t]], actT_lo[:, k, tok[t]]
                    for h in halves:
                        mm(dst[:, h], a_hi, w_hi[:, k, h], start=k == 0, stop=False)
                        mm(dst[:, h], a_hi, w_lo[:, k, h], start=False, stop=False)
                        ins = mm(dst[:, h], a_lo, w_hi[:, k, h], start=False, stop=k == NK - 1)
                ins.then_inc(pr_ps.sem, 1)

            def last_tile(ln):
                transpose_resid(ln, NT - 1)
                pe.wait_ge(tp_lo.sem, tp_lo.ready((ln + 1) * NT - 1))

            for t in range(NT):
                square_tile(0, t, wo_hi, wo_lo)
                if t:
                    transpose_resid(1, t - 1)

            def up(l, f, slot, between=None):
                item = f + l * NF
                w_hi, w_lo, _ = up_w[l]
                pe.wait_ge(w13_lo_done.sem, w13_lo_done.ready(item))
                for n, h in enumerate(halves):
                    if n and between:
                        between()
                    pe.wait_ge(hid_f_done.sem, hid_f_done.free(item * 2 + n, 2))
                    for g in range(2):
                        ins = product(ps[g][:, h], [((w_hi[:, slot, g, k, :], w_lo[:, slot, g, k, :]),
                                                     (actT_hi[:, k, h], actT_lo[:, k, h])) for k in range(NK)])
                    ins.then_inc(up_ps.sem, 1)

            def down(l, f, slot, behind=None):
                item = f + l * NF
                hid_hi, hid_lo, w2_hi, w2_lo = ffn_m[l][0:4]
                pe.wait_ge(w2_lo_done.sem, w2_lo_done.ready(item))
                pe.wait_ge(hid_lo_done.sem, hid_lo_done.ready(item * 2 + 1))
                for m in range(2 * NT):
                    t, h = divmod(m, 2)
                    pe.wait_ge(acc_done.sem, acc_done.free(item * 16 + m, 4))
                    product(bank(m), [((hid_hi[:, slot, tok[t]], hid_lo[:, slot, tok[t]]),
                                       (w2_hi[:, slot, halves[h]], w2_lo[:, slot, halves[h]]))]
                            ).then_inc(down_ps.sem, 1)
                    if h and behind:
                        behind(t)

            def ffn(l, between, behind=None):
                up(l, 0, 0, between)
                with pe.Fori(0, NF // 2 - 1) as i:
                    up(l, i * 2 + 1, 1)
                    down(l, i * 2, 0)
                    up(l, i * 2 + 2, 0)
                    down(l, i * 2 + 1, 1)
                up(l, NF - 1, 1)
                down(l, NF - 2, 0)
                down(l, NF - 1, 1, behind)

            def first_tiles(t):
                if 3 <= t < 7:
                    transpose_resid(2, t - 3)

            def last_tiles():
                pe.wait_ge(acc_done.sem, acc_done.ready(NF * 16 - 1))
                for t in range(4, NT):
                    transpose_resid(2, t)
                pe.wait_ge(tp_lo.sem, tp_lo.ready(3 * NT - 1))

            pe.wait_ge(tp_lo.sem, tp_lo.ready(2 * NT - 2))
            ffn(0, lambda: last_tile(1), first_tiles)

            def conv_in(c, slot, between=None):
                pe.wait_ge(win_lo_done.sem, win_lo_done.ready(c))
                for n, h in enumerate(halves):
                    if n and between:
                        between()
                    pe.wait_ge(glu_done.sem, glu_done.free(c * 2 + n, 2))
                    for g in range(2):
                        ins = product(ps[g][:, h],
                                      [((win_hi[:, slot, g, k, :], win_lo[:, slot, g, k, :]),
                                        (actT_hi[:, k, h], actT_lo[:, k, h])) for k in range(NK)])
                    ins.then_inc(in_ps.sem, 1)

            def conv_taps(c, slot, more=False):
                pe.wait_ge(glu_lo_done.sem, glu_lo_done.ready(c))
                pe.wait_ge(conv_out.sem, conv_out.free(c, 2))

                def tap_sum(d_hi, d_lo, first, count, start, stop):
                    for n, h in enumerate(halves):
                        for j in range(count):
                            src = slice(HALF * n + first + j, HALF * (n + 1) + first + j)
                            g_hi, g_lo = glu_hi[:, slot, src], glu_lo[:, slot, src]
                            mm(ps[2 + slot][:, h], d_hi[:, j, :], g_hi, start=start and j == 0, stop=False)
                            mm(ps[2 + slot][:, h], d_hi[:, j, :], g_lo, start=False, stop=False)
                            ins = mm(ps[2 + slot][:, h], d_lo[:, j, :], g_hi, start=False, stop=stop and j == count - 1)
                    return ins

                if more:
                    pe.wait_ge(more_diag_done, 1)
                    tap_sum(more_diag_hi, more_diag_lo, PE_TAPS, MORE_TAPS, True, False)
                pe.wait_ge(diag_done.sem, diag_done.ready(c))
                tap_sum(diag_hi, diag_lo, 0, PE_TAPS, not more, True).then_inc(conv_ps.sem, 1)

            pe.wait_ge(tp_lo.sem, tp_lo.ready(2 * NT + 3))
            conv_in(0, 0, last_tiles)
            conv_in(1, 1)
            with pe.Fori(0, NK // 2 - 1) as i:
                for b in range(2):
                    conv_taps(i * 2 + b, b)
                    conv_in(i * 2 + b + 2, b)
            conv_taps(NK - 2, 0)
            conv_taps(NK - 1, 1, True)

            pe.wait_ge(tap_done.sem, tap_done.ready(TAP_STEPS - 1))

            def to_tokens(t):
                if t:
                    pe.wait_ge(cl_norm.sem, cl_norm.ready(t - 1))
                for k in range(NK):
                    ins = nc.tensor.transpose(ps[0][:, tok[k]], convT[:, k, tok[t]], ident[:])
                ins.then_inc(cl_ps.sem, 1)

            def to_channels(t):
                pe.wait_ge(cl_norm.sem, cl_norm.ready(t))
                if t:
                    pe.wait_ge(silu_done.sem, silu_done.ready(t - 1))
                for k in range(NK):
                    ins = nc.tensor.transpose(ps[1][:, tok[k]], convT[:, k, tok[t]], ident[:])
                ins.then_inc(cb_ps.sem, 1)

            def convolved(t):
                pe.wait_ge(sT_lo_done.sem, sT_lo_done.ready(t))
                square_tile(1, t, wx_hi, wx_lo)

            for t in range(NT + 1):
                if t < NT:
                    to_tokens(t)
                if t:
                    to_channels(t - 1)
                if t in (3, 5, 7):
                    convolved((t - 3) // 2)
            for t, behind in ((3, (0, 1)), (4, (2, 3)), (5, (4,)), (6, (5,)), (7, (6,))):
                convolved(t)
                if t == 3:
                    pe.wait_ge(silu_done.sem, silu_done.ready(NT - 1))
                for b in behind:
                    transpose_resid(3, b)
            pe.wait_ge(tp_lo.sem, tp_lo.ready(4 * NT - 2))
            ffn(1, lambda: last_tile(3))

        @block.scalar
        def _(act):
            copy, activate = nc.scalar.copy, nc.scalar.activation

            def split_tile(use, t):
                act.wait_ge(tp_ps.sem, tp_ps.ready(use * NT + t))
                copy(actT_hi[:, :, tok[t]], turned(use, t)[:].rearrange("p (k n) -> p k n", k=NK)
                     ).then_inc(tp_hi.sem, 1)

            def split_wd(k):
                act.wait_ge(wd_in[k], 32)
                copy(wd_hi[:, k, :], wd_raw[:, k, :]).then_inc(wd_hi_done.sem, 1)

            act.wait_ge(started, 1)
            for t in range(4):
                split_tile(0, t)
            split_wd(0)
            split_wd(1)
            for t in range(4, NT):
                split_tile(0, t)
                split_wd(t - 2)
            split_wd(6)
            split_wd(7)
            act.wait_ge(cols_ps, 1)
            copy(cols[:, 0:N_COLS], ps[3][:, 0:N_COLS])
            taps_ps = ps[3][:, 64:64 + 32 * NK].rearrange("p (k j) -> p k j", k=NK)
            copy(conv_cols[:, :, CC_DW:CC_DW + TAPS], taps_ps[:, :, 0:TAPS])
            copy(dw_hi[:], taps_ps[:, :, 0:PE_TAPS])
            copy(more_hi[:], taps_ps[:, NK - 1, PE_TAPS:PE_TAPS + MORE_TAPS])
            for k in range(NK):
                for dst, src in ((CC_BIAS, C_DWB), (CC_VALUE, C_BIN), (CC_GATE, C_BIN + NK)):
                    ins = copy(conv_cols[:, k, dst:dst + 1], ps[3][:, src + k:src + k + 1])
            ins.then_inc(cols_done, 1)

            def squares(t):
                act.wait_ge(c_ps.sem, c_ps.ready(t))
                activate(x_stage[:, t % 2, 0:Q_RANK], ps[2 + t % 2][:, 0:Q_RANK], ACT.Square, accum_out=stats[:, t, 0:1])
                activate(x_stage[:, t % 2, HALF:HALF + KV_RANK], ps[2 + t % 2][:, HALF:HALF + KV_RANK], ACT.Square,
                         accum_out=stats[:, t, 1:2]).then_inc(c_sq.sem, 1)

            def split_c(t):
                act.wait_ge(ct_ps.sem, ct_ps.ready(t))
                for j in range(5):
                    ins = activate(cT_hi[:, j, tok[t]], ps[t % 2][:, tok[j]], ACT.Copy,
                                   scale=cols[:, C_GQ + j:C_GQ + j + 1])
                ins.then_inc(ct_hi.sem, 1)

            def split_pair(i, wait_used=True):
                if wait_used:
                    act.wait_ge(vt_ps.sem, vt_ps.ready(i - 1))
                act.wait_ge(wq_in, (i + 1) * 16)
                for dst, src in pair_views(wq_hi, wq_raw):
                    copy(dst, src)
                act.wait_ge(wkv_in, (i + 1) * 16)
                for dst, src in kv_views(wkv_hi, wkv_raw):
                    ins = copy(dst, src)
                ins.then_inc(wa_hi_done.sem, 1)

            def rotary_tables():
                act.wait_ge(ang_done, 1)
                activate(absr[:], ang[:], ACT.Abs).then_inc(act_steps, 1)
                activate(sinv[:], ang[:], ACT.Sin, scale=consts[:, 1:2]).then_inc(act_steps, 1)
                act.wait_ge(act_steps, 1)
                activate(cosv[:], absr[:], ACT.Sin, bias=consts[:, 2:3], scale=-1.0).then_inc(act_steps, 1)
                act.wait_ge(act_steps, 3)

            def spread_tables(q):
                rows, cs = slice(32 * q, 32 * q + 32), slice(QUARTER * q, QUARTER * (q + 1))
                for j in range(2):
                    copy(tab[32 * j:32 * j + 32, cs], cosv[rows, :])
                    ins = copy(tab[64 + 32 * j:96 + 32 * j, cs], sinv[rows, :])
                if q == 3:
                    ins.then_inc(tab_done, 1)

            act.wait_ge(cols_done, 1)
            for t in range(NT):
                squares(t)
                if t:
                    split_c(t - 1)
                if t == 2:
                    rotary_tables()
                if 3 <= t < 7:
                    spread_tables(t - 3)
            split_pair(0, wait_used=False)
            split_c(NT - 1)

            def head_part(dst, src, j):
                return copy(dst[0:NOPE, j, :], src[NOPE * j:NOPE * (j + 1), :])

            def square_hi(use, w_hi, raw, k):
                act.wait_ge(wsq_in[k], 16 * (use + 1))
                copy(w_hi[:, k, :], raw[:, k, :]).then_inc(wsq_hi_done.sem, 1)

            def split_keys(i):
                act.wait_ge(k_ps.sem, k_ps.ready(i))
                head_part(k_hi, ps[1], 0)
                head_part(k_hi, ps[1], 1).then_inc(k_hi_done.sem, 1)

            def split_rotary(i):
                act.wait_ge(qr_sum.sem, qr_sum.ready(i))
                copy(q_hi[NOPE:QK, :, :], rope_m[NOPE:QK, :, :]).then_inc(qr_hi_done.sem, 1)

            def split_plain(i):
                act.wait_ge(qn_ps.sem, qn_ps.ready(i))
                head_part(q_hi, ps[0], 0)
                head_part(q_hi, ps[0], 1).then_inc(qn_hi_done.sem, 1)

            def values_transposed(i):
                act.wait_ge(vt_ps.sem, vt_ps.ready(i))
                copy(vT[:], ps[1][:]).then_inc(vt_done.sem, 1)

            def values(i):
                act.wait_ge(v_ps.sem, v_ps.ready(i))
                copy(v2[:, :, :, 0:VDIM], ps[2][:].rearrange("p (t j d) -> p t j d", t=NT, j=2)
                     ).then_inc(v_hi_done.sem, 1)

            def exponentials(i, n):
                item = i * NQT + n
                act.wait_ge(pt_ps.sem, pt_ps.free(item * 2, 1) if n == 0 else pt_ps.ready((item - 3) * 2 + 1) if n > 2
                            else pt_ps.free(item * 2 + 1, 4))
                act.wait_ge(s_max.sem, s_max.ready(item))
                activate(p_f[:, n % 3, :], ps[n % 2][:], ACT.Exp, bias=negmax[:, n:n + 1], scale=-1.0,
                         accum_out=sums[:, n:n + 1]).then_inc(p_done.sem, 1)

            def split_probs(i, n):
                c = n // 4
                act.wait_ge(o_ps.sem, o_ps.free(i * NC + c, 2))
                for a in range(2):
                    act.wait_ge(pt_ps.sem, pt_ps.ready((i * NQT + n) * 2 + a))
                    copy(pt_hi[:, c % 2, 4 * a:4 * a + 4, tok[n % 4]],
                         ps[2][:, halves[a]].rearrange("p (k n) -> p k n", k=4)).then_inc(pt_hi_done.sem, 1)

            def first_half(i, c):
                act.wait_ge(o_stored[c % 2].sem, (i * 2 + c // 2) * 16 + CREDIT)
                act.wait_ge(o_ps.sem, o_ps.ready(i * NC + c))
                copy(o_sum[0:VDIM, c % 2, :], ps[3][0:VDIM, halves[c % 2]]).then_inc(o_first_done.sem, 1)

            def attend(i, more):
                for n in range(NQT):
                    if n >= 3:
                        split_probs(i, n - 3)
                    exponentials(i, n)
                    if n == 0:
                        values(i)
                    if n >= 11 and (n - 11) % 4 == 0:
                        first_half(i, (n - 11) // 4)
                    if more and n == 4:
                        split_pair(i + 1)
                    if not more and n in (5, 7, 9):
                        square_hi(0, wo_hi, wo_raw, (n - 5) // 2)
                split_probs(i, NQT - 3)
                split_probs(i, NQT - 2)
                if more:
                    split_keys(i + 1)
                    split_rotary(i + 1)
                split_probs(i, NQT - 1)
                first_half(i, 2)
                if more:
                    split_plain(i + 1)
                    values_transposed(i + 1)
                first_half(i, 3)

            act.wait_ge(ct_ps.sem, ct_ps.ready(NT - 1))
            act.wait_ge(krope_done, 1)
            for j in range(2):
                ins = copy(k_hi[NOPE:QK, j, :], rope_m[NOPE:QK, 0, :])
            ins.then_inc(krope_hi, 1)
            split_rotary(0)
            split_keys(0)
            split_plain(0)
            values_transposed(0)
            with act.Fori(0, PAIRS - 1) as i:
                attend(i, True)
            attend(PAIRS - 1, False)

            def unit_tile(u, t):
                act.wait_ge(ln_rstd.sem, ln_rstd.ready(u * NT + t))
                act.wait_ge(ln_centred.sem, ln_centred.ready(u * NT + t))
                activate(resid[:, t, :], resid[:, t, :], ACT.Copy, scale=rstd[:, t, 0:1]).then_inc(ln_unit.sem, 1)

            def rescale(use, t):
                act.wait_ge(tp_ps.sem, tp_ps.ready(use * NT + t))
                nc.scalar.mul(resid[:, t, :], resid[:, t, :], ALPHA).then_inc(ln_scaled.sem, 1)

            act.wait_ge(o_done.sem, o_done.ready(NC * PAIRS - 1))
            for k in range(NK):
                act.wait_ge(oT_in[k], 16)
                copy(actT_hi[:, k, :], oT_f[:, k, :]).then_inc(oT_hi_done.sem, 1)
                if k >= 3:
                    square_hi(0, wo_hi, wo_raw, k)

            def split_13(l, f, slot):
                w13_hi, _, w13_raw = up_w[l]
                item = f + l * NF
                act.wait_ge(w13_in[slot], (item - slot) * 16 + 32)
                copy(w13_hi[:, slot], w13_raw[:, slot]).then_inc(w13_hi_done.sem, 1)

            for t in range(NT):
                if t:
                    split_tile(1, t - 1)
                unit_tile(0, t)
                if t:
                    rescale(1, t - 1)
                if t in (2, 4):
                    split_13(0, t // 4, t // 4)

            def ffn(l):
                hid_hi, _, w2_hi, _, w2_raw, gate, hid_f = ffn_m[l]

                def split_2(f, slot):
                    item = f + l * NF
                    act.wait_ge(w2_in[slot], (item - slot) * 8 + 16)
                    copy(w2_hi[:, slot, :], w2_raw[:, slot, :]).then_inc(w2_hi_done.sem, 1)

                def hidden(f, slot, used=True):
                    item = f + l * NF
                    for n, h in enumerate(halves):
                        act.wait_ge(up_ps.sem, up_ps.ready(item * 2 + n))
                        act.wait_ge(hid_f_done.sem, hid_f_done.free(item * 2 + n, 2))
                        activate(gate[:, h], ps[0][:, h], ACT.Silu).then_inc(gate_done.sem, 1)
                        if used and n == 0:
                            act.wait_ge(down_ps.sem, down_ps.ready((item - 2) * 16 + 15))
                        act.wait_ge(hid_f_done.sem, hid_f_done.ready(item * 2 + n))
                        copy(hid_hi[:, slot, h], hid_f[:, h]).then_inc(hid_hi_done.sem, 1)

                split_tile(2 * l + 1, NT - 1)
                rescale(2 * l + 1, NT - 1)
                split_2(0, 0)
                hidden(0, 0, False)
                split_13(l, 2, 0)
                split_2(1, 1)
                hidden(1, 1, False)
                split_13(l, 3, 1)
                split_2(2, 0)
                with act.Fori(1, NF // 2 - 1) as i:
                    for b in range(2):
                        hidden(i * 2 + b, b)
                        split_13(l, i * 2 + b + 2, b)
                        split_2(i * 2 + b + 1, 1 - b)
                hidden(NF - 2, 0)
                split_2(NF - 1, 1)
                hidden(NF - 1, 1)

            ffn(0)

            def split_win(c, slot, loads):
                act.wait_ge(win_in[slot], loads)
                copy(win_hi[:, slot], win_raw[:, slot]).then_inc(win_hi_done.sem, 1)

            split_win(0, 0, 32)
            for t in range(NT):
                if 3 <= t < 7:
                    split_tile(2, t - 3)
                unit_tile(1, t)
            split_win(1, 1, 32)
            for t in range(4):
                rescale(2, t)
            for t in range(4, NT):
                split_tile(2, t)
                rescale(2, t)

            def sigmoids(c, slot):
                act.wait_ge(now_done.sem, now_done.ready(c))
                for n, h in enumerate(halves):
                    act.wait_ge(glu_done.sem, glu_done.free(c * 2 + n, 2))
                    act.wait_ge(in_ps.sem, in_ps.ready(c * 2 + n))
                    activate(sig[:, h], ps[1][:, h], ACT.Sigmoid, bias=conv_now[:, slot, CC_GATE:CC_GATE + 1]
                             ).then_inc(sig_done.sem, 1)

            def split_glu(c, slot):
                act.wait_ge(glu_done.sem, glu_done.ready(c * 2 + 1))
                act.wait_ge(conv_ps.sem, conv_ps.free(c, 2))
                copy(glu_hi[:, slot, :], glu[:, slot, :]).then_inc(glu_hi_done.sem, 1)

            def conv_start(c, slot):
                act.wait_ge(conv_ps.sem, conv_ps.ready(c))
                act.wait_ge(tap_done.sem, tap_done.free(c * (TAPS - PE_TAPS) * 2, 1))
                activate(conv_acc[:], ps[2 + slot][:], ACT.Identity, bias=conv_now[:, slot, CC_BIAS:CC_BIAS + 1]
                         ).then_inc(conv_out.sem, 1)

            act.wait_ge(ln_bout.sem, ln_bout.ready(NT - 1))
            sigmoids(0, 0)
            split_glu(0, 0)
            split_win(2, 0, 64)
            sigmoids(1, 1)
            split_glu(1, 1)

            def conv_step(c, b, loads=None):
                conv_start(c, b)
                if loads is not None:
                    split_win(c + 3, 1 - b, loads)
                sigmoids(c + 2, b)
                split_glu(c + 2, b)

            with act.Fori(0, NK // 2 - 2) as i:
                conv_step(i * 2, 0, i * 32 + 64)
                conv_step(i * 2 + 1, 1, i * 32 + 96)
            conv_step(NK - 4, 0, 16 * NK)
            conv_step(NK - 3, 1)
            conv_start(NK - 2, 0)

            act.wait_ge(tap_done.sem, tap_done.ready(TAP_STEPS - 1))

            def activated(t):
                act.wait_ge(cb_ps.sem, cb_ps.ready(t))
                for k in range(NK):
                    ins = activate(convT[:, k, tok[t]], ps[1][:, tok[k]], ACT.Silu,
                                   bias=cols[:, C_LNB + k:C_LNB + k + 1], scale=cols[:, C_LNG + k:C_LNG + k + 1])
                ins.then_inc(silu_done.sem, 1)
                act.wait_ge(silu_done.sem, silu_done.ready(t))
                copy(actT_hi[:, :, tok[t]], convT[:, :, tok[t]]).then_inc(sT_hi_done.sem, 1)

            for t in range(NT + 1):
                if t < 4:
                    square_hi(1, wx_hi, wx_raw, 2 * t)
                    square_hi(1, wx_hi, wx_raw, 2 * t + 1)
                if t:
                    activated(t - 1)
                if t in (5, 7):
                    unit_tile(2, (t - 5) // 2)
            unit_tile(2, 2)
            for t, behind in ((3, (0, 1)), (4, (2, 3)), (5, (4,)), (6, (5,)), (7, (6,))):
                if t in (3, 5):
                    split_13(1, t // 4, t // 4)
                for b in behind:
                    split_tile(3, b)
                unit_tile(2, t)
                for b in behind:
                    rescale(3, b)
            ffn(1)
            for t in range(NT):
                unit_tile(3, t)

        @block.vector
        def _(v):
            V = nc.vector
            own = Chain(dve_steps, v)
            tt, sub = V.tensor_tensor, ALU.subtract

            v.wait_ge(started, 1)
            def split_tile(use, t):
                v.wait_ge(tp_hi.sem, tp_hi.ready(use * NT + t))
                tt(actT_lo[:, :, tok[t]], turned(use, t)[:].rearrange("p (k n) -> p k n", k=NK),
                   actT_hi[:, :, tok[t]], sub).then_inc(tp_lo.sem, 1)

            for t in range(NT):
                split_tile(0, t)

            v.wait_ge(small_in, 5 * 16)
            own.link(V.tensor_scalar(ang[:], pos_i[:], consts[:, 0:1], None, ALU.mult))
            for size, count in ((2.0 ** 20, 4), (2.0 ** 10, 4), (1.0, 4)):
                own.link(V.tensor_scalar(turns[:], ang[:], 1.0 / (2 * math.pi * size), MAGIC, ALU.mult, ALU.add))
                own.link(V.tensor_scalar(turns[:], turns[:], MAGIC, None, ALU.subtract))
                for piece in turn_pieces(size, count):
                    own.link(V.scalar_tensor_tensor(out=ang[:], in0=turns[:], scalar=-piece, in1=ang[:],
                                                    op0=ALU.mult, op1=ALU.add))
            V.tensor_scalar(ang[:], ang[:], 3.1415925, -3.1415925, ALU.min, ALU.max).then_inc(ang_done, 1)

            def norm_c(t):
                src = ps[2 + t % 2]
                v.wait_ge(c_sq.sem, c_sq.ready(t))
                V.tensor_scalar(mean_var[:, t, 0:1], stats[:, t, 0:1], 1.0 / Q_RANK, RMS_EPS, ALU.mult, ALU.add)
                V.tensor_scalar(mean_var[:, t, 1:2], stats[:, t, 1:2], 1.0 / KV_RANK, RMS_EPS, ALU.mult, ALU.add
                                ).then_inc(c_ms.sem, 1)
                v.wait_ge(c_rstd.sem, c_rstd.ready(t))
                v.wait_ge(ct_ps.sem, ct_ps.free(t, 1))
                V.tensor_scalar(c_tok[:, 0:Q_RANK], src[:, 0:Q_RANK], rstd[:, t, 0:1], None, ALU.mult)
                V.tensor_scalar(c_tok[:, Q_RANK:Q_RANK + KV_RANK], src[:, HALF:HALF + KV_RANK], rstd[:, t, 1:2],
                                None, ALU.mult)
                r0, h = HALF + KV_RANK, ROPE // 2
                V.tensor_copy(c_tok[:, 5 * P:5 * P + ROPE], src[:, r0:r0 + ROPE])
                V.tensor_copy(c_tok[:, 5 * P + ROPE:5 * P + ROPE + h], src[:, r0 + h:r0 + ROPE])
                V.tensor_copy(c_tok[:, 5 * P + ROPE + h:5 * P + 2 * ROPE], src[:, r0:r0 + h]
                              ).then_inc(c_tok_done.sem, 1)

            def split_c(t):
                v.wait_ge(ct_hi.sem, ct_hi.ready(t))
                for j in range(5):
                    V.scalar_tensor_tensor(out=cT_lo[:, j, tok[t]], in0=ps[t % 2][:, tok[j]],
                                           scalar=cols[:, C_GQ + j:C_GQ + j + 1], in1=cT_hi[:, j, tok[t]],
                                           op0=ALU.mult, op1=sub)
                V.tensor_copy(kr_f[0:ROPE, tok[t]], ps[t % 2][0:ROPE, tok[5]])
                V.tensor_copy(kr_f[2 * ROPE:3 * ROPE, tok[t]], ps[t % 2][ROPE:2 * ROPE, tok[5]]).then_inc(ct_lo.sem, 1)

            v.wait_ge(cols_done, 1)
            for t in range(NT):
                norm_c(t)
                if t:
                    split_c(t - 1)
            split_c(NT - 1)

            v.wait_ge(tab_done, 1)
            v.wait_ge(ct_lo.sem, ct_lo.ready(NT - 1))
            v.wait_ge(ct_ps.sem, ct_ps.ready(NT - 1))
            tt(rope_m[0:ROPE, 0, :], kr_f[0:ROPE, :], tab[0:ROPE, :], ALU.mult)
            own.link(tt(rope_m[0:ROPE, 1, :], kr_f[2 * ROPE:3 * ROPE, :], tab[2 * ROPE:3 * ROPE, :], ALU.mult))
            tt(rope_m[NOPE:QK, 0, :], rope_m[0:ROPE, 0, :], rope_m[0:ROPE, 1, :], ALU.add).then_inc(krope_done, 1)
            v.wait_ge(krope_hi, 1)
            for j in range(2):
                ins = tt(k_lo[NOPE:QK, j, :], rope_m[NOPE:QK, 0, :], k_hi[NOPE:QK, j, :], sub)
            ins.then_inc(krope_lo, 1)
            v.wait_ge(krope_lo, 1)

            def head_part(lo, hi, src, j):
                return tt(lo[0:NOPE, j, :], src[NOPE * j:NOPE * (j + 1), :], hi[0:NOPE, j, :], sub)

            def square_lo(use, w_hi, w_lo, raw, k):
                v.wait_ge(wsq_hi_done.sem, wsq_hi_done.ready(use * NK + k))
                tt(w_lo[:, k, :], raw[:, k, :], w_hi[:, k, :], sub).then_inc(wsq_odd_lo.sem, 1)

            def split_keys(i):
                v.wait_ge(k_hi_done.sem, k_hi_done.ready(i))
                head_part(k_lo, k_hi, ps[1], 0)
                head_part(k_lo, k_hi, ps[1], 1).then_inc(k_lo_done.sem, 1)

            def rotary_parts(i):
                v.wait_ge(qr_ps.sem, qr_ps.ready(i))
                tt(rope_m[0:2 * ROPE, 0, :], ps[0][0:2 * ROPE, :], tab[0:2 * ROPE, :], ALU.mult)
                tt(rope_m[0:2 * ROPE, 1, :], ps[0][2 * ROPE:P, :], tab[2 * ROPE:P, :], ALU.mult
                   ).then_inc(qr_parts.sem, 1)

            def rotary_sums(i):
                v.wait_ge(qr_parts.sem, qr_parts.ready(i))
                for j in range(2):
                    rows = slice(ROPE * j, ROPE * (j + 1))
                    ins = tt(rope_m[NOPE:QK, j, :], rope_m[rows, 0, :], rope_m[rows, 1, :], ALU.add)
                ins.then_inc(qr_sum.sem, 1)

            def split_rotary(i):
                v.wait_ge(qr_sum.sem, qr_sum.ready(i))
                v.wait_ge(qr_hi_done.sem, qr_hi_done.ready(i))
                tt(q_lo[NOPE:QK, :, :], rope_m[NOPE:QK, :, :], q_hi[NOPE:QK, :, :], sub).then_inc(qr_lo_done.sem, 1)

            def split_plain(i):
                v.wait_ge(qn_hi_done.sem, qn_hi_done.ready(i))
                head_part(q_lo, q_hi, ps[0], 0)
                head_part(q_lo, q_hi, ps[0], 1).then_inc(qn_lo_done.sem, 1)

            def values(i):
                v.wait_ge(v_hi_done.sem, v_hi_done.ready(i))
                tt(v2[:, :, :, VDIM:2 * VDIM], ps[2][:].rearrange("p (t j d) -> p t j d", t=NT, j=2),
                   v2[:, :, :, 0:VDIM], sub).then_inc(v_lo_done.sem, 1)

            def row_max(i, n):
                v.wait_ge(s_ps.sem, s_ps.ready(i * NQT + n))
                V.tensor_scalar(ps[n % 2][:], ps[n % 2][:], -SCALE, None, ALU.mult, ALU.min,
                                accum_out=negmax[:, n:n + 1]).then_inc(s_max.sem, 1)

            def split_probs(i, n):
                c = n // 4
                for a in range(2):
                    v.wait_ge(pt_hi_done.sem, pt_hi_done.ready((i * NQT + n) * 2 + a))
                    tt(pt_lo[:, c % 2, 4 * a:4 * a + 4, tok[n % 4]],
                       ps[2][:, halves[a]].rearrange("p (k n) -> p k n", k=4),
                       pt_hi[:, c % 2, 4 * a:4 * a + 4, tok[n % 4]], sub).then_inc(pt_lo_done.sem, 1)

            def inverse_sum(i, n):
                v.wait_ge(p_done.sem, p_done.ready(i * NQT + n))
                V.reciprocal(rsums[:, n:n + 1], sums[:, n:n + 1]).then_inc(rsum_done.sem, 1)

            def outputs(i, c):
                v.wait_ge(o_first_done.sem, o_first_done.ready(i * NC + c))
                o = o_sum[0:VDIM, c % 2, :]
                tt(o, ps[3][VDIM:P, halves[c % 2]], o, ALU.add).then_inc(o_done.sem, 1)

            def attend(i, more):
                for n in range(NQT):
                    if n:
                        inverse_sum(i, n - 1)
                    row_max(i, n)
                    if n == 1:
                        values(i)
                    if n >= 3:
                        split_probs(i, n - 3)
                    if n >= 11 and (n - 11) % 4 == 0:
                        outputs(i, (n - 11) // 4)
                    if not more and n == 10:
                        square_lo(0, wo_hi, wo_lo, wo_raw, 1)
                inverse_sum(i, NQT - 1)
                split_probs(i, NQT - 3)
                if more:
                    rotary_parts(i + 1)
                split_probs(i, NQT - 2)
                if more:
                    rotary_sums(i + 1)
                    split_keys(i + 1)
                split_probs(i, NQT - 1)
                outputs(i, 2)
                if more:
                    split_rotary(i + 1)
                    split_plain(i + 1)
                outputs(i, 3)

            rotary_parts(0)
            rotary_sums(0)
            split_keys(0)
            split_rotary(0)
            split_plain(0)
            with v.Fori(0, PAIRS - 1) as i:
                attend(i, True)
            attend(PAIRS - 1, False)

            def norm_tile(u, t):
                item = u * NT + t
                V.bn_stats(stats[:, t, 0:6], resid[:, t, halves[0]])
                own.link(V.bn_stats(stats[:, t, 6:12], resid[:, t, halves[1]]))
                own.link(V.bn_aggr(mean_var[:, t, :], stats[:, t, :]))
                V.tensor_scalar_add(mean_var[:, t, 1:2], mean_var[:, t, 1:2], LN_EPS).then_inc(ln_var.sem, 1)
                v.wait_ge(gb_in, (u + 1) * 32)
                V.scalar_tensor_tensor(out=resid[:, t, :], in0=resid[:, t, :], scalar=mean_var[:, t, 0:1],
                                       in1=gb[:, 0, :], op0=sub, op1=ALU.mult).then_inc(ln_centred.sem, 1)

            def add_norm(use, u, t, scale, behind=()):
                if use == 0:
                    v.wait_ge(xr_in[t], 16)
                else:
                    v.wait_ge(ln_bout.sem, ln_bout.ready(t))
                v.wait_ge(pr_ps.sem, pr_ps.ready(use * NT + t))
                V.scalar_tensor_tensor(out=resid[:, t, :], in0=resid[:, t, :], scalar=scale,
                                       in1=ps[2 + t % 2][:], op0=ALU.mult, op1=ALU.add).then_inc(pr_add.sem, 1)
                for b in behind:
                    split_tile(u + 1, b)
                v.wait_ge(pr_add.sem, pr_add.ready(use * NT + t))
                norm_tile(u, t)

            for k in range(NK):
                v.wait_ge(oT_hi_done.sem, oT_hi_done.ready(k))
                tt(actT_lo[:, k, :], oT_f[:, k, :], actT_hi[:, k, :], sub).then_inc(oT_lo_done.sem, 1)
                if k % 2 and k > 1:
                    square_lo(0, wo_hi, wo_lo, wo_raw, k)
            for t in range(NT):
                add_norm(0, 0, t, ALPHA, (t - 1,) if t else ())
            split_tile(1, NT - 1)

            def ffn(l, behind):
                hid_hi, hid_lo, _, _, _, gate, hid_f = ffn_m[l]

                def product_half(f, n):
                    item, h = (f + l * NF) * 2 + n, halves[n]
                    v.wait_ge(gate_done.sem, gate_done.ready(item))
                    v.wait_ge(hid_lo_done.sem, hid_lo_done.free(item, 2))
                    tt(hid_f[:, h], ps[1][:, h], gate[:, h], ALU.mult).then_inc(hid_f_done.sem, 1)

                def split_half(f, slot, n):
                    item, h = (f + l * NF) * 2 + n, halves[n]
                    v.wait_ge(hid_hi_done.sem, hid_hi_done.ready(item))
                    tt(hid_lo[:, slot, h], hid_f[:, h], hid_hi[:, slot, h], sub).then_inc(hid_lo_done.sem, 1)

                def accumulate(f, first, last, behind=None):
                    item = f + l * NF
                    for m in range(first, last):
                        t, h = divmod(m, 2)
                        v.wait_ge(down_ps.sem, down_ps.ready(item * 16 + m))
                        r = resid[:, t, halves[h]]
                        tt(r, bank(m), r, ALU.add).then_inc(acc_done.sem, 1)
                        if h and behind:
                            behind(t)

                def step(f, slot):
                    product_half(f, 0)
                    split_half(f, slot, 0)
                    product_half(f, 1)
                    accumulate(f - 1, 0, 4)
                    split_half(f, slot, 1)
                    accumulate(f - 1, 4, 2 * NT)

                product_half(0, 0)
                split_half(0, 0, 0)
                product_half(0, 1)
                split_half(0, 0, 1)
                with v.Fori(0, NF // 2 - 1) as i:
                    step(i * 2 + 1, 1)
                    step(i * 2 + 2, 0)
                step(NF - 1, 1)
                accumulate(NF - 1, 0, 2 * NT, behind)

            def first_norm(t):
                v.wait_ge(acc_done.sem, acc_done.ready((NF - 1) * 16 + 2 * t + 1))
                if 3 <= t < 7:
                    split_tile(2, t - 3)
                norm_tile(1, t)

            def last_norm(t):
                v.wait_ge(acc_done.sem, acc_done.ready((2 * NF - 1) * 16 + 2 * t + 1))
                norm_tile(3, t)

            v.wait_ge(ln_scaled.sem, ln_scaled.ready(NT - 1))
            ffn(0, first_norm)

            V.tensor_copy(more_cols[:, 0, :], more_hi[:])
            tt(more_cols[:, 1, :], conv_cols[:, NK - 1, CC_DW + PE_TAPS:CC_DW + PE_TAPS + MORE_TAPS], more_hi[:], sub)
            V.tensor_copy(conv_cols[:, :, CC_HI:CC_HI + PE_TAPS], dw_hi[:])
            tt(conv_cols[:, :, CC_LO:CC_LO + PE_TAPS], conv_cols[:, :, CC_DW:CC_DW + PE_TAPS], dw_hi[:], sub
               ).then_inc(cc_done, 1)
            v.wait_ge(cc_done, 1)

            def columns(c, slot, used=True):
                if used:
                    v.wait_ge(tap_done.sem, tap_done.ready((c - 1) * (TAPS - PE_TAPS) * 2 - 1))
                V.tensor_copy(conv_now[:, slot, :], conv_cols[:, bass.ds(c, 1), :].rearrange("p o n -> p (o n)")
                              ).then_inc(now_done.sem, 1)

            def gated(c, slot):
                v.wait_ge(now_done.sem, now_done.ready(c))
                for n, h in enumerate(halves):
                    v.wait_ge(sig_done.sem, sig_done.ready(c * 2 + n))
                    V.scalar_tensor_tensor(out=glu[:, slot, PAD + HALF * n:PAD + HALF * (n + 1)],
                                           in0=ps[0][:, h], scalar=conv_now[:, slot, CC_VALUE:CC_VALUE + 1],
                                           in1=sig[:, h], op0=ALU.add, op1=ALU.mult).then_inc(glu_done.sem, 1)
            def taps(c, slot, more=0):
                first, base = PE_TAPS + more, c * (TAPS - PE_TAPS)
                count = TAPS - first
                if more:
                    v.wait_ge(tap_done.sem, tap_done.ready(base * 2 - 1))
                else:
                    v.wait_ge(conv_out.sem, conv_out.ready(c))
                for j in range(count):
                    w = conv_now[:, slot, CC_DW + first + j:CC_DW + first + j + 1]
                    for n in range(2):
                        start = HALF * n + first + j
                        acc = conv_acc[:, halves[n]]
                        if j:
                            v.wait_ge(tap_done.sem, tap_done.ready((base + j - 1) * 2 + n))
                        src = glu[:, slot, start:start + HALF]
                        if more and j == 0:
                            V.tensor_scalar(acc, src, w, conv_now[:, slot, CC_BIAS:CC_BIAS + 1], ALU.mult, ALU.add
                                            ).then_inc(tap_done.sem, 1)
                            continue
                        dst = acc if more or j < count - 1 else (
                            convT[:, bass.ds(c, 1), halves[n]].rearrange("p o n -> p (o n)"))
                        V.scalar_tensor_tensor(out=dst, in0=src, scalar=w, in1=acc,
                                               op0=ALU.mult, op1=ALU.add).then_inc(tap_done.sem, 1)
                if more:
                    v.wait_ge(conv_ps.sem, conv_ps.ready(c))
                    for n, h in enumerate(halves):
                        v.wait_ge(tap_done.sem, tap_done.ready((base + count - 1) * 2 + n))
                        tt(convT[:, c, h], ps[2 + slot][:, h], conv_acc[:, h], ALU.add).then_inc(tap_done.sem, 1)

            columns(0, 0, False)
            columns(1, 1, False)
            for t in range(4, NT):
                split_tile(2, t)
            v.wait_ge(pads_done, 1)
            gated(0, 0)
            gated(1, 1)
            with v.Fori(0, NK // 2 - 1) as i:
                for b in range(2):
                    taps(i * 2 + b, b)
                    columns(i * 2 + b + 2, b)
                    gated(i * 2 + b + 2, b)
            taps(NK - 2, 0)
            taps(NK - 1, 1, MORE_TAPS)
            v.wait_ge(tap_done.sem, tap_done.ready(TAP_STEPS - 1))

            def channel_norm(t):
                src = ps[0]
                v.wait_ge(cl_ps.sem, cl_ps.ready(t))
                V.bn_stats(stats[:, t, 0:6], src[:, halves[0]])
                own.link(V.bn_stats(stats[:, t, 6:12], src[:, halves[1]]))
                own.link(V.bn_aggr(mean_var[:, t, :], stats[:, t, :]))
                V.tensor_scalar_add(mean_var[:, t, 1:2], mean_var[:, t, 1:2], LN_EPS).then_inc(cl_var.sem, 1)
                v.wait_ge(cl_rstd.sem, cl_rstd.ready(t))
                V.tensor_scalar(convT[:, :, tok[t]], src[:].rearrange("p (k n) -> p k n", k=NK),
                                mean_var[:, t, 0:1], rstd[:, t, 0:1], sub, ALU.mult).then_inc(cl_norm.sem, 1)

            for t in range(NT + 2):
                if t < NT:
                    channel_norm(t)
                if t < 4:
                    square_lo(1, wx_hi, wx_lo, wx_raw, 2 * t + 1)
                if t >= 2:
                    v.wait_ge(sT_hi_done.sem, sT_hi_done.ready(t - 2))
                    tt(actT_lo[:, :, tok[t - 2]], convT[:, :, tok[t - 2]], actT_hi[:, :, tok[t - 2]], sub
                       ).then_inc(sT_lo_done.sem, 1)
                if t in (5, 7):
                    add_norm(1, 2, (t - 5) // 2, 1.0)
            add_norm(1, 2, 2, 1.0)
            for t, behind in ((3, (0, 1)), (4, (2, 3)), (5, (4,)), (6, (5,)), (7, (6,))):
                add_norm(1, 2, t, 1.0, behind)
            split_tile(3, NT - 1)
            v.wait_ge(ln_scaled.sem, ln_scaled.ready(3 * NT - 1))
            ffn(1, last_norm)

        @block.gpsimd
        def _(pool):
            G = nc.gpsimd
            sub = ALU.subtract
            for f in flows:
                pool.sem_inc(f.sem, CREDIT)
            pool.sem_inc(started, 1)
            G.memset(minus_half[:], -0.5).then_inc(pool_steps, 1)
            G.memset(ident[:], 0.0).then_inc(pool_steps, 1)
            pool.wait_ge(pool_steps, 2)
            G.affine_select(out=ident[:], in_=ident[:], compare_op=ALU.not_equal, fill=1.0, base=0,
                            pattern=[[-1, P]], channel_multiplier=1).then_inc(made_consts, 1)
            pool.wait_ge(made_consts, 1)
            for k in range(NK):
                pool.wait_ge(wd_hi_done.sem, wd_hi_done.ready(k))
                G.tensor_tensor(wd_lo[:, k, :], wd_raw[:, k, :], wd_hi[:, k, :], sub).then_inc(wd_lo_done.sem, 1)
            for t in range(NT):
                pool.wait_ge(c_ms.sem, c_ms.ready(t))
                G.tensor_tensor(rstd[:, t, :], mean_var[:, t, :], minus_half[:], ALU.pow).then_inc(c_rstd.sem, 1)

            weight_parts = list(zip(pair_views(wq_lo, wq_raw) + kv_views(wkv_lo, wkv_raw),
                                    pair_views(wq_hi, wq_raw) + kv_views(wkv_hi, wkv_raw)))

            def split_pair(i, part):
                if part == 0:
                    pool.wait_ge(wa_hi_done.sem, wa_hi_done.ready(i))
                (lo, raw), (hi, _) = weight_parts[part]
                ins = G.tensor_tensor(lo, raw, hi, sub)
                if part == len(weight_parts) - 1:
                    ins.then_inc(wa_lo_done.sem, 1)

            def square_lo(use, w_hi, w_lo, raw, k):
                pool.wait_ge(wsq_hi_done.sem, wsq_hi_done.ready(use * NK + k))
                G.tensor_tensor(w_lo[:, k, :], raw[:, k, :], w_hi[:, k, :], sub).then_inc(wsq_even_lo.sem, 1)

            def normalise(i, n):
                pool.wait_ge(rsum_done.sem, rsum_done.ready(i * NQT + n))
                G.tensor_tensor(p_f[:, n % 3, :], p_f[:, n % 3, :], rsums[:, n:n + 1].to_broadcast([P, SEQ]),
                                ALU.mult).then_inc(p_normed.sem, 1)

            def attend(i, more):
                for n in range(NQT):
                    normalise(i, n)
                    if more and 6 <= n < 6 + len(weight_parts):
                        split_pair(i + 1, n - 6)
                    if not more and n in (8, 12):
                        square_lo(0, wo_hi, wo_lo, wo_raw, n // 2 - 4)

            for part in range(len(weight_parts)):
                split_pair(0, part)
            with pool.Fori(0, PAIRS - 1) as i:
                attend(i, True)
            attend(PAIRS - 1, False)

            def norm_tile(u, t):
                item = u * NT + t
                pool.wait_ge(ln_var.sem, ln_var.ready(item))
                G.tensor_tensor(rstd[:, t, 0:1], mean_var[:, t, 1:2], minus_half[:, 0:1], ALU.pow
                                ).then_inc(ln_rstd.sem, 1)
                pool.wait_ge(gb_in, (u + 1) * 32)
                pool.wait_ge(ln_unit.sem, ln_unit.ready(item))
                G.tensor_tensor(resid[:, t, :], resid[:, t, :], gb[:, 1, :], ALU.add).then_inc(ln_done.sem, 1)

            def split_13(l, f, slot):
                w13_hi, w13_lo, w13_raw = up_w[l]
                pool.wait_ge(w13_hi_done.sem, w13_hi_done.ready(f + l * NF))
                G.tensor_tensor(w13_lo[:, slot], w13_raw[:, slot], w13_hi[:, slot], sub).then_inc(w13_lo_done.sem, 1)

            for k in range(4, NK, 2):
                square_lo(0, wo_hi, wo_lo, wo_raw, k)
            for t in range(NT):
                norm_tile(0, t)
                if t in (3, 5):
                    split_13(0, t // 4, t // 4)

            def ffn(l):
                w2_hi, w2_lo, w2_raw = ffn_m[l][2:5]

                def split_2(f, slot):
                    pool.wait_ge(w2_hi_done.sem, w2_hi_done.ready(f + l * NF))
                    G.tensor_tensor(w2_lo[:, slot, :], w2_raw[:, slot, :], w2_hi[:, slot, :], sub
                                    ).then_inc(w2_lo_done.sem, 1)

                split_2(0, 0)
                with pool.Fori(0, NF // 2 - 1) as i:
                    for b in range(2):
                        split_13(l, i * 2 + b + 2, b)
                        split_2(i * 2 + b + 1, 1 - b)
                split_2(NF - 1, 1)

            ffn(0)

            def split_win(c, slot):
                pool.wait_ge(win_hi_done.sem, win_hi_done.ready(c))
                G.tensor_tensor(win_lo[:, slot], win_raw[:, slot], win_hi[:, slot], sub).then_inc(win_lo_done.sem, 1)

            def diagonals(c, slot):
                pool.wait_ge(now_done.sem, now_done.ready(c))
                pool.wait_ge(conv_ps.sem, conv_ps.free(c, 1))
                for dst, first in ((diag_hi, CC_HI), (diag_lo, CC_LO)):
                    for j in range(PE_TAPS):
                        w = conv_now[:, slot, first + j:first + j + 1]
                        ins = G.tensor_tensor(dst[:, j, :], ident[:], w.to_broadcast([P, P]), ALU.mult)
                ins.then_inc(diag_done.sem, 1)

            def split_glu(c, slot):
                pool.wait_ge(glu_hi_done.sem, glu_hi_done.ready(c))
                G.tensor_tensor(glu_lo[:, slot, :], glu[:, slot, :], glu_hi[:, slot, :], sub).then_inc(glu_lo_done.sem, 1)

            split_win(0, 0)
            for t in range(NT):
                norm_tile(1, t)
            split_win(1, 1)
            pool.wait_ge(bout_in, 16)
            for t in range(NT):
                pool.wait_ge(ln_scaled.sem, ln_scaled.ready(NT + t))
                G.tensor_tensor(resid[:, t, :], resid[:, t, :], bout_b[:], ALU.add).then_inc(ln_bout.sem, 1)
            pool.wait_ge(ln_bout.sem, ln_bout.ready(NT - 1))
            G.memset(glu[:, :, 0:PAD], 0.0)
            G.memset(glu[:, :, PAD + SEQ:], 0.0).then_inc(pads_done, 1)
            pool.wait_ge(ln_done.sem, ln_done.ready(2 * NT - 1))
            split_glu(0, 0)
            diagonals(0, 0)
            split_win(2, 0)
            split_glu(1, 1)

            def conv_step(c, b):
                diagonals(c + 1, 1 - b)
                split_win(c + 3, 1 - b)
                split_glu(c + 2, b)

            with pool.Fori(0, NK // 2 - 2) as i:
                conv_step(i * 2, 0)
                conv_step(i * 2 + 1, 1)
            conv_step(NK - 4, 0)
            diagonals(NK - 2, 0)
            pool.wait_ge(in_ps.sem, in_ps.ready(2 * (NK - 2) + 1))
            for n, dst in enumerate((more_diag_hi, more_diag_lo)):
                for j in range(MORE_TAPS):
                    ins = G.tensor_tensor(dst[:, j, :], ident[:], more_cols[:, n, j:j + 1].to_broadcast([P, P]), ALU.mult)
            ins.then_inc(more_diag_done, 1)
            split_glu(NK - 1, 1)
            diagonals(NK - 1, 1)
            for t in range(NT):
                pool.wait_ge(cl_var.sem, cl_var.ready(t))
                G.tensor_tensor(rstd[:, t, 0:1], mean_var[:, t, 1:2], minus_half[:, 0:1], ALU.pow
                                ).then_inc(cl_rstd.sem, 1)
                if t < 4:
                    square_lo(1, wx_hi, wx_lo, wx_raw, 2 * t)
                if t == 5:
                    norm_tile(2, 0)
            for t in range(1, NT):
                norm_tile(2, t)
                if t in (3, 5):
                    split_13(1, t // 4, t // 4)
            ffn(1)
            for t in range(NT):
                norm_tile(3, t)


_INS = ['x', 'positions', 'ln_g', 'ln_b', 'mla_w_dq', 'mla_q_norm', 'mla_w_uq', 'mla_w_dkv', 'mla_kv_norm',
        'mla_w_ukv', 'mla_w_o', 'conv_w_in', 'conv_b_in', 'conv_dw', 'conv_dw_b', 'conv_ln_g', 'conv_ln_b',
        'conv_w_out', 'conv_b_out', 'ffn_w1', 'ffn_w3', 'ffn_w2']


def kernel(**inputs):
    import concourse.bacc as bacc
    from concourse.bass_utils import run_bass_kernel_spmd as run

    nc = bacc.Bacc("TRN2", target_bir_lowering=False, num_devices=1)
    arrays, args = {}, []

    def add(name, a):
        arrays[name] = a
        args.append(nc.dram_tensor(name, a.shape, mybir.dt.from_np(a.dtype), kind="ExternalInput").ap())

    for name in _INS:
        add(f"in_{name}_dram", np.ascontiguousarray(inputs[name]))
    j = np.arange(P) % ROPE
    exponent = (-2.0 * (j % (ROPE // 2)) / ROPE).astype(np.float32)
    inv_freq = np.float32(10000.0) ** exponent
    rope_const = np.stack([inv_freq, np.where(j < ROPE // 2, -1.0, 1.0), np.full(P, math.pi / 2)], axis=1)
    add("rope_const_dram", np.ascontiguousarray(rope_const.astype(np.float32)))
    args.append(nc.dram_tensor("out_0_dram", (1, SEQ, D), F32, kind="ExternalOutput").ap())
    trunk(nc, *args)
    r = run(nc, [arrays], core_ids=[0])
    return r.results[0]["out_0_dram"]
```
